# Optimizing a Trainium2 kernel written in Bass

```python
import jax, jax.numpy as jnp
from jax import lax
import numpy as np
import math

D_MODEL = 1024
BATCH = 1
SEQ = 512
DEPTH = 1

HEAD_DIM = 64
SCALE = HEAD_DIM ** -0.5
EPS = 1e-6
NEG = -1e30
DIL_PAIRS = ((128, 1), (512, 4), (2048, 16))
N_DIL_GROUPS = len(DIL_PAIRS)
HEADS_A = 8
WIDTH_A = N_DIL_GROUPS * HEADS_A * HEAD_DIM
OUT_A = HEADS_A * HEAD_DIM
ROT_DIM_A = HEAD_DIM // 4
THETA_PARTIAL = 500000.0
HEADS_B_Q = 8
HEADS_B_KV = 2
WIDTH_B_Q = HEADS_B_Q * HEAD_DIM
WIDTH_B_KV = HEADS_B_KV * HEAD_DIM
OUT_B = WIDTH_B_Q
Q_BLOCK = 128
GRID_W = 64
THETA_AXIAL = 10000.0
N_BRANCHES = 2
IN_COLS = 3 * WIDTH_A + WIDTH_B_Q + 2 * WIDTH_B_KV + N_BRANCHES * D_MODEL
N_EXPERTS = 32
TOP_K = 4
D_FF = 1024
SWIGLU_LIMIT = 7.0
SWIGLU_ALPHA = 1.702
EXPERT_BLOCK = 128


def rmsnorm(x, g):
    xf = x.astype(jnp.float32)
    y = xf * lax.rsqrt(jnp.mean(xf * xf, axis=-1, keepdims=True) + EPS)
    return (y * g).astype(x.dtype)

def rope(x, pos, theta):
    half = x.shape[-1] // 2
    inv = theta ** (-(jnp.arange(half, dtype=jnp.float32) / half))
    ang = pos.astype(jnp.float32)[:, None] * inv[None, :]
    cos, sin = jnp.cos(ang)[:, None, :], jnp.sin(ang)[:, None, :]
    xf = x.astype(jnp.float32)
    x1, x2 = xf[..., :half], xf[..., half:]
    return jnp.concatenate([x1 * cos - x2 * sin, x2 * cos + x1 * sin], axis=-1).astype(x.dtype)

def partial_rope(x, pos):
    return jnp.concatenate([rope(x[..., :ROT_DIM_A], pos, THETA_PARTIAL), x[..., ROT_DIM_A:]], axis=-1)

def axial_rope(x, row, col):
    h = x.shape[-1] // 2
    return jnp.concatenate([rope(x[..., :h], row, THETA_AXIAL), rope(x[..., h:], col, THETA_AXIAL)], axis=-1)

def _pad_axis3(x, lo, hi):
    return jnp.pad(x, ((0, 0), (0, 0), (0, 0), (lo, hi), (0, 0)))

def dilated_window_attention(q, k, v, window, dil):
    b, s, h, e = q.shape
    half = window // (2 * dil)
    L = s // dil
    nb = -(-L // half)
    lp = nb * half
    pad = lp - L

    def to_sub(t):
        return t.reshape(b, L, dil, h, e).transpose(0, 2, 3, 1, 4)

    qs, ks, vs = to_sub(q), to_sub(k), to_sub(v)
    qb = _pad_axis3(qs, 0, pad).reshape(b, dil, h, nb, half, e)

    def windows(t):
        tp = _pad_axis3(t, half, pad + half).reshape(b, dil, h, nb + 2, half, e)
        return jnp.concatenate([tp[:, :, :, :-2], tp[:, :, :, 1:-1], tp[:, :, :, 2:]], axis=4)

    kw, vw = windows(ks), windows(vs)
    sc = jnp.einsum('bdhnqe,bdhnke->bdhnqk', qb, kw).astype(jnp.float32) * SCALE
    blk = jnp.arange(nb)[:, None, None]
    qi = blk * half + jnp.arange(half)[None, :, None]
    ki = (blk - 1) * half + jnp.arange(3 * half)[None, None, :]
    valid = (jnp.abs(ki - qi) <= half) & (ki >= 0) & (ki < L)
    sc = jnp.where(valid, sc, NEG)
    lse = jax.nn.logsumexp(sc, axis=-1)
    p = jnp.exp(sc - lse[..., None])
    o = jnp.einsum('bdhnqk,bdhnke->bdhnqe', p.astype(v.dtype), vw)
    o = o.reshape(b, dil, h, lp, e)[:, :, :, :L].transpose(0, 3, 1, 2, 4).reshape(b, s, h, e)
    lse = lse.reshape(b, dil, h, lp)[..., :L].transpose(0, 3, 1, 2).reshape(b, s, h)
    return o, lse

def gqa_blocked_attention(q, k, v):
    b, s, hq, e = q.shape
    hkv = k.shape[2]
    g = hq // hkv
    nq = s // Q_BLOCK
    qb = q.reshape(b, nq, Q_BLOCK, hkv, g, e).transpose(1, 0, 3, 4, 2, 5)
    kt = k.transpose(0, 2, 1, 3)
    vt = v.transpose(0, 2, 1, 3)

    def one_block(qblk):
        sc = jnp.einsum('bkgqe,bkse->bkgqs', qblk, kt).astype(jnp.float32) * SCALE
        p = jax.nn.softmax(sc, axis=-1)
        return jnp.einsum('bkgqs,bkse->bkgqe', p.astype(vt.dtype), vt)

    ob = lax.map(one_block, qb)
    return ob.transpose(1, 0, 4, 2, 3, 5).reshape(b, s, hq * e)

def moe_ffn(h, w_router, b_router, w_gate_up, b_gate_up, w_down, b_down):
    t, d = h.shape
    logits = (h @ w_router).astype(jnp.float32) + b_router
    topv, idx = lax.top_k(logits, TOP_K)
    gates = jax.nn.softmax(topv, axis=-1)
    a = t * TOP_K
    flat_e = idx.reshape(a)
    flat_w = gates.reshape(a)
    flat_tok = jnp.arange(a) // TOP_K
    order = jnp.argsort(flat_e)
    e_s, tok_s, w_s = flat_e[order], flat_tok[order], flat_w[order]
    counts = jnp.bincount(flat_e, length=N_EXPERTS)
    starts = jnp.cumsum(counts) - counts
    padded = ((counts + EXPERT_BLOCK - 1) // EXPERT_BLOCK) * EXPERT_BLOCK
    pends = jnp.cumsum(padded)
    pstarts = pends - padded
    dest = pstarts[e_s] + (jnp.arange(a) - starts[e_s])
    p_rows = a + N_EXPERTS * EXPERT_BLOCK
    n_blk = p_rows // EXPERT_BLOCK
    block_e = jnp.clip(jnp.searchsorted(pends, jnp.arange(n_blk) * EXPERT_BLOCK, side='right'), 0, N_EXPERTS - 1)
    xbuf = jnp.zeros((p_rows, d), h.dtype).at[dest].set(h[tok_s])
    wbuf = jnp.zeros((p_rows,), jnp.float32).at[dest].set(w_s)
    tbuf = jnp.zeros((p_rows,), jnp.int32).at[dest].set(tok_s.astype(jnp.int32))

    def expert_block(args):
        xblk, e = args
        gu = xblk @ w_gate_up[e] + b_gate_up[e]
        gate = jnp.minimum(gu[:, :D_FF], SWIGLU_LIMIT)
        up = jnp.clip(gu[:, D_FF:], -SWIGLU_LIMIT, SWIGLU_LIMIT)
        act = (up + 1.0) * (gate * jax.nn.sigmoid(SWIGLU_ALPHA * gate))
        return act @ w_down[e] + b_down[e]

    ybuf = lax.map(expert_block, (xbuf.reshape(n_blk, EXPERT_BLOCK, d), block_e)).reshape(p_rows, d)
    out = jnp.zeros((t, d), jnp.float32).at[tbuf].add(ybuf.astype(jnp.float32) * wbuf[:, None])
    return out

def first_inputs(seed: int = 0) -> dict:
    key = jax.random.key(seed)
    ks = jax.random.split(key, 18)
    f32 = jnp.float32
    nrm = lambda k, shp: jax.random.normal(k, shp, f32)
    return {
        "x": nrm(ks[0], (BATCH, SEQ, D_MODEL)),
        "norm_mix_g": 1.0 + 0.02 * nrm(ks[1], (D_MODEL,)),
        "w_in": nrm(ks[2], (D_MODEL, IN_COLS)) * D_MODEL ** -0.5,
        "b_gate": 0.1 * nrm(ks[3], (N_BRANCHES, D_MODEL)),
        "qn_a": 1.0 + 0.02 * nrm(ks[4], (N_DIL_GROUPS, HEAD_DIM)),
        "kn_a": 1.0 + 0.02 * nrm(ks[5], (N_DIL_GROUPS, HEAD_DIM)),
        "qn_b": 1.0 + 0.02 * nrm(ks[6], (HEAD_DIM,)),
        "kn_b": 1.0 + 0.02 * nrm(ks[7], (HEAD_DIM,)),
        "w_proj_a": nrm(ks[8], (OUT_A, D_MODEL)) * OUT_A ** -0.5,
        "w_proj_b": nrm(ks[9], (OUT_B, D_MODEL)) * OUT_B ** -0.5,
        "w_out": nrm(ks[10], (D_MODEL, D_MODEL)) * D_MODEL ** -0.5,
        "norm_ffn_g": 1.0 + 0.02 * nrm(ks[11], (D_MODEL,)),
        "w_router": nrm(ks[12], (D_MODEL, N_EXPERTS)) * D_MODEL ** -0.5,
        "b_router": 0.01 * nrm(ks[13], (N_EXPERTS,)),
        "w_gate_up": nrm(ks[14], (N_EXPERTS, D_MODEL, 2 * D_FF)) * D_MODEL ** -0.5,
        "b_gate_up": 0.02 * nrm(ks[15], (N_EXPERTS, 2 * D_FF)),
        "w_down": nrm(ks[16], (N_EXPERTS, D_FF, D_MODEL)) * D_FF ** -0.5,
        "b_down": 0.02 * nrm(ks[17], (N_EXPERTS, D_MODEL)),
    }

def first_block(x, norm_mix_g, w_in, b_gate, qn_a, kn_a, qn_b, kn_b, w_proj_a, w_proj_b, w_out,
              norm_ffn_g, w_router, b_router, w_gate_up, b_gate_up, w_down, b_down):
    b, s, d = x.shape
    pos = jnp.arange(s)
    rows = s // GRID_W
    row = jnp.repeat(jnp.arange(rows), GRID_W)
    col = jnp.tile(jnp.arange(GRID_W), rows)
    split_at = list(np.cumsum([3 * WIDTH_A, WIDTH_B_Q, WIDTH_B_KV, WIDTH_B_KV]))

    for _layer in range(DEPTH):
        h = rmsnorm(x, norm_mix_g)
        proj = h @ w_in
        qkv_a, q_b, k_b, v_b, gate_logits = jnp.split(proj, split_at, axis=-1)

        qkv_a = qkv_a.reshape(b, s, 3, N_DIL_GROUPS, HEADS_A, HEAD_DIM)
        outs, lses = [], []
        for gi, (window, dil) in enumerate(DIL_PAIRS):
            qg = partial_rope(rmsnorm(qkv_a[:, :, 0, gi], qn_a[gi]), pos)
            kg = partial_rope(rmsnorm(qkv_a[:, :, 1, gi], kn_a[gi]), pos)
            og, lg = dilated_window_attention(qg, kg, qkv_a[:, :, 2, gi], window, dil)
            outs.append(og)
            lses.append(lg)
        wts = jax.nn.softmax(jnp.stack(lses, axis=0), axis=0)
        o_a = jnp.sum(wts[..., None] * jnp.stack(outs, axis=0).astype(jnp.float32), axis=0)
        o_a = o_a.astype(x.dtype).reshape(b, s, OUT_A)

        qb = axial_rope(rmsnorm(q_b.reshape(b, s, HEADS_B_Q, HEAD_DIM), qn_b), row, col)
        kb = axial_rope(rmsnorm(k_b.reshape(b, s, HEADS_B_KV, HEAD_DIM), kn_b), row, col)
        vb = v_b.reshape(b, s, HEADS_B_KV, HEAD_DIM)
        o_b = gqa_blocked_attention(qb, kb, vb)

        gates = jax.nn.sigmoid(gate_logits.reshape(b, s, N_BRANCHES, d) + b_gate)
        merged = gates[:, :, 0] * (o_a @ w_proj_a) + gates[:, :, 1] * (o_b @ w_proj_b)
        x = x + (merged @ w_out).astype(x.dtype)

        h2 = rmsnorm(x, norm_ffn_g).reshape(b * s, d)
        ff = moe_ffn(h2, w_router, b_router, w_gate_up, b_gate_up, w_down, b_down)
        x = x + ff.reshape(b, s, d).astype(x.dtype)
    return x


DEPTH_2 = 2

CHUNK = 64
NEG_INF = -1e30
N_BRANCH = 3
BR_WIDTH = 512

SGU_BLOCK = 128
SGU_GROUPS = 8
SGU_GROUP_DIM = BR_WIDTH // SGU_GROUPS

MLA_HEADS = 8
MLA_NOPE = 64
MLA_ROPE = 32
MLA_V = 64
MLA_QK = MLA_NOPE + MLA_ROPE
MLA_Q_RANK = 256
MLA_KV_RANK = 128
ROPE_BASE = 10000.0

CA_HEADS = 8
CA_HEAD_DIM = BR_WIDTH // CA_HEADS
LEFT_CHUNKS = 8
BAND = (LEFT_CHUNKS + 1) * CHUNK
REL_CLIP = 128

IN_WIDTHS = (BR_WIDTH, BR_WIDTH, BR_WIDTH,
             MLA_Q_RANK, MLA_KV_RANK, MLA_ROPE, BR_WIDTH,
             BR_WIDTH, BR_WIDTH, BR_WIDTH, BR_WIDTH,
             N_BRANCH * D_MODEL)
D_IN = sum(IN_WIDTHS)


def rmsnorm_2(x, g):
    xf = x.astype(jnp.float32)
    y = xf * lax.rsqrt(jnp.mean(xf * xf, axis=-1, keepdims=True) + EPS)
    return (y * g.astype(jnp.float32)).astype(x.dtype)

def layernorm(x, g, b):
    xf = x.astype(jnp.float32)
    mu = jnp.mean(xf, axis=-1, keepdims=True)
    xc = xf - mu
    y = xc * lax.rsqrt(jnp.mean(xc * xc, axis=-1, keepdims=True) + EPS)
    return (y * g.astype(jnp.float32) + b.astype(jnp.float32)).astype(x.dtype)

def apply_rope(x, pos):
    half = x.shape[-1] // 2
    inv = ROPE_BASE ** (-jnp.arange(half, dtype=jnp.float32) / half)
    ang = pos.astype(jnp.float32)[:, None] * inv[None, :]
    cos = jnp.cos(ang)[:, None, :]
    sin = jnp.sin(ang)[:, None, :]
    xf = x.astype(jnp.float32)
    x1, x2 = xf[..., :half], xf[..., half:]
    return jnp.concatenate([x1 * cos - x2 * sin, x1 * sin + x2 * cos], axis=-1).astype(x.dtype)

def sgu_mixer(u, v, ln_g, ln_b, w_s, b_s):
    B, S, _ = u.shape
    nb = S // SGU_BLOCK
    v = layernorm(v, ln_g, ln_b)
    vb = v.reshape(B, nb, SGU_BLOCK, SGU_GROUPS, SGU_GROUP_DIM)
    tri = jnp.tril(jnp.ones((SGU_BLOCK, SGU_BLOCK), dtype=bool))
    ws = jnp.where(tri[None], w_s, 0.0).astype(v.dtype)
    mixed = jnp.einsum('gts,bnsgc->bntgc', ws, vb) + b_s.T.astype(v.dtype)[None, None, :, :, None]
    return u * mixed.reshape(B, S, BR_WIDTH)

def mla_mixer(q_down, kv_down, k_rope_in, q_norm_g, kv_norm_g, w_uq, w_ukv, pos):
    B, S, _ = q_down.shape
    cq = rmsnorm_2(q_down, q_norm_g)
    q = (cq @ w_uq).reshape(B, S, MLA_HEADS, MLA_QK)
    q = jnp.concatenate([q[..., :MLA_NOPE], apply_rope(q[..., MLA_NOPE:], pos)], axis=-1)
    ckv = rmsnorm_2(kv_down, kv_norm_g)
    kv = (ckv @ w_ukv).reshape(B, S, MLA_HEADS, MLA_NOPE + MLA_V)
    k_nope, v = kv[..., :MLA_NOPE], kv[..., MLA_NOPE:]
    k_r = apply_rope(k_rope_in[:, :, None, :], pos)
    k = jnp.concatenate([k_nope, jnp.broadcast_to(k_r, (B, S, MLA_HEADS, MLA_ROPE))], axis=-1)
    scale = MLA_QK ** -0.5
    nqb = S // Q_BLOCK
    qb = q.reshape(B, nqb, Q_BLOCK, MLA_HEADS, MLA_QK).transpose(1, 0, 2, 3, 4)
    key_chunk = jnp.arange(S) // CHUNK

    def block(args):
        qi, bi = args
        s = jnp.einsum('bqhd,bkhd->bhqk', qi, k).astype(jnp.float32) * scale
        q_chunk = (bi * Q_BLOCK + jnp.arange(Q_BLOCK)) // CHUNK
        mask = key_chunk[None, :] <= q_chunk[:, None]
        s = jnp.where(mask[None, None], s, NEG_INF)
        p = jax.nn.softmax(s, axis=-1).astype(v.dtype)
        return jnp.einsum('bhqk,bkhd->bqhd', p, v)

    o = lax.map(block, (qb, jnp.arange(nqb)))
    return o.transpose(1, 0, 2, 3, 4).reshape(B, S, MLA_HEADS * MLA_V)

def chunk_band_mixer(q, k, v, rel_table):
    B, S, _ = q.shape
    nc = S // CHUNK
    pad = LEFT_CHUNKS * CHUNK
    q = q.reshape(B, S, CA_HEADS, CA_HEAD_DIM)
    k = k.reshape(B, S, CA_HEADS, CA_HEAD_DIM)
    v = v.reshape(B, S, CA_HEADS, CA_HEAD_DIM)
    kp = jnp.pad(k, ((0, 0), (pad, 0), (0, 0), (0, 0)))
    vp = jnp.pad(v, ((0, 0), (pad, 0), (0, 0), (0, 0)))
    qc = q.reshape(B, nc, CHUNK, CA_HEADS, CA_HEAD_DIM).transpose(1, 0, 2, 3, 4)
    i = jnp.arange(CHUNK)
    j = jnp.arange(BAND)
    dist = i[:, None] + pad - j[None, :]
    idx = jnp.clip(dist, -REL_CLIP, REL_CLIP) + REL_CLIP
    bias = rel_table[:, idx].astype(jnp.float32)
    scale = CA_HEAD_DIM ** -0.5

    def chunk(args):
        qi, ci = args
        kb = lax.dynamic_slice_in_dim(kp, ci * CHUNK, BAND, axis=1)
        vb = lax.dynamic_slice_in_dim(vp, ci * CHUNK, BAND, axis=1)
        s = jnp.einsum('bqhd,bkhd->bhqk', qi, kb).astype(jnp.float32) * scale + bias[None]
        valid = j >= (LEFT_CHUNKS - ci) * CHUNK
        s = jnp.where(valid[None, None, None, :], s, NEG_INF)
        p = jax.nn.softmax(s, axis=-1).astype(vb.dtype)
        return jnp.einsum('bhqk,bkhd->bqhd', p, vb)

    o = lax.map(chunk, (qc, jnp.arange(nc)))
    return o.transpose(1, 0, 2, 3, 4).reshape(B, S, BR_WIDTH)

def second_inputs(seed: int = 0) -> dict:
    key = jax.random.key(seed)
    ks = jax.random.split(key, 16)
    f32 = jnp.float32
    L, D = DEPTH_2, D_MODEL
    nrm = lambda k, shape, s: jax.random.normal(k, shape, f32) * s
    return {
        "x": jax.random.normal(ks[0], (BATCH, SEQ, D), f32),
        "w_in": nrm(ks[1], (L, D, D_IN), D ** -0.5),
        "pre_g": 1.0 + nrm(ks[2], (L, D), 0.1),
        "post_g": 1.0 + nrm(ks[3], (L, D), 0.1),
        "sgu_ln_g": 1.0 + nrm(ks[4], (L, BR_WIDTH), 0.1),
        "sgu_ln_b": nrm(ks[5], (L, BR_WIDTH), 0.02),
        "sgu_w": nrm(ks[6], (L, SGU_GROUPS, SGU_BLOCK, SGU_BLOCK), SGU_BLOCK ** -0.5),
        "sgu_b": 1.0 + nrm(ks[7], (L, SGU_GROUPS, SGU_BLOCK), 0.1),
        "mla_q_norm_g": 1.0 + nrm(ks[8], (L, MLA_Q_RANK), 0.1),
        "mla_kv_norm_g": 1.0 + nrm(ks[9], (L, MLA_KV_RANK), 0.1),
        "mla_w_uq": nrm(ks[10], (L, MLA_Q_RANK, MLA_HEADS * MLA_QK), MLA_Q_RANK ** -0.5),
        "mla_w_ukv": nrm(ks[11], (L, MLA_KV_RANK, MLA_HEADS * (MLA_NOPE + MLA_V)), MLA_KV_RANK ** -0.5),
        "ca_rel_bias": nrm(ks[12], (L, CA_HEADS, 2 * REL_CLIP + 1), 0.5),
        "w_branch": nrm(ks[13], (L, N_BRANCH, BR_WIDTH, D), BR_WIDTH ** -0.5),
        "gate_b": nrm(ks[14], (L, N_BRANCH, D), 0.1),
        "w_out": nrm(ks[15], (L, D, D), D ** -0.5),
    }

def second_block(x, w_in, pre_g, post_g, sgu_ln_g, sgu_ln_b, sgu_w, sgu_b,
              mla_q_norm_g, mla_kv_norm_g, mla_w_uq, mla_w_ukv, ca_rel_bias,
              w_branch, gate_b, w_out):
    B, S, D = x.shape
    pos = jnp.arange(S)
    offsets = [0]
    for w in IN_WIDTHS:
        offsets.append(offsets[-1] + w)
    for l in range(DEPTH_2):
        xn = rmsnorm_2(x, pre_g[l])
        proj = xn @ w_in[l]
        (u_a, v_a, z_a, qd_b, kvd_b, kr_b, z_b,
         q_c, k_c, v_c, z_c, g_logits) = [proj[..., offsets[n]:offsets[n + 1]] for n in range(len(IN_WIDTHS))]
        y_a = sgu_mixer(u_a, v_a, sgu_ln_g[l], sgu_ln_b[l], sgu_w[l], sgu_b[l]) * jax.nn.silu(z_a)
        y_b = mla_mixer(qd_b, kvd_b, kr_b, mla_q_norm_g[l], mla_kv_norm_g[l],
                        mla_w_uq[l], mla_w_ukv[l], pos) * jax.nn.silu(z_b)
        y_c = chunk_band_mixer(q_c, k_c, v_c, ca_rel_bias[l]) * jax.nn.silu(z_c)
        ys = jnp.stack([y_a, y_b, y_c], axis=2)
        br = jnp.einsum('bsnc,ncd->bsnd', ys, w_branch[l])
        gates = jax.nn.sigmoid(g_logits.reshape(B, S, N_BRANCH, D) + gate_b[l])
        merged = jnp.sum(gates * br, axis=2)
        x = x + rmsnorm_2(merged @ w_out[l], post_g[l])
    return x


def setup_inputs(seed=0):
    out = dict(first_inputs(seed))
    for name, value in second_inputs(seed + 1).items():
        if name != "x":
            out[name + "_2"] = value
    return out


def reference(
    x, norm_mix_g, w_in, b_gate, qn_a, kn_a, qn_b, kn_b, w_proj_a, w_proj_b, w_out, norm_ffn_g,
    w_router, b_router, w_gate_up, b_gate_up, w_down, b_down, w_in_2, pre_g_2, post_g_2,
    sgu_ln_g_2, sgu_ln_b_2, sgu_w_2, sgu_b_2, mla_q_norm_g_2, mla_kv_norm_g_2, mla_w_uq_2,
    mla_w_ukv_2, ca_rel_bias_2, w_branch_2, gate_b_2, w_out_2,
):
    x = first_block(
        x, norm_mix_g, w_in, b_gate, qn_a, kn_a, qn_b, kn_b, w_proj_a, w_proj_b, w_out,
        norm_ffn_g, w_router, b_router, w_gate_up, b_gate_up, w_down, b_down,
    )
    return second_block(
        x, w_in_2, pre_g_2, post_g_2, sgu_ln_g_2, sgu_ln_b_2, sgu_w_2, sgu_b_2, mla_q_norm_g_2,
        mla_kv_norm_g_2, mla_w_uq_2, mla_w_ukv_2, ca_rel_bias_2, w_branch_2, gate_b_2, w_out_2,
    )


_drawn_inputs = setup_inputs


def setup_inputs(seed=0):
    import zlib

    import numpy as np

    out = dict(_drawn_inputs(seed))
    spreads = {}
    factors = {'b_gate': 6.055,
     'kn_a': 4.745,
     'qn_b': 3.036,
     'b_gate_up': 3.193,
     'b_down': 3.562,
     'sgu_ln_b_2': 5.314,
     'mla_q_norm_g_2': 5.081,
     'mla_kv_norm_g_2': 3.425}
    for name, (base, spread) in spreads.items():
        noise = np.random.default_rng([zlib.crc32(name.encode()), seed]).standard_normal(out[name].shape)
        drawn = base * np.exp(spread * noise) if base else spread * noise
        out[name] = __import__('jax').numpy.asarray(drawn.astype(out[name].dtype))
    for name, factor in factors.items():
        out[name] = (out[name] * factor).astype(out[name].dtype)
    return out
```

```python
from contextlib import ExitStack

import numpy as np

import concourse.bass as bass
from concourse import mybir

P = 128
S = 512
TT = S // P
D = 1024
E = 64
EPS = 1e-6
NEG = -1e30
ATT_SCALE = E ** -0.5
DILATIONS = ((128, 1), (512, 4), (2048, 16))
GRID_W = 64
NE, TOPK, FF = 32, 4, 1024
LIMIT, ALPHA = 7.0, 1.702
NPOS = S + P
MAXBLK = S * TOPK // P + NE
MLA_SCALE = 96 ** -0.5

F32 = mybir.dt.float32
BF16 = mybir.dt.bfloat16
I32 = mybir.dt.int32
U32 = mybir.dt.uint32
ALU = mybir.AluOpType
ACT = mybir.ActivationFunctionType
AX = mybir.AxisListType



def rope_tables(dim, theta, pos):
    half = dim // 2
    inv = (theta ** (-(np.arange(half, dtype=np.float32) / np.float32(half)))).astype(np.float32)
    ang = pos.astype(np.float32)[:, None] * inv[None, :]
    c, s = np.cos(ang).astype(np.float32), np.sin(ang).astype(np.float32)
    return np.concatenate([c, c], 1), np.concatenate([-s, s], 1)


def tiled(a):
    return a.reshape(TT, P, -1).transpose(1, 0, 2).reshape(P, -1)


def window_masks():
    t = np.arange(S)
    ok = []
    for window, dil in DILATIONS:
        d = t[None, :] - t[:, None]
        ok.append((d % dil == 0) & (np.abs(d) <= (window // (2 * dil)) * dil))
    cols = []
    for i in range(TT):
        r = slice(i * P, (i + 1) * P)
        lo, hi = near(i)
        cols.append(np.concatenate([ok[2][r], ok[1][r], ok[0][r, lo * P:hi * P]], 1))
    return np.where(np.concatenate(cols, 1), 0.0, NEG).astype(np.float32)


def near(i):
    return max(0, i - 1), min(TT, i + 2)


def width_a(i):
    lo, hi = near(i)
    return 2 * S + (hi - lo) * P


def constant_parts():
    t = np.arange(S)
    r = np.arange(P)
    ca, sa = rope_tables(16, 500000.0, t)
    rc, rs = rope_tables(32, 10000.0, t // GRID_W)
    cc, cs = rope_tables(32, 10000.0, t % GRID_W)
    cm, sm = rope_tables(32, 10000.0, t)
    chunk = np.where((r[None, :] // 64) <= (r[:, None] // 64), 0.0, NEG)
    parts = [
        ("ident", np.eye(P)), ("ropeA_c", tiled(ca)), ("ropeA_s", tiled(sa)),
        ("ropeB_c", tiled(np.concatenate([rc, cc], 1))), ("ropeB_s", tiled(np.concatenate([rs, cs], 1))),
        ("ropeM_c", tiled(cm)), ("ropeM_s", tiled(sm)),
        ("chunk_mask", np.concatenate([np.zeros((P, S - P)), chunk], 1)), ("zeros", np.zeros((P, S))),
        ("before", (r[:, None] < r[None, :]) * 1.0), ("ones", np.ones((P, P))),
        ("tril_T", (r[:, None] <= r[None, :]) * 1.0),
        ("iota_e", np.tile(np.arange(NE), (P, 1))), ("iota_list", np.tile(np.arange(NE) * NPOS, (P, 1))),
        ("iota_j", np.tile(np.arange(MAXBLK + 1), (P, 1))),
        ("steps", np.tile(np.arange(TOPK) * P, (P, 1))),
    ]
    return [(n, np.ascontiguousarray(a, dtype=np.float32)) for n, a in parts]


class At(dict):

    def of(self, name):
        return self.get(name, 0)

    def step(self, by, times=1):
        for k, v in by.items():
            self[k] = self.of(k) + times * v

    def inside(self, i, by):
        c = At(self)
        for k, v in by.items():
            c[k] = self.of(k) + i * v
        return c


def build(nc, A, out):
    ctx = ExitStack()
    with ctx:
        consts = constant_parts()
        AR = ctx.enter_context(nc.sbuf_tensor("arena", [P, 53200], F32))
        PS = ctx.enter_context(nc.psum_tensor("banks", [P, 8, 512], F32))
        H2D = nc.dram_tensor("h2_rows", [S, D], F32, kind="Internal").ap()
        LIST = nc.dram_tensor("expert_lists", [(NE + 1) * NPOS, 1], I32, kind="Internal").ap()
        YD = nc.dram_tensor("expert_rows", [S * TOPK, D], F32, kind="Internal").ap()

        X, HT, W, CON = 0, 4096, 8192, 12288
        off = CON
        CO = {}
        for n, a in consts:
            CO[n] = off
            off += a.shape[1]
        NCONST = off - CON
        GAINS = off
        off += 512
        MASKA = off
        MW = sum(width_a(i) for i in range(TT))
        off += MW // 2
        RVAL = off
        off += 16
        SC = off
        PTS = SC + 3072
        QST = PTS + 1536
        SM = QST + 1536
        GROW = SM + 1024
        KST = GROW
        BIG = GROW + 1536
        LB = BIG + 6144
        assert LB + 20000 <= 53200, (BIG, LB)

        def v(o, n, p=P, p0=0):
            return AR[p0:p0 + p, o:o + n]

        def v2(o, a, b, p=P, p0=0):
            return AR[p0:p0 + p, o:o + a * b].rearrange("p (a b) -> p a b", a=a)

        def v3(o, a, b, c, p=P, p0=0):
            return AR[p0:p0 + p, o:o + a * b * c].rearrange("p (a b c) -> p a b c", a=a, b=b)

        def dyn(o, n, p=P, p0=0):
            return AR[p0:p0 + p, bass.ds(o, n)]

        ident = v(CO["ident"], P)
        x3 = v2(X, TT, D)
        hT = v2(HT, 8, S)
        Wh = [v2(W, 4, 512), v2(W + 2048, 4, 512)]

        names = ("const_in grow_in norm_sq norm_ms norm_sd norm_h tr tr_free "
                 "w0_in w1_in w0_free mm ev qk_ms qk_sd qk_ready "
                 "staged qk sm p_rdy pt_rdy pt_free pv o_done "
                 "gb_in sig_in sig_out applied "
                 "h2_out logit_mm top_rdy top_exp sel_rdy pos_mm addr_rdy list_in listed gathered gmat_rdy table_rdy "
                 "slot_in ch0 ch1 ch2 ch3 ch4 ch5 ch_free rows_in xt xt_free act_g sig_g act_rdy rows_out "
                 "y_rdy rsc_rdy tok_rdy scattered bdown_in comb0 comb1 comb2 comb3 fin_mm x_out "
                 "ws_in ws_rdy sgu_mm sgu_in ln_sd z_sig z_in lat_sq lat_ms lat_sd lat_rdy kv_rdy "
                 "bias_rows0 bias_rows1 seen post_ms post_sd "
                 "pe_done act_done dve_done pool_done").split()
        SEM = {n: ctx.enter_context(nc.semaphore(n)) for n in names}

        BASE = 16
        FROM_ZERO = set("const_in grow_in w0_in w1_in h2_out gb_in list_in listed gathered slot_in ch0 ch1 ch2 "
                        "ch3 ch4 ch5 rows_in scattered bdown_in comb0 comb1 comb2 comb3 x_out ws_in bias_rows0 "
                        "bias_rows1 seen pe_done act_done dve_done pool_done".split())

        def up(count):
            return count + BASE

        def apart(eng, count):
            if not isinstance(count, int):
                eng.sem_inc(SEM["seen"])

        V, AC, G, PE = nc.vector, nc.scalar, nc.gpsimd, nc.tensor
        ENG = {"pe": PE, "act": AC, "dve": V, "pool": G}
        def fence(who, eng, c):
            ENG[who].drain().then_inc(SEM[who + "_done"], 1)
            for other in ("pe", "act", "dve", "pool"):
                if other != who:
                    eng.wait_ge(SEM[other + "_done"], c.of("fence") + 1)
                    apart(eng, c.of("fence") + 1)
            c["fence"] = c.of("fence") + 1

        def sp_after(sp, c):
            for other in ("pe", "act", "dve", "pool"):
                sp.wait_ge(SEM[other + "_done"], c.of("fence"))
                apart(sp, c.of("fence"))

        class Stage:

            def __init__(self, counts, sp=None, pe=None, act=None, dve=None, pool=None):
                self.counts = counts
                self.of_sp, self.of_pe, self.of_act, self.of_dve, self.of_pool = sp, pe, act, dve, pool

            def done(self, c):
                c.step(self.counts)

            def sp(self, sp, c):
                c["fence"] = c.of("fence") + 1
                if self.of_sp:
                    self.of_sp(sp, c)
                self.done(c)

            def pe(self, pe, c):
                fence("pe", pe, c)
                if self.of_pe:
                    self.of_pe(pe, c)
                self.done(c)

            def act(self, act, c):
                fence("act", act, c)
                if self.of_act:
                    self.of_act(act, c)
                self.done(c)

            def dve(self, dve, c):
                fence("dve", dve, c)
                if self.of_dve:
                    self.of_dve(dve, c)
                self.done(c)

            def pool(self, pool, c):
                fence("pool", pool, c)
                if self.of_pool:
                    self.of_pool(pool, c)
                self.done(c)

        def tr_pe(pe, c, k, ins):
            n = c.of("tr") + k
            pe.wait_ge(SEM["tr_free"], up(n - 3))
            apart(pe, n - 3)
            for q, a in enumerate(ins):
                m = 1
                for s_ in a.shape[1:]:
                    m *= s_
                last = PE.transpose(PS[0:m, 4 + k % 4, q * P:q * P + a.shape[0]], a, ident)
            last.then_inc(SEM["tr"], 1)

        def tr_out(eng, who, c, k, dst, cnt, m=P):
            eng.wait_ge(SEM["tr"], up(c.of("tr") + k + 1))
            apart(eng, c.of("tr") + k + 1)
            src = PS[0:m, 4 + k % 4, 0:cnt * P].rearrange("p (a t) -> p a t", a=cnt)
            if who == "act":
                AC.activation(dst, src, ACT.Copy).then_inc(SEM["tr_free"], 1)
            else:
                V.tensor_copy(dst, src).then_inc(SEM["tr_free"], 1)

        def dense_sp(sp, c, k, src):
            T = c.of("T") + k
            for h in range(2):
                for dst, s_ in [src(h)]:
                    if h == 0:
                        sp.wait_ge(SEM["w0_free"], up(T))
                        apart(sp, T)
                    else:
                        sp.wait_ge(SEM["mm"], up(4 * T))
                        apart(sp, 4 * T)
                    sp.dma_start(dst, s_).then_inc(SEM["w0_in" if h == 0 else "w1_in"], 16)

        def dense_pe(pe, c, k, lhsT, kt, ncols, before=None, after_fence=False):
            T = c.of("T") + k
            for h in range(2):
                pe.wait_ge(SEM["w0_in" if h == 0 else "w1_in"], 16 * T + 16)
                apart(pe, 16 * T + 16)
                for tt in range(TT):
                    if h == 0:
                        pe.wait_ge(SEM["ev"], up(4 * T + tt - 3))
                        apart(pe, 4 * T + tt - 3)
                    elif before:
                        before(tt)
                    if kt == 1:
                        hc = ncols // 2
                        last = PE.matmul(PS[:, tt, h * hc:(h + 1) * hc], lhsT(0, tt), Wh[h][:, 0, 0:hc],
                                         start=True, stop=True)
                    else:
                        for q in range(kt // 2):
                            kk = h * (kt // 2) + q
                            last = PE.matmul(PS[:, tt, 0:ncols], lhsT(kk, tt), Wh[h][:, q, 0:ncols],
                                             start=(kk == 0), stop=(kk == kt - 1))
                    if h == 1:
                        last.then_inc(SEM["mm"], 1)
                if h == 0:
                    last.then_inc(SEM["w0_free"], 1)

        def unit(c, k, tt):
            return 4 * (c.of("T") + k) + tt + 1

        def rows(ap2d, kt, h, c0, ncols):
            src = ap2d.rearrange("(k p) n -> p k n", p=P)[:, h * (kt // 2):(h + 1) * (kt // 2), bass.ds(c0, ncols)]
            return Wh[h][:, 0:kt // 2, 0:ncols], src

        def norm_stage(gain, HB, get_x=None, want_h2=False):
            ss = v(SM, 4)
            sd = v(SM + 4, 4)
            hb = v2(HB, TT, D)

            def sp_(sp, c):
                sp_after(sp, c)
                sp.dma_start(v(GROW, D), gain(c).partition_broadcast(P)).then_inc(SEM["grow_in"], 16)
                if want_h2:
                    sp.wait_ge(SEM["norm_h"], up(c.of("norm_h") + 4))
                    apart(sp, c.of("norm_h") + 4)
                    sp.dma_start(H2D.rearrange("(t p) d -> p t d", p=P), hb).then_inc(SEM["h2_out"], 16)

            def act_(act, c):
                for tt in range(TT):
                    last = AC.activation(hb[:, tt], x3[:, tt], ACT.Square, accum_out=ss[:, tt:tt + 1])
                last.then_inc(SEM["norm_sq"], 1)
                act.wait_ge(SEM["norm_ms"], up(c.of("norm_ms") + 1))
                apart(act, c.of("norm_ms") + 1)
                AC.activation(sd, ss, ACT.Sqrt).then_inc(SEM["norm_sd"], 1)
                for tt in range(TT):
                    for q in range(2):
                        tr_out(act, "act", c, 2 * tt + q, hT[:, 4 * q:4 * q + 4, tt * P:(tt + 1) * P], 4)

            def dve_(dve, c):
                dve.wait_ge(SEM["norm_sq"], up(c.of("norm_sq") + 1))
                apart(dve, c.of("norm_sq") + 1)
                V.tensor_scalar(ss, ss, 1.0 / D, EPS, ALU.mult, ALU.add).then_inc(SEM["norm_ms"], 1)
                dve.wait_ge(SEM["norm_sd"], up(c.of("norm_sd") + 1))
                apart(dve, c.of("norm_sd") + 1)
                V.reciprocal(sd, sd)
                V.drain()
                dve.wait_ge(SEM["grow_in"], 16 * c.of("grow") + 16)
                apart(dve, 16 * c.of("grow") + 16)
                for tt in range(TT):
                    V.scalar_tensor_tensor(hb[:, tt], x3[:, tt], sd[:, tt:tt + 1], v(GROW, D),
                                           ALU.mult, ALU.mult).then_inc(SEM["norm_h"], 1)

            def pe_(pe, c):
                for tt in range(TT):
                    pe.wait_ge(SEM["norm_h"], up(c.of("norm_h") + tt + 1))
                    apart(pe, c.of("norm_h") + tt + 1)
                    for q in range(2):
                        tr_pe(pe, c, 2 * tt + q, [hb[:, tt, (4 * q + a) * P:(4 * q + a + 1) * P] for a in range(4)])

            return Stage({"norm_sq": 1, "norm_ms": 1, "norm_sd": 1, "norm_h": 4, "grow": 1, "tr": 8},
                  sp=sp_, act=act_, dve=dve_, pe=pe_)

        ST = [v(SC + 512 * tt, 512) for tt in range(TT)]
        SQ = [v(PTS + 512 * (tt % 2), 512) for tt in range(TT)]

        def rotate(dst, src, tc, ts, nh, nb, half, paired=False):
            w = nb * 2 * half
            cu = v(QST, nh * w).rearrange("p (h b) -> p h b", h=nh)
            cv = v(QST + 512, nh * w).rearrange("p (h b j e) -> p h b j e", h=nh, b=nb, j=2)
            V.tensor_tensor(cu, src, tc.unsqueeze(1).to_broadcast([P, nh, w]), ALU.mult)
            s5 = src.rearrange("p h (b j e) -> p h b j e", b=nb, j=2)
            t4 = ts.rearrange("p (b j e) -> p b j e", b=nb, j=2)
            for b in range(nb):
                for j in range(2):
                    V.tensor_tensor(cv[:, :, b, j], s5[:, :, b, 1 - j],
                                    t4[:, b, j].unsqueeze(1).to_broadcast([P, nh, half]), ALU.mult)
            V.drain()
            cv3 = v(QST + 512, nh * w).rearrange("p (h b) -> p h b", h=nh)
            if paired:
                def by(a):
                    return a.rearrange("p (s a) e -> p s a e", s=2)
                to = dst.rearrange("p (a s) e -> p s a e", s=2)
                return V.tensor_tensor(to, by(cu), by(cv3), ALU.add)
            return V.tensor_tensor(dst, cu, cv3, ALU.add)

        def qk_tile(k, cfg, prev):
            nh = cfg["nh"]

            def pe_(pe, c):
                def before(tt):
                    if prev:
                        pe.wait_ge(SEM["qk_ready"], up(c.of("qk_ready") + 4 * (k - 1) + tt + 1))
                        apart(pe, c.of("qk_ready") + 4 * (k - 1) + tt + 1)
                        tr_pe(pe, c, 4 * (k - 1) + tt, prev["ins"](tt))
                dense_pe(pe, c, k, lambda kk, tt: hT[:, kk, tt * P:(tt + 1) * P], 8, cfg["ncols"], before)

            def act_(act, c):
                for tt in range(TT):
                    if prev:
                        tr_out(act, "act", c, 4 * (k - 1) + tt, prev["dst"](c, k - 1, tt), prev["cnt"])
                    act.wait_ge(SEM["mm"], up(unit(c, k, tt)))
                    apart(act, unit(c, k, tt))
                    AC.activation(ST[tt][:, 0:cfg["ncols"]], PS[:, tt, 0:cfg["ncols"]], ACT.Copy)
                    if cfg.get("v_out"):
                        AC.activation(cfg["v_out"](tt), PS[:, tt, nh * E:cfg["ncols"]], ACT.Copy)
                    act.wait_ge(SEM["qk_ms"], up(c.of("qk_ms") + 4 * k + tt - 1 if k + tt else c.of("qk_ms")))
                    apart(act, c.of("qk_ms") + 4 * k + tt - 1 if k + tt else c.of("qk_ms"))
                    AC.activation(SQ[tt][:, 0:nh * E], PS[:, tt, 0:nh * E], ACT.Square).then_inc(SEM["ev"], 1)
                    act.wait_ge(SEM["qk_ms"], up(c.of("qk_ms") + 4 * k + tt + 1))
                    apart(act, c.of("qk_ms") + 4 * k + tt + 1)
                    AC.activation(v(SM + 16 + 8 * tt, nh), v(SM + 16 + 8 * tt, nh), ACT.Sqrt).then_inc(SEM["qk_sd"], 1)

            def dve_(dve, c):
                for tt in range(TT):
                    ms = v(SM + 16 + 8 * tt, nh)
                    st = ST[tt][:, 0:nh * E].rearrange("p (h e) -> p h e", h=nh)
                    dve.wait_ge(SEM["ev"], up(unit(c, k, tt)))
                    apart(dve, unit(c, k, tt))
                    V.tensor_reduce(ms, SQ[tt][:, 0:nh * E].rearrange("p (h e) -> p h e", h=nh), AX.X, ALU.add)
                    V.drain()
                    V.tensor_scalar(ms, ms, 1.0 / E, EPS, ALU.mult, ALU.add).then_inc(SEM["qk_ms"], 1)
                    dve.wait_ge(SEM["qk_sd"], up(c.of("qk_sd") + 4 * k + tt + 1))
                    apart(dve, c.of("qk_sd") + 4 * k + tt + 1)
                    V.reciprocal(ms, ms)
                    V.drain()
                    V.tensor_tensor(st, st, ms.unsqueeze(2).to_broadcast([P, nh, E]), ALU.mult)
                    V.drain()
                    V.tensor_tensor(st, st, cfg["gain"](c, k).unsqueeze(1).to_broadcast([P, nh, E]), ALU.mult)
                    V.drain()
                    nb, half, tc, ts = cfg["rope"]
                    w = nb * 2 * half
                    rot = st[:, :, 0:w]
                    rotate(rot, rot, v(tc + w * tt, w), v(ts + w * tt, w), nh, nb, half,
                           cfg.get("paired")).then_inc(SEM["qk_ready"], 1)

            return {"pe": pe_, "act": act_, "dve": dve_}

        QKT, VA, QBT, KBT, VB, OA, OB = (BIG + o for o in (0, 12288, 18432, 20480, 20992, 21504, 23552))
        w_in = A["w_in"]
        RA = (1, 8, CO["ropeA_c"], CO["ropeA_s"])
        RB = (2, 16, CO["ropeB_c"], CO["ropeB_s"])

        def pair_ins(tt):
            return [ST[tt][:, a * P:(a + 1) * P] for a in range(4)]

        def dst_pairs(base):
            def dst(c, k, tt):
                o = (c.of("tile") + k) * 2048 + base
                return dyn(o, 2048).rearrange("p (a t) -> p a t", a=4)[:, :, tt * P:(tt + 1) * P]
            return dst

        cfgA = {"nh": 8, "ncols": 512, "rope": RA, "ins": pair_ins, "cnt": 4, "dst": dst_pairs(QKT),
                "gain": lambda c, k: dyn(GAINS + (c.of("tile") + k) * E, E)}
        cfgQB = {"nh": 8, "ncols": 512, "rope": RB, "cnt": 4, "ins": pair_ins, "paired": True,
                 "dst": lambda c, k, tt: v2(QBT, 4, S)[:, :, tt * P:(tt + 1) * P],
                 "gain": lambda c, k: v(GAINS + 6 * E, E)}
        cfgKB = {"nh": 2, "ncols": 256, "rope": RB, "cnt": 1,
                 "ins": lambda tt: [ST[tt][:, 0:P]],
                 "dst": lambda c, k, tt: v2(KBT, 1, S)[:, :, tt * P:(tt + 1) * P],
                 "v_out": lambda tt: v2(VB, TT, P)[:, tt],
                 "gain": lambda c, k: v(GAINS + 7 * E, E)}
        QKC = {"tr": 4, "T": 1, "qk_ms": 4, "qk_sd": 4, "qk_ready": 4, "tile": 1}

        def constants():
            def sp_(sp, c):
                sp.dma_start(x3, A["x"].rearrange("b (t p) d -> p (b t) d", p=P)).then_inc(SEM["const_in"], 16)
                sp.dma_start(v(CON, NCONST), A["consts"]).then_inc(SEM["const_in"], 16)
                sp.dma_start(v(GAINS, 512), A["qk_gains"].partition_broadcast(P)).then_inc(SEM["const_in"], 16)
                sp.dma_start(v(RVAL, 16).bitcast(I32), A["assignment"]).then_inc(SEM["const_in"], 16)
                sp.dma_start(v(MASKA, MW // 2).bitcast(BF16), A["masks"]).then_inc(SEM["const_in"], 16)

            def any_(eng, c):
                eng.wait_ge(SEM["const_in"], 80)

            return Stage({}, sp=sp_, pe=any_, act=any_, dve=any_, pool=any_)

        def project_first():
            first, inner = qk_tile(0, cfgA, None), qk_tile(0, cfgA, cfgA)
            qb, kb = qk_tile(6, cfgQB, cfgA), qk_tile(7, cfgKB, cfgQB)

            def qk_program(who):
                def run(eng, c):
                    first[who](eng, c)
                    with eng.Fori(1, 6) as i:
                        inner[who](eng, c.inside(i, QKC))
                    qb[who](eng, c)
                    kb[who](eng, c)
                    if who == "pe":
                        for tt in range(TT):
                            eng.wait_ge(SEM["qk_ready"], up(c.of("qk_ready") + 28 + tt + 1))
                            apart(eng, c.of("qk_ready") + 28 + tt + 1)
                            tr_pe(eng, c, 28 + tt, cfgKB["ins"](tt))
                    if who == "act":
                        for tt in range(TT):
                            tr_out(eng, "act", c, 28 + tt, cfgKB["dst"](c, 7, tt), 1)
                return run

            def sp_(sp, c):
                with sp.Fori(0, 6) as i:
                    dense_sp(sp, c.inside(i, QKC), 0, lambda h: rows(w_in, 8, h, i * 512, 512))
                dense_sp(sp, c, 6, lambda h: rows(w_in, 8, h, 4608, 512))
                dense_sp(sp, c, 7, lambda h: rows(w_in, 8, h, 5120, 256))
            heads = Stage({k: 8 * n for k, n in QKC.items()}, sp=sp_, pe=qk_program("pe"), act=qk_program("act"),
                  dve=qk_program("dve"))

            def v_sp(sp, c):
                with sp.Fori(0, 3) as i:
                    dense_sp(sp, c.inside(i, {"T": 1}), 0, lambda h: rows(w_in, 8, h, i * 512 + 3072, 512))

            def v_pe(pe, c):
                with pe.Fori(0, 3) as i:
                    dense_pe(pe, c.inside(i, {"T": 1}), 0, lambda kk, tt: hT[:, kk, tt * P:(tt + 1) * P], 8, 512)

            def v_act(act, c):
                with act.Fori(0, 3) as i:
                    ci = c.inside(i, {"T": 1})
                    for tt in range(TT):
                        act.wait_ge(SEM["mm"], up(unit(ci, 0, tt)))
                        apart(act, unit(ci, 0, tt))
                        AC.activation(dyn(VA + tt * 1536 + i * 512, 512), PS[:, tt], ACT.Copy).then_inc(SEM["ev"], 1)
            return heads, Stage({"T": 3}, sp=v_sp, pe=v_pe, act=v_act)

        def attention(a):
            Gn, npairs, wide = a["groups"], a["pairs"], a.get("wide")
            KC = {"u": 8, "g": 8 * Gn, "staged": 2, "bias": 1 if a.get("sp") else 0}

            def prob(x):
                return (SC, SC + 1536, W, W + 2048)[x % 4] if wide else SC + 512 * (x % 4)

            def negmax(x):
                return v(SM + 128 + x % 4, 1)

            def rowsum(x):
                return v(SM + 132 + x % 4, 1)

            def pairs(eng, c0, first, body):
                first(c0)
                with eng.Fori(0, npairs - 1) as p:
                    body(c0.inside(p, KC), p, 10)
                c = At(c0)
                c.step(KC, npairs - 1)
                body(c, npairs - 1, 8)

            def place(p, x):
                return p + x // 8, x % 8 // TT, x % TT

            def pe_(pe, c0):
                def QK(c, p, x):
                    pp, s, i = place(p, x)
                    if i == 0:
                        pe.wait_ge(SEM["staged"], up(c.of("staged") + x // 4 + 1))
                        apart(pe, c.of("staged"))
                    pe.wait_ge(SEM["sm"], up(c.of("u") + x))
                    apart(pe, c.of("u"))
                    for lhsT, rhs, o, n in a["scores"](pp, s, i):
                        last = PE.matmul(PS[:, o // 512, o % 512:o % 512 + n], lhsT, rhs, start=True, stop=True)
                    last.then_inc(SEM["qk"], 1)

                def body(c, p, end):
                    u, g = c.of("u"), c.of("g")
                    for x in range(8):
                        _, s, i = place(p, x)
                        nt = a["W"](i) // P
                        pe.wait_ge(SEM["p_rdy"], up(u + x + 1))
                        apart(pe, u)
                        for gi in range(Gn):
                            gg = x * Gn + gi
                            pe.wait_ge(SEM["pt_free"], up(g + gg - 1))
                            apart(pe, g)
                            for q in range(gi * 4, min(nt, gi * 4 + 4)):
                                last = PE.transpose(PS[:, 3 + gg % 2, (q % 4) * P:(q % 4 + 1) * P],
                                                    v(prob(x) + q * P, P), ident)
                            last.then_inc(SEM["pt_rdy"], 1)
                        if x + 2 < end:
                            QK(c, p, x + 2)
                        pe.wait_ge(SEM["o_done"], up(u + x - 1))
                        apart(pe, u)
                        vs = a["values"](p, s, i)
                        for q in range(nt):
                            if q % 4 == 0:
                                pe.wait_ge(SEM["pt_free"], up(g + x * Gn + q // 4 + 1))
                                apart(pe, g)
                            last = PE.matmul(PS[:, 5 + x % 2, 0:E], v(PTS + q * P, P), vs[q],
                                             start=(q == 0), stop=(q == nt - 1))
                        last.then_inc(SEM["pv"], 1)

                def first(c):
                    QK(c, 0, 0)
                    QK(c, 0, 1)
                pairs(pe, c0, first, body)

            def act_(act, c0):
                def exp(c, p, x):
                    w = a["W"](x % TT)
                    act.wait_ge(SEM["sm"], up(c.of("u") + x + 1))
                    apart(act, c.of("u"))
                    sc = v(prob(x), w)
                    AC.activation(sc, sc, ACT.Exp, bias=negmax(x), scale=a["scale"],
                                  accum_out=rowsum(x)).then_inc(SEM["p_rdy"], 1)

                def body(c, p, end):
                    u, g = c.of("u"), c.of("g")
                    for x in range(8):
                        w = a["W"](x % TT)
                        for gi in range(Gn):
                            gg = x * Gn + gi
                            n = min(w - gi * 512, 512)
                            act.wait_ge(SEM["pt_rdy"], up(g + gg + 1))
                            apart(act, g)
                            if gi == 0:
                                act.wait_ge(SEM["pv"], up(u + x))
                                apart(act, u)
                            AC.activation(v(PTS + gi * 512, n), PS[:, 3 + gg % 2, 0:n], ACT.Copy).then_inc(
                                SEM["pt_free"], 1)
                        if x + 2 < end:
                            exp(c, p, x + 1)
                        elif x + 1 < end:
                            exp(c, p, x + 1)

                pairs(act, c0, lambda c: exp(c, 0, 0), lambda c, p, end: body(c, p, end if end == 8 else 9))

            def dve_(dve, c0):
                def top(c, p, x):
                    pp, s, i = place(p, x)
                    w = a["W"](i)
                    dve.wait_ge(SEM["qk"], up(c.of("u") + x + 1))
                    apart(dve, c.of("u"))
                    dve.wait_ge(SEM["pt_rdy"], up(c.of("g") + Gn * (x - 3)))
                    apart(dve, c.of("g"))
                    if i == 0 and a.get("sp"):
                        dve.wait_ge(SEM["staged"], up(c.of("staged") + x // 4 + 1))
                        apart(dve, c.of("staged"))
                    m = v(SM + 136 + x % 4, 1)
                    sc = PS[:, 0:3].rearrange("p a b -> p (a b)")[:, 0:w]
                    V.tensor_tensor_reduce(out=v(prob(x), w), in0=sc, in1=a["mask"](s, i), scale=1.0,
                                           scalar=-3e38, op0=ALU.add, op1=ALU.max, accum_out=m)
                    V.drain()
                    V.tensor_scalar(negmax(x), m, -a["scale"], None, ALU.mult).then_inc(SEM["sm"], 1)

                def body(c, p, end):
                    for x in range(8):
                        if x + 2 < end:
                            top(c, p, x + 2)
                        _, s, i = place(p, x)
                        dve.wait_ge(SEM["pv"], up(c.of("u") + x + 1))
                        apart(dve, c.of("u"))
                        r = v(SM + 140 + x % 2, 1)
                        V.reciprocal(r, rowsum(x))
                        V.drain()
                        a["finish"](p, s, i, PS[:, 5 + x % 2, 0:E], r).then_inc(SEM["o_done"], 1)

                def first(c):
                    top(c, 0, 0)
                    top(c, 0, 1)
                pairs(dve, c0, first, body)

            def pool_(pool, c0):
                def bring(c, p, s):
                    G.drain()
                    a["stage"](pool, c, p, s).then_inc(SEM["staged"], 1)

                bring(c0, 0, 0)
                bring(c0, 0, 1)
                with pool.Fori(0, npairs - 1) as p:
                    c = c0.inside(p, KC)
                    for s in range(2):
                        pool.wait_ge(SEM["sm"], up(c.of("u") + 4 * (s + 1)))
                        apart(pool, c.of("u"))
                        bring(c.inside(1, KC), p + 1, s)

            def sp_(sp, c0):
                if a.get("sp"):
                    sp_after(sp, c0)
                    a["sp"](sp, c0, 0, 0)
                    a["sp"](sp, c0, 0, 1)
                    with sp.Fori(0, npairs - 1) as p:
                        c = c0.inside(p, KC)
                        for s in range(2):
                            sp.wait_ge(SEM["staged"], up(c.of("staged") + s + 1))
                            apart(sp, c.of("staged"))
                            a["sp"](sp, c, p + 1, s)

            return Stage({k: n * npairs for k, n in KC.items()}, pe=pe_, act=act_, dve=dve_, pool=pool_, sp=sp_)

        def qst(s, g, n, p=E):
            return v(QST + 512 * g, n, p, E * s)

        def kst(s, g, n):
            return v(KST + 512 * g, n, E, E * s)

        def attention_first():
            def stage_(pool, c, p, s):
                for g in range(3):
                    G.tensor_copy(qst(s, g, S), dyn(QKT + (4 * g) * 512 + p * 512, S, E, E * s))
                    last = G.tensor_copy(kst(s, g, S), dyn(QKT + (12 + 4 * g) * 512 + p * 512, S, E, E * s))
                return last

            def scores(p, s, i):
                lo, hi = near(i)
                r = []
                for g, o, c0, n in ((2, 0, 0, S), (1, S, 0, S), (0, 2 * S, lo * P, (hi - lo) * P)):
                    r.append((v(QST + 512 * g + i * P, P, E, E * s),
                              v(KST + 512 * g + c0, n, E, E * s), o, n))
                return r

            moff = [sum(width_a(j) for j in range(i)) for i in range(TT)]
            maskb = v(MASKA, MW // 2).bitcast(BF16)

            def values(p, s, i):
                lo, hi = near(i)
                return [dyn(VA + kt * 1536 + g * 512 + s * E + p * P, E)
                        for g, ks in ((2, range(TT)), (1, range(TT)), (0, range(lo, hi))) for kt in ks]

            def finish(p, s, i, ps, r):
                return V.tensor_scalar(dyn(OA + i * 512 + s * E + p * P, E), ps, r, None, ALU.mult)

            dilated = attention({"groups": 3, "wide": True, "pairs": 4, "scale": ATT_SCALE, "W": width_a, "stage": stage_,
                       "scores": scores, "values": values, "finish": finish,
                       "mask": lambda s, i: maskb[:, moff[i]:moff[i] + width_a(i)]})

            grouped = attention({"groups": 1, "pairs": 4, "scale": ATT_SCALE, "W": lambda i: S,
                       "stage": lambda pool, c, p, s: G.tensor_copy(qst(s, 0, S), dyn(QBT + p * 512, S, E, E * s)),
                       "scores": lambda p, s, i: [(v(QST + i * P, P, E, E * s), v(KBT, S, E, E * s), 0, S)],
                       "values": lambda p, s, i: [v(VB + kt * P + s * E, E) for kt in range(TT)],
                       "finish": lambda p, s, i, ps, r: V.tensor_scalar(
                           dyn(OB + i * 512 + s * 256 + p * E, E), ps, r, None, ALU.mult),
                       "mask": lambda s, i: v(CO["zeros"], S)})
            return dilated, grouped

        def transpose_stage(items):
            def units():
                k = 0
                for src, dst, F in items:
                    for tt in range(TT):
                        for q in range(F // 4):
                            yield k, tt, q, src, dst
                            k += 1
            total = sum(F for _, _, F in items)

            def pe_(pe, c):
                for k, tt, q, src, dst in units():
                    tr_pe(pe, c, k, [src[:, tt, (4 * q + a) * P:(4 * q + a + 1) * P] for a in range(4)])

            def dve_(dve, c):
                for k, tt, q, src, dst in units():
                    if k % 2 == 1:
                        dve.wait_ge(SEM["tr_free"], up(c.of("tr") + k))
                        apart(dve, c.of("tr") + k)
                        tr_out(dve, "dve", c, k, dst[:, 4 * q:4 * q + 4, tt * P:(tt + 1) * P], 4)

            def act2(act, c):
                for k, tt, q, src, dst in units():
                    if k % 2 == 0:
                        act.wait_ge(SEM["tr_free"], up(c.of("tr") + k))
                        apart(act, c.of("tr") + k)
                        tr_out(act, "act", c, k, dst[:, 4 * q:4 * q + 4, tt * P:(tt + 1) * P], 4)
            return Stage({"tr": total}, pe=pe_, act=act2, dve=dve_)

        def merge_stage(B, nbr, yT, w_branch, w_gate, gate_bias, gb_at):
            merged = v2(B + 4096 + (2048 if nbr == 3 else 0), TT, D)
            base = B + 4096 + (2048 if nbr == 3 else 0)
            PJ = base + 8192
            GS = PJ + 2048
            KC = {"T": 2 * nbr, "sig": 4 * nbr}

            def sp_(sp, c0):
                sp_after(sp, c0)
                sp.dma_start(v(gb_at, nbr * D), gate_bias(c0).partition_broadcast(P)).then_inc(SEM["gb_in"], 16)
                with sp.Fori(0, 2) as n:
                    c = c0.inside(n, KC)
                    for b in range(nbr):
                        dense_sp(sp, c, 2 * b, lambda h: rows(w_branch(c0, b), 4, h, n * 512, 512))
                        dense_sp(sp, c, 2 * b + 1, lambda h: rows(w_gate[0](c0), 8, h, n * 512 + w_gate[1] + b * D, 512))

            def pe_(pe, c0):
                with pe.Fori(0, 2) as n:
                    c = c0.inside(n, KC)
                    for b in range(nbr):
                        dense_pe(pe, c, 2 * b, lambda kk, tt: yT[b][:, kk, tt * P:(tt + 1) * P], 4, 512)
                        dense_pe(pe, c, 2 * b + 1, lambda kk, tt: hT[:, kk, tt * P:(tt + 1) * P], 8, 512)

            def act_(act, c0):
                with act.Fori(0, 2) as n:
                    c = c0.inside(n, KC)
                    for b in range(nbr):
                        for tt in range(TT):
                            act.wait_ge(SEM["mm"], up(unit(c, 2 * b, tt)))
                            apart(act, unit(c, 2 * b, tt))
                            act.wait_ge(SEM["applied"], up(c.of("sig") + (4 * b + tt - 3 if b else 0)))
                            apart(act, c.of("sig") + (4 * b + tt - 3 if b else 0))
                            AC.activation(v(PJ + 512 * tt, 512), PS[:, tt], ACT.Copy).then_inc(SEM["ev"], 1)
                        for tt in range(TT):
                            act.wait_ge(SEM["sig_in"], up(c.of("sig") + 4 * b + tt + 1))
                            apart(act, c.of("sig") + 4 * b + tt + 1)
                            g = v(GS + 512 * tt, 512)
                            AC.activation(g, g, ACT.Sigmoid).then_inc(SEM["sig_out"], 1)

            def dve_(dve, c0):
                V.memset(v(base, 4096), 0.0)
                V.drain()
                dve.wait_ge(SEM["gb_in"], 16 * c0.of("gb") + 16)
                apart(dve, 16 * c0.of("gb") + 16)
                with dve.Fori(0, 2) as n:
                    c = c0.inside(n, KC)
                    for b in range(nbr):
                        def logits(tt):
                            dve.wait_ge(SEM["mm"], up(unit(c, 2 * b + 1, tt)))
                            apart(dve, unit(c, 2 * b + 1, tt))
                            V.tensor_tensor(v(GS + 512 * tt, 512), PS[:, tt], dyn(gb_at + b * D + n * 512, 512),
                                            ALU.add).then_inc(SEM["ev"], 1)
                            V.drain().then_inc(SEM["sig_in"], 1)

                        def apply(tt):
                            dve.wait_ge(SEM["sig_out"], up(c.of("sig") + 4 * b + tt + 1))
                            apart(dve, c.of("sig") + 4 * b + tt + 1)
                            dve.wait_ge(SEM["ev"], up(unit(c, 2 * b, tt)))
                            apart(dve, unit(c, 2 * b, tt))
                            g = v(GS + 512 * tt, 512)
                            V.tensor_tensor(g, g, v(PJ + 512 * tt, 512), ALU.mult)
                            V.drain()
                            m = dyn(base + tt * D + n * 512, 512)
                            V.tensor_tensor(m, m, g, ALU.add).then_inc(SEM["applied"], 1)
                        for tt in range(TT):
                            logits(tt)
                            if tt:
                                apply(tt - 1)
                        apply(TT - 1)
                        V.drain()
            merge = Stage({"T": 4 * nbr, "sig": 8 * nbr, "gb": 1}, sp=sp_, pe=pe_, act=act_, dve=dve_)
            turned = v2(base + 4096, 8, S)
            return merge, transpose_stage([(merged, turned, 8)]), turned

        def out_stage(mT, w_out, dst):
            def sp_(sp, c0):
                with sp.Fori(0, 2) as n:
                    dense_sp(sp, c0.inside(n, {"T": 1}), 0, lambda h: rows(w_out(c0), 8, h, n * 512, 512))

            def pe_(pe, c0):
                with pe.Fori(0, 2) as n:
                    dense_pe(pe, c0.inside(n, {"T": 1}), 0, lambda kk, tt: mT[:, kk, tt * P:(tt + 1) * P], 8, 512)

            def dve_(dve, c0):
                with dve.Fori(0, 2) as n:
                    c = c0.inside(n, {"T": 1})
                    for tt in range(TT):
                        dve.wait_ge(SEM["mm"], up(unit(c, 0, tt)))
                        apart(dve, unit(c, 0, tt))
                        if dst is None:
                            xs = dyn(X + tt * D + n * 512, 512)
                            V.tensor_tensor(xs, xs, PS[:, tt], ALU.add).then_inc(SEM["ev"], 1)
                        else:
                            V.tensor_copy(dyn(dst + tt * D + n * 512, 512), PS[:, tt]).then_inc(SEM["ev"], 1)
            return Stage({"T": 2}, sp=sp_, pe=pe_, dve=dve_)

        R = SC
        GATES, GT, BT = R + 2560, R + 2624, R + 3200
        WR = BIG + 8192
        TAB = QST
        BE, BOFF, NBLK = SM + 64, SM + 128, SM + 192

        def router_stage():
            lg, mx, ix, e4, idxf = (v2(R, TT, NE), v2(R + 128, TT, 8), v2(R + 160, TT, 8),
                                    v2(R + 192, TT, 4), v2(R + 208, TT, 4))
            oh = v2(R + 256, 16, NE)
            M = v2(R + 768, TT, NE)
            tmp = v2(R + 896, 16, NE)
            posd = v2(R + 1408, TT, NE)
            Gm = v2(R + 1536, TT, NE)
            addrf = v(R + 1664, 16)
            addr = v(R + 1696, 16).bitcast(I32)
            brow = v(R + 1728, NE)
            gates = v2(GATES, TT, 4)
            sent = v(BIG + 12288, (NE + 1) * NPOS // P).bitcast(I32)
            tot = v(R + 1792, 16)

            def sp_(sp, c):
                sp.dma_start(v2(WR, 8, NE), A["w_router"].rearrange("(k p) e -> p k e", p=P)).then_inc(SEM["slot_in"], 16)
                sp.dma_start(brow, A["b_router"].partition_broadcast(P)).then_inc(SEM["slot_in"], 16)
                sp.dma_start(sent, A["nobody"]).then_inc(SEM["slot_in"], 16)
                sp.dma_start(v(BT, 512), A["b_gate_up_T"]).then_inc(SEM["slot_in"], 16)
                sp.wait_ge(SEM["slot_in"], 64)
                sp.dma_start(LIST.rearrange("(p n) o -> p (n o)", p=P), sent).then_inc(SEM["list_in"], 16)

            def pe_(pe, c):
                pe.wait_ge(SEM["slot_in"], 64)
                for tt in range(TT):
                    for k in range(8):
                        last = PE.matmul(PS[:, 0, tt * NE:(tt + 1) * NE], hT[:, k, tt * P:(tt + 1) * P],
                                         v2(WR, 8, NE)[:, k], start=(k == 0), stop=(k == 7))
                last.then_inc(SEM["logit_mm"], 1)
                pe.wait_ge(SEM["sel_rdy"], up(1))
                for tt in range(TT):
                    for q in range(tt + 1):
                        PE.matmul(PS[:, 1, tt * NE:(tt + 1) * NE], v(CO["ones"] if q < tt else CO["before"], P),
                                  M[:, q], start=(q == 0), stop=(q == tt))
                for q in range(TT):
                    last = PE.matmul(PS[:, 2, 0:NE], v(CO["ones"], P), M[:, q], start=(q == 0), stop=(q == TT - 1))
                last.then_inc(SEM["pos_mm"], 1)
                pe.wait_ge(SEM["gmat_rdy"], up(1))
                for tt in range(TT):
                    last = PE.transpose(PS[0:NE, 3, tt * P:(tt + 1) * P], Gm[:, tt], ident)
                last.then_inc(SEM["logit_mm"], 1)

            def act_(act, c):
                act.wait_ge(SEM["top_rdy"], up(1))
                AC.activation(e4, e4, ACT.Exp).then_inc(SEM["top_exp"], 1)
                act.wait_ge(SEM["logit_mm"], up(2))
                AC.activation(v(GT, S, NE), PS[0:NE, 3], ACT.Copy)

            def dve_(dve, c):
                dve.wait_ge(SEM["slot_in"], 64)
                dve.wait_ge(SEM["logit_mm"], up(1))
                V.tensor_tensor(lg, PS[:, 0, 0:TT * NE].rearrange("p (t e) -> p t e", t=TT),
                                brow.unsqueeze(1).to_broadcast([P, TT, NE]), ALU.add)
                V.drain()
                for tt in range(TT):
                    V.max(mx[:, tt], lg[:, tt])
                V.drain()
                for tt in range(TT):
                    V.max_index(ix[:, tt].bitcast(U32), mx[:, tt], lg[:, tt])
                V.tensor_tensor(e4, mx[:, :, 0:4], mx[:, :, 0:1].to_broadcast([P, TT, 4]), ALU.subtract)
                V.drain().then_inc(SEM["top_rdy"], 1)
                V.tensor_copy(idxf, ix[:, :, 0:4].bitcast(U32))
                V.drain()
                V.tensor_tensor(oh, v(CO["iota_e"], NE).unsqueeze(1).to_broadcast([P, 16, NE]),
                                v(R + 208, 16).unsqueeze(2).to_broadcast([P, 16, NE]), ALU.is_equal)
                V.drain()
                oh4 = v3(R + 256, TT, 4, NE)
                V.tensor_reduce(M, oh4.rearrange("p t k e -> p t e k"), AX.X, ALU.add)
                V.drain().then_inc(SEM["sel_rdy"], 1)
                dve.wait_ge(SEM["top_exp"], up(1))
                V.tensor_reduce(v(R + 1792, 4), e4, AX.X, ALU.add)
                V.drain()
                V.reciprocal(v(R + 1792, 4), v(R + 1792, 4))
                V.drain()
                V.tensor_tensor(gates, e4, v(R + 1792, 4).unsqueeze(2).to_broadcast([P, TT, 4]), ALU.mult)
                V.drain()
                V.tensor_tensor(tmp, oh, v(GATES, 16).unsqueeze(2).to_broadcast([P, 16, NE]), ALU.mult)
                V.drain()
                V.tensor_reduce(Gm, v3(R + 896, TT, 4, NE).rearrange("p t k e -> p t e k"), AX.X, ALU.add)
                V.drain().then_inc(SEM["gmat_rdy"], 1)
                dve.wait_ge(SEM["pos_mm"], up(1))
                V.tensor_tensor(posd, PS[:, 1, 0:TT * NE].rearrange("p (t e) -> p t e", t=TT),
                                v(CO["iota_list"], NE).unsqueeze(1).to_broadcast([P, TT, NE]), ALU.add)
                V.drain()
                for tt in range(TT):
                    V.tensor_tensor(tmp[:, 4 * tt:4 * tt + 4], oh[:, 4 * tt:4 * tt + 4],
                                    posd[:, tt].unsqueeze(1).to_broadcast([P, 4, NE]), ALU.mult)
                V.drain()
                V.tensor_reduce(addrf, tmp, AX.X, ALU.add)
                V.drain()
                V.tensor_copy(addr, addrf)
                V.drain().then_inc(SEM["addr_rdy"], 1)
                J = MAXBLK + 1
                cnt, nb, cum = v(TAB, NE, 1), v(TAB + 32, NE, 1), v(TAB + 64, NE, 1)
                t1 = v(TAB + 96, 4 * NE, 1).rearrange("p (e b) -> p e b", e=NE)
                big = v(PTS, J * 0 + 1536, 1)
                V.tensor_copy(cnt, PS[0:1, 2, 0:NE])
                V.drain()
                V.tensor_tensor(t1, cnt.unsqueeze(2).to_broadcast([1, NE, 4]),
                                v(CO["steps"], 4, 1).unsqueeze(1).to_broadcast([1, NE, 4]), ALU.is_gt)
                V.drain()
                V.tensor_reduce(nb, t1, AX.X, ALU.add)
                V.drain()
                V.tensor_tensor_scan(cum, v(CO["ones"], NE, 1), nb, 0.0, ALU.mult, ALU.add)
                V.drain()
                cmp_ = AR[0:1, HT:HT + J * NE].rearrange("p (j e) -> p j e", j=J)
                cm2 = AR[0:1, HT + 2048:HT + 2048 + J * NE].rearrange("p (j e) -> p j e", j=J)
                V.tensor_tensor(cmp_, cum.unsqueeze(1).to_broadcast([1, J, NE]),
                                v(CO["iota_j"], J, 1).unsqueeze(2).to_broadcast([1, J, NE]), ALU.is_le)
                V.drain()
                V.tensor_tensor(cm2, cmp_, nb.unsqueeze(1).to_broadcast([1, J, NE]), ALU.mult)
                bef, stf, of = v(TAB + 256, J, 1), v(TAB + 320, J, 1), v(TAB + 384, J, 1)
                V.tensor_reduce(bef, cmp_, AX.X, ALU.add)
                V.drain()
                V.tensor_reduce(stf, cm2, AX.X, ALU.add)
                V.drain()
                V.tensor_tensor(stf, v(CO["iota_j"], J, 1), stf, ALU.subtract)
                V.drain()
                V.tensor_scalar(stf, stf, float(P), None, ALU.mult)
                V.drain()
                V.scalar_tensor_tensor(of, bef, float(NPOS), stf, ALU.mult, ALU.add)
                V.tensor_scalar(bef, bef, float(NE - 1), None, ALU.min)
                V.drain()
                V.tensor_copy(v(BE, J, 1).bitcast(I32), bef)
                V.tensor_copy(v(BOFF, J, 1).bitcast(I32), of)
                V.tensor_copy(v(NBLK, 1, 1).bitcast(I32), cum[:, NE - 1:NE])
                V.drain().then_inc(SEM["table_rdy"], 1)

            def pool_(pool, c):
                pool.wait_ge(SEM["addr_rdy"], up(1))
                pool.wait_ge(SEM["list_in"], 16)
                for a_ in range(16):
                    G.indirect_dma_start(out=LIST, out_offset=bass.IndirectOffsetOnAxis(ap=addr.bitcast(U32)[:, a_:a_ + 1], axis=0),
                                         in_=v(RVAL, 16).bitcast(I32)[:, a_:a_ + 1], in_offset=None).then_inc(SEM["listed"], 16)
                pool.wait_ge(SEM["listed"], 16 * 16)
            return Stage({}, sp=sp_, pe=pe_, act=act_, dve=dve_, pool=pool_)

        XG, XT, AT_, Y_, GS_, US_, SG_ = HT, HT + 1024, HT + 2048, W, W + 1024, W + 1536, W + 2048
        IDXL, RSC, TOK, BCUR = W + 2560, W + 2561, W + 2562, W + 2564
        ch = [v2(BIG + 4096 * q, 8, 512) for q in range(4)] + [v2(BIG + 4096 * q, 4, D) for q in (4, 5)]

        def expert_stage():
            xg, y = v(XG, D), v(Y_, D)
            xT = v2(XT, 8, P)
            aT = v2(AT_, 8, P)
            idxl, rsc, tok = (v(o, 1).bitcast(I32) for o in (IDXL, RSC, TOK))
            J = MAXBLK + 1

            def nblocks(eng):
                return eng.value_load(v(NBLK, 1, 1).bitcast(I32), min_val=1, max_val=MAXBLK)

            def entry(eng, at, j, hi):
                return eng.value_load(AR[0:1, bass.ds(j + at, 1)].bitcast(I32), min_val=0, max_val=hi)

            def sp_(sp, c):
                sp.wait_ge(SEM["table_rdy"], up(1))
                sp.wait_ge(SEM["listed"], 16 * 16)
                sp_after(sp, c)
                nb = nblocks(sp)
                o0 = entry(sp, BOFF, 0, NE * NPOS)
                sp.dma_start(idxl, LIST[bass.ds(o0, P), :]).then_inc(SEM["rows_in"], 16)
                with sp.Fori(0, nb) as j:
                    e = entry(sp, BE, j, NE - 1)
                    gu = A["w_gate_up"][bass.ds(e, 1)].rearrange("o (k p) f -> p (o k) f", p=P)
                    dn = A["w_down"][bass.ds(e, 1)].rearrange("o (f p) d -> p (o f) d", p=P)
                    srcs = [gu[:, :, 0:512], gu[:, :, 1024:1536], gu[:, :, 512:1024], gu[:, :, 1536:2048],
                            dn[:, 0:4], dn[:, 4:8]]
                    o1 = entry(sp, BOFF, j + 1, NE * NPOS)
                    for q in range(6):
                        sp.wait_ge(SEM["ch_free"], up(6 * j + q + 1))
                        apart(sp, 6 * j + q + 1)
                        sp.dma_start(ch[q], srcs[q]).then_inc(SEM[f"ch{q}"], 16)
                        if q == 2:
                            sp.wait_ge(SEM["rsc_rdy"], up(j + 1))
                            apart(sp, j + 1)
                            sp.dma_start(idxl, LIST[bass.ds(o1, P), :]).then_inc(SEM["rows_in"], 16)

            def pe_(pe, c):
                pe.wait_ge(SEM["table_rdy"], up(1))
                nb = nblocks(pe)
                for _ in range(6):
                    PE.nop().then_inc(SEM["ch_free"], 1)

                def gather_T(n):
                    pe.wait_ge(SEM["gathered"], 16 * n)
                    apart(pe, 16 * n)
                    for q in range(8):
                        last = PE.transpose(PS[:, 4 + q // 4, (q % 4) * P:(q % 4 + 1) * P], xg[:, q * P:(q + 1) * P], ident)
                    last.then_inc(SEM["xt"], 1)
                gather_T(1)
                with pe.Fori(0, nb) as j:
                    pe.wait_ge(SEM["xt_free"], up(j + 1))
                    apart(pe, j + 1)
                    for q in range(4):
                        pe.wait_ge(SEM[f"ch{q}"], 16 * j + 16)
                        apart(pe, 16 * j + 16)
                        for f in range(4):
                            for k in range(8):
                                last = PE.matmul(PS[:, q, f * P:(f + 1) * P], ch[q][:, k, f * P:(f + 1) * P],
                                                 xT[:, k], start=(k == 0), stop=(k == 7))
                        last.then_inc(SEM["ch_free"], 1)
                    gather_T(j + 2)
                    pe.wait_ge(SEM["y_rdy"], up(j))
                    apart(pe, j)
                    for f in range(8):
                        if f % 4 == 0:
                            pe.wait_ge(SEM[f"ch{4 + f // 4}"], 16 * j + 16)
                            apart(pe, 16 * j + 16)
                            pe.wait_ge(SEM["act_rdy"], up(2 * j + 1 + f // 4))
                            apart(pe, 2 * j + 1 + f // 4)
                        for n in range(2):
                            last = PE.matmul(PS[:, 6 + n], aT[:, f], ch[4 + f // 4][:, f % 4, n * 512:(n + 1) * 512],
                                             start=(f == 0), stop=(f == 7))
                        if f % 4 == 3:
                            last.then_inc(SEM["ch_free"], 1)

            def act_(act, c):
                act.wait_ge(SEM["table_rdy"], up(1))
                nb = nblocks(act)

                def copy_T(n):
                    act.wait_ge(SEM["xt"], up(n))
                    apart(act, n)
                    AC.activation(v(XT, D), PS[:, 4:6].rearrange("p a b -> p (a b)"), ACT.Copy).then_inc(SEM["xt_free"], 1)
                copy_T(1)
                with act.Fori(0, nb) as j:
                    for h in range(2):
                        act.wait_ge(SEM["act_g"], up(2 * j + h + 1))
                        apart(act, 2 * j + h + 1)
                        AC.activation(v(SG_, 512), v(GS_, 512), ACT.Sigmoid, scale=ALPHA).then_inc(SEM["sig_g"], 1)
                    copy_T(j + 2)
                    act.wait_ge(SEM["ch_free"], up(6 * j + 12))
                    apart(act, 6 * j + 12)
                    act.wait_ge(SEM["rows_out"], up(j))
                    apart(act, j)
                    AC.activation(y, PS[:, 6:8].rearrange("p a b -> p (a b)"), ACT.Copy).then_inc(SEM["y_rdy"], 1)

            def dve_(dve, c):
                nb = nblocks(dve)
                dve.wait_ge(SEM["rows_in"], 16)
                V.tensor_scalar(tok, idxl, 2, None, ALU.logical_shift_right).then_inc(SEM["tok_rdy"], 1)
                with dve.Fori(0, nb) as j:
                    e = entry(dve, BE, j, NE - 1)
                    dve.wait_ge(SEM["rows_out"], up(j))
                    apart(dve, j)
                    V.tensor_copy(rsc, idxl)
                    V.tensor_copy(v(BCUR, 16), dyn(BT + e * 16, 16))
                    V.drain().then_inc(SEM["rsc_rdy"], 1)
                    dve.wait_ge(SEM["rows_in"], 16 * j + 32)
                    apart(dve, 16 * j + 32)
                    dve.wait_ge(SEM["gathered"], 16 * j + 16)
                    apart(dve, 16 * j + 16)
                    V.tensor_scalar(tok, idxl, 2, None, ALU.logical_shift_right).then_inc(SEM["tok_rdy"], 1)
                    for h in range(2):
                        g, u, s_ = v2(GS_, 4, P), v2(US_, 4, P), v2(SG_, 4, P)

                        def bias(o):
                            return v(BCUR + o + 4 * h, 4).unsqueeze(2).to_broadcast([P, 4, P])
                        dve.wait_ge(SEM["ch_free"], up(6 * j + 6 + 2 * h + 1))
                        apart(dve, 6 * j + 6 + 2 * h + 1)
                        V.tensor_tensor(g, PS[:, 2 * h].rearrange("p (f t) -> p f t", f=4), bias(0), ALU.add)
                        V.drain()
                        V.tensor_scalar(g, g, LIMIT, None, ALU.min).then_inc(SEM["act_g"], 1)
                        dve.wait_ge(SEM["ch_free"], up(6 * j + 6 + 2 * h + 2))
                        apart(dve, 6 * j + 6 + 2 * h + 2)
                        V.tensor_tensor(u, PS[:, 2 * h + 1].rearrange("p (f t) -> p f t", f=4), bias(8), ALU.add)
                        V.drain()
                        V.tensor_scalar(u, u, LIMIT, -LIMIT, ALU.min, ALU.max)
                        V.drain()
                        V.scalar_tensor_tensor(v(US_, 512), v(US_, 512), 1.0, v(GS_, 512), ALU.add, ALU.mult)
                        V.drain()
                        dve.wait_ge(SEM["sig_g"], up(2 * j + h + 1))
                        apart(dve, 2 * j + h + 1)
                        V.tensor_tensor(v(AT_ + 512 * h, 512), v(US_, 512), v(SG_, 512), ALU.mult)
                        V.drain().then_inc(SEM["act_rdy"], 1)

            def pool_(pool, c):
                G.memset(xg, 0.0)
                G.drain()
                pool.wait_ge(SEM["table_rdy"], up(1))
                pool.wait_ge(SEM["h2_out"], 16)
                nb = nblocks(pool)

                def gather(n):
                    pool.wait_ge(SEM["tok_rdy"], up(n))
                    apart(pool, n)
                    G.indirect_dma_start(out=xg, out_offset=None, in_=H2D,
                                         in_offset=bass.IndirectOffsetOnAxis(ap=tok.bitcast(U32), axis=0),
                                         bounds_check=S - 1, oob_is_err=False).then_inc(SEM["gathered"], 16)
                gather(1)
                with pool.Fori(0, nb) as j:
                    pool.wait_ge(SEM["xt"], up(j + 1))
                    apart(pool, j + 1)
                    gather(j + 2)
                    pool.wait_ge(SEM["y_rdy"], up(j + 1))
                    apart(pool, j + 1)
                    G.indirect_dma_start(out=YD, out_offset=bass.IndirectOffsetOnAxis(ap=rsc.bitcast(U32), axis=0),
                                         in_=y, in_offset=None,
                                         bounds_check=S * TOPK - 1, oob_is_err=False).then_inc(SEM["scattered"], 16)
                    pool.wait_ge(SEM["scattered"], 16 * j + 16)
                    apart(pool, 16 * j + 16)
                    pool.sem_inc(SEM["rows_out"])
                pool.wait_ge(SEM["gathered"], nb * 16 + 16)
                apart(pool, nb * 16 + 16)
            return Stage({}, sp=sp_, pe=pe_, act=act_, dve=dve_, pool=pool_)

        def combine_stage():
            BD = W

            def sp_(sp, c):
                sp_after(sp, c)
                sp.dma_start(v(BD, D, NE), A["b_down"]).then_inc(SEM["bdown_in"], 16)
                for tt in range(TT):
                    sp.dma_start(v(BIG + 4096 * tt, 4096),
                                 YD[tt * 512:(tt + 1) * 512, :].rearrange("(p k) d -> p (k d)", k=4)).then_inc(
                                     SEM[f"comb{tt}"], 16)

            def pe_(pe, c):
                pe.wait_ge(SEM["bdown_in"], 16)
                for tt in range(TT):
                    for n in range(2):
                        last = PE.matmul(PS[:, 2 * tt + n], v(GT + tt * P, P, NE), v(BD + n * 512, 512, NE),
                                         start=True, stop=True)
                last.then_inc(SEM["fin_mm"], 1)

            def dve_(dve, c):
                dve.wait_ge(SEM["fin_mm"], up(1))
                for tt in range(TT):
                    V.tensor_tensor(x3[:, tt], x3[:, tt], PS[:, 2 * tt:2 * tt + 2].rearrange("p a b -> p (a b)"), ALU.add)
                V.drain()
                for tt in range(TT):
                    dve.wait_ge(SEM[f"comb{tt}"], 16)
                    for k in range(4):
                        V.scalar_tensor_tensor(x3[:, tt], v(BIG + 4096 * tt + D * k, D), v(GATES + 4 * tt + k, 1),
                                               x3[:, tt], ALU.mult, ALU.add)
                        V.drain()
            return Stage({}, sp=sp_, pe=pe_, dve=dve_)

        def output_stage():
            def sp_(sp, c):
                sp_after(sp, c)
                sp.dma_start(out.rearrange("b (t p) d -> p (b t) d", p=P), x3).then_inc(SEM["x_out"], 16)
                sp.wait_ge(SEM["x_out"], 16)
            return Stage({}, sp=sp_)

        YA, YB, YC = BIG, BIG + 2048, BIG + 4096

        def wl(name):
            return lambda c: A[name][bass.ds(c.of("layer"), 1)].rearrange("o a b -> (o a) b")

        w2 = wl("w_in_2")

        def dense_hT(k0, cols):
            def sp_(sp, c):
                for k, (c0, n) in enumerate(cols):
                    dense_sp(sp, c, k0 + k, lambda h: rows(w2(c), 8, h, c0, n))

            def pe_(pe, c):
                for k, (c0, n) in enumerate(cols):
                    dense_pe(pe, c, k0 + k, lambda kk, tt: hT[:, kk, tt * P:(tt + 1) * P], 8, n)
            return sp_, pe_

        def sgu_stage():
            U, Vv, Z, WS, SCR, ROW = (LB + o for o in (0, 2048, 4096, 6144, 7168, 9216))
            sp0, pe0 = dense_hT(0, [(0, 512), (512, 512), (1024, 512)])
            st = v(SM, 16)

            def sp_(sp, c):
                sp_after(sp, c)
                l = c.of("layer")
                sp.dma_start(v2(WS, 8, P), A["sgu_w_T"][bass.ds(l, 1)].rearrange("o s g t -> s (o g) t")).then_inc(SEM["ws_in"], 16)
                sp.dma_start(v(ROW, 1024), A["sgu_ln"][bass.ds(l, 1)].rearrange("o w -> (o w)").partition_broadcast(P)).then_inc(SEM["ws_in"], 16)
                sp.dma_start(v(SM + 32, 8), A["sgu_b_T"][bass.ds(l, 1)].rearrange("o t g -> t (o g)")).then_inc(SEM["ws_in"], 16)
                sp0(sp, c)

            def pe_(pe, c):
                pe0(pe, c)
                pe.wait_ge(SEM["ws_rdy"], up(2 * c.of("lay") + 2))
                apart(pe, 2 * c.of("lay") + 2)
                for g in range(8):
                    last = PE.matmul(PS[:, 4 + g // 2, (g % 2) * 256:(g % 2 + 1) * 256], v2(WS, 8, P)[:, g],
                                     v3(Vv, TT, 8, E)[:, :, g], start=True, stop=True)
                last.then_inc(SEM["sgu_mm"], 1)

            def act_(act, c):
                for tt in range(TT):
                    act.wait_ge(SEM["mm"], up(unit(c, 0, tt)))
                    apart(act, unit(c, 0, tt))
                    AC.activation(v(U + 512 * tt, 512), PS[:, tt], ACT.Copy).then_inc(SEM["ev"], 1)
                for tt in range(TT):
                    act.wait_ge(SEM["mm"], up(unit(c, 1, tt)))
                    apart(act, unit(c, 1, tt))
                    AC.activation(v(Vv + 512 * tt, 512), PS[:, tt], ACT.Copy, accum_out=st[:, tt:tt + 1]).then_inc(SEM["ev"], 1)
                act.wait_ge(SEM["sgu_in"], up(2 * c.of("lay") + 1))
                apart(act, 2 * c.of("lay") + 1)
                for tt in range(TT):
                    last = AC.activation(v(SCR + 512 * tt, 512), v(Vv + 512 * tt, 512), ACT.Square, accum_out=st[:, 4 + tt:5 + tt])
                last.then_inc(SEM["ln_sd"], 1)
                act.wait_ge(SEM["sgu_in"], up(2 * c.of("lay") + 2))
                apart(act, 2 * c.of("lay") + 2)
                AC.activation(st[:, 4:8], st[:, 4:8], ACT.Sqrt).then_inc(SEM["ln_sd"], 1)
                for tt in range(TT):
                    act.wait_ge(SEM["mm"], up(unit(c, 2, tt)))
                    apart(act, unit(c, 2, tt))
                    AC.activation(v(Z + 512 * tt, 512), PS[:, tt], ACT.Copy)
                    AC.activation(v(YA + 512 * tt, 512), PS[:, tt], ACT.Sigmoid).then_inc(SEM["ev"], 1)

            def dve_(dve, c):
                lay = c.of("lay")
                v3d = v2(Vv, TT, 512)
                dve.wait_ge(SEM["ws_in"], 48 * lay + 48)
                apart(dve, 48 * lay + 48)
                V.tensor_tensor(v2(WS, 8, P), v2(WS, 8, P), v(CO["tril_T"], P).unsqueeze(1).to_broadcast([P, 8, P]),
                                ALU.mult).then_inc(SEM["ws_rdy"], 1)
                dve.wait_ge(SEM["ev"], up(unit(c, 1, 3)))
                apart(dve, unit(c, 1, 3))
                V.tensor_scalar(st[:, 0:4], st[:, 0:4], -1.0 / 512, None, ALU.mult)
                V.drain()
                for tt in range(TT):
                    last = V.tensor_scalar(v3d[:, tt], v3d[:, tt], st[:, tt:tt + 1], None, ALU.add)
                last.then_inc(SEM["sgu_in"], 1)
                dve.wait_ge(SEM["ln_sd"], up(2 * lay + 1))
                apart(dve, 2 * lay + 1)
                V.tensor_scalar(st[:, 4:8], st[:, 4:8], 1.0 / 512, EPS, ALU.mult, ALU.add).then_inc(SEM["sgu_in"], 1)
                dve.wait_ge(SEM["ln_sd"], up(2 * lay + 2))
                apart(dve, 2 * lay + 2)
                V.reciprocal(st[:, 4:8], st[:, 4:8])
                V.drain()
                for tt in range(TT):
                    V.scalar_tensor_tensor(v3d[:, tt], v3d[:, tt], st[:, 4 + tt:5 + tt], v(ROW, 512), ALU.mult, ALU.mult)
                V.drain()
                V.tensor_tensor(v3d, v3d, v(ROW + 512, 512).unsqueeze(1).to_broadcast([P, TT, 512]), ALU.add)
                V.drain().then_inc(SEM["ws_rdy"], 1)
                dve.wait_ge(SEM["ev"], up(unit(c, 2, 3)))
                apart(dve, unit(c, 2, 3))
                V.tensor_tensor(v(YA, 2048), v(YA, 2048), v(Z, 2048), ALU.mult)
                V.drain()
                V.tensor_tensor(v(YA, 2048), v(YA, 2048), v(U, 2048), ALU.mult)
                dve.wait_ge(SEM["sgu_mm"], up(lay + 1))
                apart(dve, lay + 1)
                for q in range(4):
                    V.tensor_tensor(v(SCR + 512 * q, 512).rearrange("p (g x) -> p g x", g=2),
                                    PS[:, 4 + q].rearrange("p (g x) -> p g x", g=2),
                                    v(SM + 32 + 2 * q, 2).unsqueeze(2).to_broadcast([P, 2, 256]), ALU.add)
                V.drain()
                for tt in range(TT):
                    ya = v(YA + 512 * tt, 512).rearrange("p (g c) -> p g c", g=8)
                    V.tensor_tensor(ya, ya, v3(SCR, 8, TT, E)[:, :, tt], ALU.mult)
            return Stage({"T": 3}, sp=sp_, pe=pe_, act=act_, dve=dve_)

        QM, KV, DN, CQT, CKVT, LROW, MQT, MKT = (LB + o for o in (0, 3072, 8192, 9856, 10880, 11392, 11776, 15872))

        def latent_stages():
            sp0, pe0 = dense_hT(0, [(1536, 416), (1952, 512)])
            st = v(SM, 8)
            dn = v2(DN, TT, 416)

            def sp_(sp, c):
                sp_after(sp, c)
                sp.dma_start(v(LROW, 384), A["mla_norms"][bass.ds(c.of("layer"), 1)].rearrange("o w -> (o w)").partition_broadcast(P)).then_inc(
                    SEM["bdown_in"], 16)
                sp0(sp, c)

            def act_(act, c):
                lay = c.of("lay")
                for tt in range(TT):
                    act.wait_ge(SEM["mm"], up(unit(c, 0, tt)))
                    apart(act, unit(c, 0, tt))
                    AC.activation(v(PTS + 384 * tt, 256), PS[:, tt, 0:256], ACT.Square, accum_out=st[:, tt:tt + 1])
                    AC.activation(v(PTS + 384 * tt + 256, 128), PS[:, tt, 256:384], ACT.Square, accum_out=st[:, 4 + tt:5 + tt])
                    AC.activation(dn[:, tt], PS[:, tt, 0:416], ACT.Copy).then_inc(SEM["ev"], 1)
                act.wait_ge(SEM["lat_ms"], up(lay + 1))
                apart(act, lay + 1)
                AC.activation(st, st, ACT.Sqrt).then_inc(SEM["lat_sd"], 1)
                for tt in range(TT):
                    act.wait_ge(SEM["mm"], up(unit(c, 1, tt)))
                    apart(act, unit(c, 1, tt))
                    AC.activation(v(SC + 512 * tt, 512), PS[:, tt], ACT.Copy)
                    AC.activation(v(YB + 512 * tt, 512), PS[:, tt], ACT.Sigmoid).then_inc(SEM["ev"], 1)
                for tt in range(TT):
                    act.wait_ge(SEM["tr"], up(c.of("tr") + tt + 1))
                    apart(act, c.of("tr") + tt + 1)
                    AC.activation(v2(CQT, 2, S)[:, :, tt * P:(tt + 1) * P],
                                  PS[:, 4 + tt, 0:256].rearrange("p (a t) -> p a t", a=2), ACT.Copy)
                    AC.activation(v(CKVT + tt * P, P), PS[:, 4 + tt, 256:384], ACT.Copy).then_inc(SEM["tr_free"], 1)

            def dve_(dve, c):
                lay = c.of("lay")
                dve.wait_ge(SEM["ev"], up(unit(c, 0, 3)))
                apart(dve, unit(c, 0, 3))
                V.tensor_scalar(st[:, 0:4], st[:, 0:4], 1.0 / 256, EPS, ALU.mult, ALU.add)
                V.tensor_scalar(st[:, 4:8], st[:, 4:8], 1.0 / 128, EPS, ALU.mult, ALU.add)
                V.drain().then_inc(SEM["lat_ms"], 1)
                dve.wait_ge(SEM["lat_sd"], up(lay + 1))
                apart(dve, lay + 1)
                V.reciprocal(st, st)
                V.drain()
                dve.wait_ge(SEM["bdown_in"], 16 * lay + 32)
                apart(dve, 16 * lay + 32)
                for tt in range(TT):
                    V.scalar_tensor_tensor(dn[:, tt, 0:256], dn[:, tt, 0:256], st[:, tt:tt + 1], v(LROW, 256), ALU.mult, ALU.mult)
                    V.scalar_tensor_tensor(dn[:, tt, 256:384], dn[:, tt, 256:384], st[:, 4 + tt:5 + tt], v(LROW + 256, 128),
                                           ALU.mult, ALU.mult)
                    V.drain().then_inc(SEM["lat_rdy"], 1)
                for tt in range(TT):
                    src = dn[:, tt, 384:416].unsqueeze(1)
                    rotate(v(SM + 64 + 32 * tt, 32).unsqueeze(1), src, v(CO["ropeM_c"] + 32 * tt, 32),
                           v(CO["ropeM_s"] + 32 * tt, 32), 1, 1, 16)
                    V.drain()
                    V.tensor_copy(v3(KV, TT, 8, 160)[:, tt, :, 0:32],
                                  v(SM + 64 + 32 * tt, 32).unsqueeze(1).to_broadcast([P, 8, 32]))
                dve.wait_ge(SEM["ev"], up(unit(c, 1, 3)))
                apart(dve, unit(c, 1, 3))
                V.tensor_tensor(v(YB, 2048), v(YB, 2048), v(SC, 2048), ALU.mult)

            def pe_(pe, c):
                pe0(pe, c)
                for tt in range(TT):
                    pe.wait_ge(SEM["lat_rdy"], up(4 * c.of("lay") + tt + 1))
                    apart(pe, 4 * c.of("lay") + tt + 1)
                    tr_pe(pe, c, tt, [dn[:, tt, a * P:(a + 1) * P] for a in range(3)])
            latents = Stage({"T": 2, "tr": 4}, sp=sp_, act=act_, dve=dve_, pe=pe_)

            uq, ukv = wl("mla_w_uq_2"), wl("mla_w_ukv_2")

            def sp2(sp, c):
                for n in range(2):
                    dense_sp(sp, c, n, lambda h: rows(uq(c), 2, h, n * 384, 384))
                for n in range(2):
                    dense_sp(sp, c, 2 + n, lambda h: (Wh[h][:, 0, 0:256], ukv(c)[:, n * 512 + h * 256:n * 512 + h * 256 + 256]))

            def pe2(pe, c):
                for n in range(2):
                    dense_pe(pe, c, n, lambda kk, tt: v2(CQT, 2, S)[:, kk, tt * P:(tt + 1) * P], 2, 384)
                for n in range(2):
                    dense_pe(pe, c, 2 + n, lambda kk, tt: v(CKVT + tt * P, P), 1, 512)

            def act2(act, c):
                for n in range(2):
                    for tt in range(TT):
                        act.wait_ge(SEM["mm"], up(unit(c, n, tt)))
                        apart(act, unit(c, n, tt))
                        src = PS[:, tt, 0:384].rearrange("p (h e) -> p h e", h=4)
                        dst = v3(QM, TT, 8, 96)[:, tt, 4 * n:4 * n + 4]
                        AC.activation(dst[:, :, 0:32], src[:, :, 64:96], ACT.Copy)
                        AC.activation(dst[:, :, 32:96], src[:, :, 0:64], ACT.Copy).then_inc(SEM["ev"], 1)
                for n in range(2):
                    for tt in range(TT):
                        act.wait_ge(SEM["mm"], up(unit(c, 2 + n, tt)))
                        apart(act, unit(c, 2 + n, tt))
                        AC.activation(v3(KV, TT, 8, 160)[:, tt, 4 * n:4 * n + 4, 32:160],
                                      PS[:, tt].rearrange("p (h e) -> p h e", h=4), ACT.Copy).then_inc(SEM["ev"], 1)

            def dve2(dve, c):
                dve.wait_ge(SEM["ev"], up(unit(c, 1, 3)))
                apart(dve, unit(c, 1, 3))
                for tt in range(TT):
                    q = v3(QM, TT, 8, 96)[:, tt, :, 0:32]
                    rotate(q, q, v(CO["ropeM_c"] + 32 * tt, 32), v(CO["ropeM_s"] + 32 * tt, 32), 8, 1, 16)
                    V.drain()
            raised = Stage({"T": 4}, sp=sp2, pe=pe2, act=act2, dve=dve2)

            def heads():
                k = 0
                for src, dst in ((v3(QM, TT, 8, 96), MQT), (v3(KV, TT, 8, 160), MKT)):
                    for tt in range(TT):
                        for hq in range(2):
                            yield k, tt, hq, src, dst
                            k += 1

            def pe3(pe, c):
                for k, tt, hq, src, dst in heads():
                    tr_pe(pe, c, k, [src[:, tt, 4 * hq + a, 0:96] for a in range(4)])

            def copy3(who, par):
                def run(eng, c):
                    for k, tt, hq, src, dst in heads():
                        if k % 2 == par:
                            eng.wait_ge(SEM["tr_free"], up(c.of("tr") + k))
                            apart(eng, c.of("tr") + k)
                            tr_out(eng, who, c, k, v2(dst, 8, S, 96)[:, 4 * hq:4 * hq + 4, tt * P:(tt + 1) * P], 4, 96)
                return run
            turned = Stage({"tr": 16}, pe=pe3, act=copy3("act", 0), dve=copy3("dve", 1))

            def W_(i):
                return P * (i + 1)

            def finish(p, s, i, ps, r):
                o = dyn(YB + i * 512 + s * E + p * P, E)
                return V.scalar_tensor_tensor(o, ps, r, o, ALU.mult, ALU.mult)
            return latents, raised, turned, attention({"groups": 1, "pairs": 4, "scale": MLA_SCALE, "W": W_,
                       "stage": lambda pool, c, p, s: G.tensor_copy(v(QST + 512 * s, S, 96), dyn(MQT + s * 512 + p * 1024, S, 96)),
                       "scores": lambda p, s, i: [(v(QST + 512 * s + i * P, P, 96), dyn(MKT + s * 512 + p * 1024, W_(i), 96), 0, W_(i))],
                       "values": lambda p, s, i: [dyn(KV + kt * 1280 + s * 160 + 96 + p * 320, E) for kt in range(i + 1)],
                       "finish": finish,
                       "mask": lambda s, i: v(CO["chunk_mask"] + S - W_(i), W_(i))})

        CQK, CV, CST = LB, LB + 4096, LB + 6144

        def chunk_stages():
            c0s = 1952 + 512
            sp0, pe0 = dense_hT(0, [(c0s, 512), (c0s + 512, 512), (c0s + 1024, 512), (c0s + 1536, 512)])

            def sp_(sp, c):
                sp_after(sp, c)
                sp0(sp, c)

            def pe_(pe, c):
                def tr(k):
                    for tt in range(TT):
                        pe.wait_ge(SEM["ev"], up(unit(c, k, tt)))
                        apart(pe, unit(c, k, tt))
                        tr_pe(pe, c, 4 * k + tt, [v(CST + k * 2048 + tt * 512 + a * P, P) for a in range(4)])
                for k in range(4):
                    dense_pe(pe, c, k, lambda kk, tt: hT[:, kk, tt * P:(tt + 1) * P], 8, 512)
                    if k in (1, 2):
                        tr(k - 1)

            def act_(act, c):
                for k in range(4):
                    for tt in range(TT):
                        act.wait_ge(SEM["mm"], up(unit(c, k, tt)))
                        apart(act, unit(c, k, tt))
                        if k < 3:
                            o = CST + k * 2048 + tt * 512 if k < 2 else CV + tt * 512
                            AC.activation(v(o, 512), PS[:, tt], ACT.Copy).then_inc(SEM["ev"], 1)
                        else:
                            AC.activation(v(SC + 512 * tt, 512), PS[:, tt], ACT.Copy)
                            AC.activation(v(YC + 512 * tt, 512), PS[:, tt], ACT.Sigmoid).then_inc(SEM["ev"], 1)
                    if k in (1, 2):
                        for tt in range(TT):
                            tr_out(act, "act", c, 4 * (k - 1) + tt,
                                   v2(CQK + 2048 * (k - 1), 4, S)[:, :, tt * P:(tt + 1) * P], 4)

            def dve_(dve, c):
                dve.wait_ge(SEM["ev"], up(unit(c, 3, 3)))
                apart(dve, unit(c, 3, 3))
                V.tensor_tensor(v(YC, 2048), v(YC, 2048), v(SC, 2048), ALU.mult)
            heads = Stage({"T": 4, "tr": 8}, sp=sp_, pe=pe_, act=act_, dve=dve_)

            def W_(i):
                return P * (i + 1)

            TR, BH = SC + 2048, QST + 512

            def raw(s):
                return v(SC + 2048 + 256 * s, 256)

            def stage_(pool, c, p, s):
                pool.wait_ge(SEM[f"bias_rows{s}"], 16 * c.of("bias") + 16)
                apart(pool, 16 * c.of("bias") + 16)
                b = BH + 512 * s
                G.tensor_scalar(v(b + 256, 256), raw(s), 1.0 / ATT_SCALE, None, ALU.mult)
                G.tensor_scalar(v(b, 256), raw(s)[:, 0:1].to_broadcast([P, 256]), 1.0 / ATT_SCALE, None, ALU.mult)
                G.drain()
                G.memset(v(b + 448, 64, 64), NEG)
                G.drain()
                G.tensor_copy(kst(s, 0, S), dyn(CQK + 2048 + p * 512, S, E, E * s))
                return G.tensor_copy(qst(s, 0, S), dyn(CQK + p * 512, S, E, E * s))

            def spb(sp, c, p, s):
                src = A["rel_rows"][bass.ds(c.of("layer") * 8 + 2 * p + s, 1)].rearrange("o p w -> (o p) w")
                sp.dma_start(raw(s), src).then_inc(SEM[f"bias_rows{s}"], 16)

            def finish(p, s, i, ps, r):
                o = dyn(YC + i * 512 + s * E + p * P, E)
                return V.scalar_tensor_tensor(o, ps, r, o, ALU.mult, ALU.mult)
            return heads, attention({"groups": 1, "pairs": 4, "scale": ATT_SCALE, "W": W_, "stage": stage_, "sp": spb,
                       "scores": lambda p, s, i: [(v(QST + i * P, P, E, E * s), kst(s, 0, W_(i)), 0, W_(i))],
                       "values": lambda p, s, i: [dyn(CV + kt * 512 + s * E + p * P, E) for kt in range(i + 1)],
                       "finish": finish,
                       "mask": lambda s, i: v(BH + 512 * s + S - W_(i), W_(i))})

        def post_stage(YO):
            st = v(SM, 4)
            yo = v2(YO, TT, D)

            def sp_(sp, c):
                sp_after(sp, c)
                sp.dma_start(v(GROW, D), A["post_g_2"][bass.ds(c.of("layer"), 1)].rearrange("o w -> (o w)").partition_broadcast(P)).then_inc(
                    SEM["grow_in"], 16)

            def act_(act, c):
                for tt in range(TT):
                    last = AC.activation(v(YO + 4096 + D * tt, D), yo[:, tt], ACT.Square, accum_out=st[:, tt:tt + 1])
                last.then_inc(SEM["post_ms"], 1)
                act.wait_ge(SEM["post_ms"], up(2 * c.of("lay") + 2))
                apart(act, 2 * c.of("lay") + 2)
                AC.activation(st, st, ACT.Sqrt).then_inc(SEM["post_sd"], 1)

            def dve_(dve, c):
                dve.wait_ge(SEM["post_ms"], up(2 * c.of("lay") + 1))
                apart(dve, 2 * c.of("lay") + 1)
                V.tensor_scalar(st, st, 1.0 / D, EPS, ALU.mult, ALU.add).then_inc(SEM["post_ms"], 1)
                dve.wait_ge(SEM["post_sd"], up(c.of("lay") + 1))
                apart(dve, c.of("lay") + 1)
                V.reciprocal(st, st)
                V.drain()
                dve.wait_ge(SEM["grow_in"], 16 * c.of("grow") + 16)
                apart(dve, 16 * c.of("grow") + 16)
                for tt in range(TT):
                    V.scalar_tensor_tensor(yo[:, tt], yo[:, tt], st[:, tt:tt + 1], v(GROW, D), ALU.mult, ALU.mult)
                    V.drain()
                    V.tensor_tensor(x3[:, tt], x3[:, tt], yo[:, tt], ALU.add)
            return Stage({"grow": 1}, sp=sp_, act=act_, dve=dve_)

        load = constants()
        norm_mix = norm_stage(lambda c: A["norm_mix_g"], BIG)
        heads_1, values_1 = project_first()
        dilated, grouped = attention_first()
        OAT, OBT = v2(BIG, 4, S), v2(BIG + 2048, 4, S)
        turn_1 = transpose_stage([(v2(OA, TT, 512), OAT, 4), (v2(OB, TT, 512), OBT, 4)])
        merge_1, turn_merged_1, mT = merge_stage(
            BIG, 2, [OAT, OBT], lambda c, b: A["w_proj_a"] if b == 0 else A["w_proj_b"],
            (lambda c: w_in, 5376), lambda c: A["b_gate"], BIG + 16384)
        out_1 = out_stage(mT, lambda c: A["w_out"], None)
        norm_ffn = norm_stage(lambda c: A["norm_ffn_g"], BIG, want_h2=True)
        route = router_stage()
        experts = expert_stage()
        combine = combine_stage()

        norm_pre = norm_stage(lambda c: A["pre_g_2"][bass.ds(c.of("layer"), 1)].rearrange("o w -> (o w)"), LB)
        gating = sgu_stage()
        latents, raised, turn_latent, latent_attention = latent_stages()
        heads_2, chunk_attention = chunk_stages()
        YT = [v2(LB + 2048 * b, 4, S) for b in range(3)]
        turn_2 = transpose_stage([(v2(y_, TT, 512), YT[b], 4) for b, y_ in enumerate((YA, YB, YC))])
        merge_2, turn_merged_2, mT2 = merge_stage(
            LB, 3, YT, lambda c, b: A["w_branch_2"][bass.ds(c.of("layer"), 1)].rearrange("o n c d -> (o n) c d")[b],
            (w2, 4512), lambda c: A["gate_b_2"][bass.ds(c.of("layer"), 1)].rearrange("o w -> (o w)"), SC)
        out_2 = out_stage(mT2, wl("w_out_2"), LB)
        post = post_stage(LB)
        output = output_stage()

        per_layer = {"layer": 1, "lay": 1}
        for st in (norm_pre, gating, latents, raised, turn_latent, latent_attention, heads_2,
                   chunk_attention, turn_2, merge_2, turn_merged_2, out_2, post):
            for k, n in st.counts.items():
                per_layer[k] = per_layer.get(k, 0) + n
            per_layer["fence"] = per_layer.get("fence", 0) + 1

        block = ctx.enter_context(nc.Block())

        @block.sync
        def _(sp):
            c = At()
            load.sp(sp, c)
            norm_mix.sp(sp, c)
            heads_1.sp(sp, c)
            values_1.sp(sp, c)
            dilated.sp(sp, c)
            grouped.sp(sp, c)
            turn_1.sp(sp, c)
            merge_1.sp(sp, c)
            turn_merged_1.sp(sp, c)
            out_1.sp(sp, c)
            norm_ffn.sp(sp, c)
            route.sp(sp, c)
            experts.sp(sp, c)
            combine.sp(sp, c)
            with sp.Fori(0, 2) as layer:
                cl = c.inside(layer, per_layer)
                norm_pre.sp(sp, cl)
                gating.sp(sp, cl)
                latents.sp(sp, cl)
                raised.sp(sp, cl)
                turn_latent.sp(sp, cl)
                latent_attention.sp(sp, cl)
                heads_2.sp(sp, cl)
                chunk_attention.sp(sp, cl)
                turn_2.sp(sp, cl)
                merge_2.sp(sp, cl)
                turn_merged_2.sp(sp, cl)
                out_2.sp(sp, cl)
                post.sp(sp, cl)
            c.step(per_layer, 2)
            output.sp(sp, c)

        @block.tensor
        def _(pe):
            c = At()
            load.pe(pe, c)
            norm_mix.pe(pe, c)
            heads_1.pe(pe, c)
            values_1.pe(pe, c)
            dilated.pe(pe, c)
            grouped.pe(pe, c)
            turn_1.pe(pe, c)
            merge_1.pe(pe, c)
            turn_merged_1.pe(pe, c)
            out_1.pe(pe, c)
            norm_ffn.pe(pe, c)
            route.pe(pe, c)
            experts.pe(pe, c)
            combine.pe(pe, c)
            with pe.Fori(0, 2) as layer:
                cl = c.inside(layer, per_layer)
                norm_pre.pe(pe, cl)
                gating.pe(pe, cl)
                latents.pe(pe, cl)
                raised.pe(pe, cl)
                turn_latent.pe(pe, cl)
                latent_attention.pe(pe, cl)
                heads_2.pe(pe, cl)
                chunk_attention.pe(pe, cl)
                turn_2.pe(pe, cl)
                merge_2.pe(pe, cl)
                turn_merged_2.pe(pe, cl)
                out_2.pe(pe, cl)
                post.pe(pe, cl)
            c.step(per_layer, 2)
            output.pe(pe, c)

        @block.scalar
        def _(act):
            c = At()
            load.act(act, c)
            norm_mix.act(act, c)
            heads_1.act(act, c)
            values_1.act(act, c)
            dilated.act(act, c)
            grouped.act(act, c)
            turn_1.act(act, c)
            merge_1.act(act, c)
            turn_merged_1.act(act, c)
            out_1.act(act, c)
            norm_ffn.act(act, c)
            route.act(act, c)
            experts.act(act, c)
            combine.act(act, c)
            with act.Fori(0, 2) as layer:
                cl = c.inside(layer, per_layer)
                norm_pre.act(act, cl)
                gating.act(act, cl)
                latents.act(act, cl)
                raised.act(act, cl)
                turn_latent.act(act, cl)
                latent_attention.act(act, cl)
                heads_2.act(act, cl)
                chunk_attention.act(act, cl)
                turn_2.act(act, cl)
                merge_2.act(act, cl)
                turn_merged_2.act(act, cl)
                out_2.act(act, cl)
                post.act(act, cl)
            c.step(per_layer, 2)
            output.act(act, c)

        @block.vector
        def _(dve):
            c = At()
            load.dve(dve, c)
            norm_mix.dve(dve, c)
            heads_1.dve(dve, c)
            values_1.dve(dve, c)
            dilated.dve(dve, c)
            grouped.dve(dve, c)
            turn_1.dve(dve, c)
            merge_1.dve(dve, c)
            turn_merged_1.dve(dve, c)
            out_1.dve(dve, c)
            norm_ffn.dve(dve, c)
            route.dve(dve, c)
            experts.dve(dve, c)
            combine.dve(dve, c)
            with dve.Fori(0, 2) as layer:
                cl = c.inside(layer, per_layer)
                norm_pre.dve(dve, cl)
                gating.dve(dve, cl)
                latents.dve(dve, cl)
                raised.dve(dve, cl)
                turn_latent.dve(dve, cl)
                latent_attention.dve(dve, cl)
                heads_2.dve(dve, cl)
                chunk_attention.dve(dve, cl)
                turn_2.dve(dve, cl)
                merge_2.dve(dve, cl)
                turn_merged_2.dve(dve, cl)
                out_2.dve(dve, cl)
                post.dve(dve, cl)
            c.step(per_layer, 2)
            output.dve(dve, c)

        @block.gpsimd
        def _(pool):
            c = At()
            for n in names:
                if n not in FROM_ZERO:
                    pool.sem_inc(SEM[n], BASE)
            load.pool(pool, c)
            norm_mix.pool(pool, c)
            heads_1.pool(pool, c)
            values_1.pool(pool, c)
            dilated.pool(pool, c)
            grouped.pool(pool, c)
            turn_1.pool(pool, c)
            merge_1.pool(pool, c)
            turn_merged_1.pool(pool, c)
            out_1.pool(pool, c)
            norm_ffn.pool(pool, c)
            route.pool(pool, c)
            experts.pool(pool, c)
            combine.pool(pool, c)
            with pool.Fori(0, 2) as layer:
                cl = c.inside(layer, per_layer)
                norm_pre.pool(pool, cl)
                gating.pool(pool, cl)
                latents.pool(pool, cl)
                raised.pool(pool, cl)
                turn_latent.pool(pool, cl)
                latent_attention.pool(pool, cl)
                heads_2.pool(pool, cl)
                chunk_attention.pool(pool, cl)
                turn_2.pool(pool, cl)
                merge_2.pool(pool, cl)
                turn_merged_2.pool(pool, cl)
                out_2.pool(pool, cl)
                post.pool(pool, cl)
            c.step(per_layer, 2)
            output.pool(pool, c)



def lay_out(inputs):
    f = {k: np.ascontiguousarray(a) for k, a in inputs.items()}
    cat = np.concatenate
    m = {k: f[k] for k in ("x", "norm_mix_g", "w_in", "w_proj_a", "w_proj_b", "w_out", "norm_ffn_g", "w_router",
                           "b_router", "w_gate_up", "w_down", "b_down", "w_in_2", "pre_g_2", "post_g_2",
                           "mla_w_uq_2", "mla_w_ukv_2", "w_branch_2", "w_out_2")}
    m["b_gate"] = f["b_gate"].reshape(-1)
    m["gate_b_2"] = f["gate_b_2"].reshape(2, -1)
    m["qk_gains"] = cat([f["qn_a"].reshape(-1), f["kn_a"].reshape(-1), f["qn_b"], f["kn_b"]])
    m["b_gate_up_T"] = f["b_gate_up"].reshape(NE, 16, P).transpose(2, 0, 1).reshape(P, NE * 16)
    m["sgu_w_T"] = f["sgu_w_2"].transpose(0, 3, 1, 2)
    m["sgu_b_T"] = f["sgu_b_2"].transpose(0, 2, 1)
    m["sgu_ln"] = cat([f["sgu_ln_g_2"], f["sgu_ln_b_2"]], 1)
    m["mla_norms"] = cat([f["mla_q_norm_g_2"], f["mla_kv_norm_g_2"]], 1)
    r, cc = np.arange(P)[:, None], np.arange(256)[None, :]
    m["rel_rows"] = f["ca_rel_bias_2"][:, :, np.minimum(r + P - cc, 128) + 128].reshape(16, P, 256)
    m["consts"] = cat([a for _, a in constant_parts()], 1)
    m["masks"] = window_masks().astype(mybir.dt.np(BF16))
    t = np.arange(S).reshape(TT, P)
    m["assignment"] = (t.T[:, :, None] * TOPK + np.arange(TOPK)).reshape(P, 16).astype(np.int32)
    m["nobody"] = np.full((P, (NE + 1) * NPOS // P), 1 << 20, np.int32)
    return {k: np.ascontiguousarray(a) for k, a in m.items()}


def kernel(**inputs):
    import concourse.bacc as bacc
    from concourse.bass_utils import run_bass_kernel_spmd

    nc = bacc.Bacc("TRN2", target_bir_lowering=False, num_devices=1)
    m = lay_out(inputs)
    A = {k: nc.dram_tensor(f"in_{k}", a.shape, mybir.dt.from_np(a.dtype), kind="ExternalInput").ap() for k, a in m.items()}
    out = nc.dram_tensor("out_0", (1, S, D), F32, kind="ExternalOutput").ap()
    build(nc, A, out)
    r = run_bass_kernel_spmd(nc, [{f"in_{k}": a for k, a in m.items()}], core_ids=[0])
    return r.results[0]["out_0"]
```

```python
from contextlib import ExitStack

import numpy as np

import concourse.bass as bass
from concourse import mybir

P = 128
S = 512
TT = S // P
D = 1024
E = 64
EPS = 1e-6
NEG = -1e30
ATT_SCALE = E ** -0.5
DILATIONS = ((128, 1), (512, 4), (2048, 16))
GRID_W = 64
NE, TOPK = 32, 4
LIMIT, ALPHA = 7.0, 1.702
NPOS = S + P
MAXBLK = S * TOPK // P + NE
MLA_SCALE = 96 ** -0.5

F32 = mybir.dt.float32
BF16 = mybir.dt.bfloat16
I32 = mybir.dt.int32
U32 = mybir.dt.uint32
ALU = mybir.AluOpType
ACT = mybir.ActivationFunctionType
AX = mybir.AxisListType



def rope_tables(dim, theta, pos):
    half = dim // 2
    inv = (theta ** (-(np.arange(half, dtype=np.float32) / np.float32(half)))).astype(np.float32)
    ang = pos.astype(np.float32)[:, None] * inv[None, :]
    c, s = np.cos(ang).astype(np.float32), np.sin(ang).astype(np.float32)
    return np.concatenate([c, c], 1), np.concatenate([-s, s], 1)


def tiled(a):
    return a.reshape(TT, P, -1).transpose(1, 0, 2).reshape(P, -1)


def window_masks():
    t = np.arange(S)
    ok = []
    for window, dil in DILATIONS:
        d = t[None, :] - t[:, None]
        ok.append((d % dil == 0) & (np.abs(d) <= (window // (2 * dil)) * dil))
    cols = []
    for i in range(TT):
        r = slice(i * P, (i + 1) * P)
        lo, hi = near(i)
        cols.append(np.concatenate([ok[2][r], ok[1][r], ok[0][r, lo * P:hi * P]], 1))
    return np.where(np.concatenate(cols, 1), 0.0, NEG).astype(np.float32)


def near(i):
    return max(0, i - 1), min(TT, i + 2)


def width_a(i):
    lo, hi = near(i)
    return 2 * S + (hi - lo) * P


def constant_parts():
    t = np.arange(S)
    r = np.arange(P)
    ca, sa = rope_tables(16, 500000.0, t)
    rc, rs = rope_tables(32, 10000.0, t // GRID_W)
    cc, cs = rope_tables(32, 10000.0, t % GRID_W)
    cm, sm = rope_tables(32, 10000.0, t)
    chunk = np.where((r[None, :] // 64) <= (r[:, None] // 64), 0.0, NEG)
    parts = [
        ("ident", np.eye(P)), ("ropeA_c", tiled(ca)), ("ropeA_s", tiled(sa)),
        ("ropeB_c", tiled(np.concatenate([rc, cc], 1))), ("ropeB_s", tiled(np.concatenate([rs, cs], 1))),
        ("ropeM_c", tiled(cm)), ("ropeM_s", tiled(sm)),
        ("chunk_mask", np.concatenate([np.zeros((P, S - P)), chunk], 1)), ("zeros", np.zeros((P, S))),
        ("before", (r[:, None] < r[None, :]) * 1.0), ("ones", np.ones((P, P))),
        ("tril_T", (r[:, None] <= r[None, :]) * 1.0),
        ("iota_e", np.tile(np.arange(NE), (P, 1))), ("iota_list", np.tile(np.arange(NE) * NPOS, (P, 1))),
        ("iota_j", np.tile(np.arange(MAXBLK + 1), (P, 1))),
        ("steps", np.tile(np.arange(TOPK) * P, (P, 1))),
    ]
    return [(n, np.ascontiguousarray(a, dtype=np.float32)) for n, a in parts]


class At(dict):

    def of(self, name):
        return self.get(name, 0)

    def step(self, by, times=1):
        for k, v in by.items():
            self[k] = self.of(k) + times * v

    def inside(self, i, by):
        c = At(self)
        for k, v in by.items():
            c[k] = self.of(k) + i * v
        return c


def build(nc, A, out):
    ctx = ExitStack()
    with ctx:
        consts = constant_parts()
        AR = ctx.enter_context(nc.sbuf_tensor("arena", [P, 53200], F32))
        PS = ctx.enter_context(nc.psum_tensor("banks", [P, 8, 512], F32))
        H2D = nc.dram_tensor("h2_rows", [S, D], F32, kind="Internal").ap()
        LIST = nc.dram_tensor("expert_lists", [(NE + 1) * NPOS, 1], I32, kind="Internal").ap()
        YD = nc.dram_tensor("expert_rows", [S * TOPK, D], F32, kind="Internal").ap()

        X, HT, W, CON = 0, 4096, 8192, 12288
        off = CON
        CO = {}
        for n, a in consts:
            CO[n] = off
            off += a.shape[1]
        NCONST = off - CON
        GAINS = off
        off += 512
        MASKA = off
        MW = sum(width_a(i) for i in range(TT))
        off += MW // 2
        RVAL = off
        off += 16
        SC = off
        PTS = SC + 3072
        QST = PTS + 1536
        SM = QST + 1536
        GROW = SM + 1024
        KST = GROW
        BIG = GROW + 1536
        LB = BIG + 6144
        VST = [SM + 256, SM + 512]
        VST3 = [SM + 256, BIG + 25600]
        assert VST3[1] + 768 <= 53200, (BIG, LB)

        def v(o, n, p=P, p0=0):
            return AR[p0:p0 + p, o:o + n]

        def v2(o, a, b, p=P, p0=0):
            return AR[p0:p0 + p, o:o + a * b].rearrange("p (a b) -> p a b", a=a)

        def v3(o, a, b, c, p=P, p0=0):
            return AR[p0:p0 + p, o:o + a * b * c].rearrange("p (a b c) -> p a b c", a=a, b=b)

        def dyn(o, n, p=P, p0=0):
            return AR[p0:p0 + p, bass.ds(o, n)]

        ident = v(CO["ident"], P)
        x3 = v2(X, TT, D)
        hT = v2(HT, 8, S)
        Wh = [v2(W, 4, 512), v2(W + 2048, 4, 512)]

        names = ("const_in mask_in grow_in norm_sq norm_ms norm_sd norm_h tr tr_free "
                 "w0_in w1_in w0_free mm ev qk_ms qk_sd qk_ready "
                 "staged qk sm p_rdy normed v_staged pt_rdy pt_free pv o_done "
                 "gb_in sig_in sig_out applied "
                 "h2_out logit_mm top_rdy top_exp sel_rdy pos_mm addr_rdy list_in listed gathered gmat_rdy table_rdy "
                 "slot_in ch0 ch1 ch2 ch3 ch4 ch5 ch_free rows_in xt xt_free act_g sig_g act_rdy rows_out "
                 "y_rdy rsc_rdy tok_rdy scattered bdown_in comb0 comb1 comb2 comb3 fin_mm x_out "
                 "ws_in ws_rdy sgu_mm sgu_in ln_sd lat_ms lat_sd lat_rdy "
                 "bias_rows0 bias_rows1 seen post_ms post_sd "
                 "pe_done act_done dve_done pool_done").split()
        SEM = {n: ctx.enter_context(nc.semaphore(n)) for n in names}

        BASE = 16
        FROM_ZERO = set("const_in mask_in grow_in w0_in w1_in h2_out gb_in list_in listed gathered slot_in ch0 ch1 ch2 "
                        "ch3 ch4 ch5 rows_in scattered bdown_in comb0 comb1 comb2 comb3 x_out ws_in bias_rows0 "
                        "bias_rows1 seen pe_done act_done dve_done pool_done".split())

        def up(count):
            return count + BASE

        def apart(eng, count):
            if not isinstance(count, int):
                eng.sem_inc(SEM["seen"])

        V, AC, G, PE = nc.vector, nc.scalar, nc.gpsimd, nc.tensor
        ENG = {"pe": PE, "act": AC, "dve": V, "pool": G}
        def fence(who, eng, c):
            ENG[who].drain().then_inc(SEM[who + "_done"], 1)
            for other in ("pe", "act", "dve", "pool"):
                if other != who:
                    eng.wait_ge(SEM[other + "_done"], c.of("fence") + 1)
                    apart(eng, c.of("fence") + 1)
            c["fence"] = c.of("fence") + 1

        def sp_after(sp, c):
            for other in ("pe", "act", "dve", "pool"):
                sp.wait_ge(SEM[other + "_done"], c.of("fence"))
                apart(sp, c.of("fence"))

        class Stage:

            def __init__(self, counts, sp=None, pe=None, act=None, dve=None, pool=None):
                self.counts = counts
                self.of_sp, self.of_pe, self.of_act, self.of_dve, self.of_pool = sp, pe, act, dve, pool

            def done(self, c):
                c.step(self.counts)

            def sp(self, sp, c):
                c["fence"] = c.of("fence") + 1
                if self.of_sp:
                    self.of_sp(sp, c)
                self.done(c)

            def pe(self, pe, c):
                fence("pe", pe, c)
                if self.of_pe:
                    self.of_pe(pe, c)
                self.done(c)

            def act(self, act, c):
                fence("act", act, c)
                if self.of_act:
                    self.of_act(act, c)
                self.done(c)

            def dve(self, dve, c):
                fence("dve", dve, c)
                if self.of_dve:
                    self.of_dve(dve, c)
                self.done(c)

            def pool(self, pool, c):
                fence("pool", pool, c)
                if self.of_pool:
                    self.of_pool(pool, c)
                self.done(c)

        def tr_pe(pe, c, k, ins):
            n = c.of("tr") + k
            pe.wait_ge(SEM["tr_free"], up(n - 3))
            apart(pe, n - 3)
            for q, a in enumerate(ins):
                m = 1
                for s_ in a.shape[1:]:
                    m *= s_
                last = PE.transpose(PS[0:m, 4 + k % 4, q * P:q * P + a.shape[0]], a, ident)
            last.then_inc(SEM["tr"], 1)

        def tr_out(eng, who, c, k, dst, cnt, m=P):
            eng.wait_ge(SEM["tr"], up(c.of("tr") + k + 1))
            apart(eng, c.of("tr") + k + 1)
            src = PS[0:m, 4 + k % 4, 0:cnt * P].rearrange("p (a t) -> p a t", a=cnt)
            if who == "act":
                AC.activation(dst, src, ACT.Copy).then_inc(SEM["tr_free"], 1)
            else:
                V.tensor_copy(dst, src).then_inc(SEM["tr_free"], 1)

        def dense_sp(sp, c, k, src):
            T = c.of("T") + k
            for h in range(2):
                for dst, s_ in [src(h)]:
                    if h == 0:
                        sp.wait_ge(SEM["w0_free"], up(T))
                        apart(sp, T)
                    else:
                        sp.wait_ge(SEM["mm"], up(4 * T))
                        apart(sp, 4 * T)
                    sp.dma_start(dst, s_).then_inc(SEM["w0_in" if h == 0 else "w1_in"], 16)

        def dense_pe(pe, c, k, lhsT, kt, ncols, before=None, moving=None):
            T = c.of("T") + k
            for h in range(2):
                pe.wait_ge(SEM["w0_in" if h == 0 else "w1_in"], 16 * T + 16)
                apart(pe, 16 * T + 16)
                for tt in range(TT):
                    if h == 0:
                        pe.wait_ge(SEM["ev"], up(4 * T + tt - 3))
                        apart(pe, 4 * T + tt - 3)
                    elif before:
                        before(tt)
                    if kt == 1:
                        hc = ncols // 2
                        last = PE.matmul(PS[:, tt, h * hc:(h + 1) * hc], lhsT(0, tt), Wh[h][:, 0, 0:hc],
                                         start=True, stop=True)
                    else:
                        for q in range(kt // 2):
                            kk = h * (kt // 2) + q
                            if moving:
                                last = PE.matmul(PS[:, tt], Wh[h][:, q, tt * P:(tt + 1) * P], moving(kk),
                                                 start=(kk == 0), stop=(kk == kt - 1))
                            else:
                                last = PE.matmul(PS[:, tt, 0:ncols], lhsT(kk, tt), Wh[h][:, q, 0:ncols],
                                                 start=(kk == 0), stop=(kk == kt - 1))
                    if h == 1:
                        last.then_inc(SEM["mm"], 1)
                if h == 0:
                    last.then_inc(SEM["w0_free"], 1)

        def unit(c, k, tt):
            return 4 * (c.of("T") + k) + tt + 1

        def rows(ap2d, kt, h, c0, ncols):
            src = ap2d.rearrange("(k p) n -> p k n", p=P)[:, h * (kt // 2):(h + 1) * (kt // 2), bass.ds(c0, ncols)]
            return Wh[h][:, 0:kt // 2, 0:ncols], src

        def norm_stage(gain, HB, want_h2=False):
            ss = v(SM, 4)
            sd = v(SM + 4, 4)
            hb = v2(HB, TT, D)

            def sp_(sp, c):
                sp_after(sp, c)
                sp.dma_start(v(GROW, D), gain(c).partition_broadcast(P)).then_inc(SEM["grow_in"], 16)
                if want_h2:
                    sp.wait_ge(SEM["norm_h"], up(c.of("norm_h") + 4))
                    apart(sp, c.of("norm_h") + 4)
                    sp.dma_start(H2D.rearrange("(t p) d -> p t d", p=P), hb).then_inc(SEM["h2_out"], 16)

            def act_(act, c):
                def square(tt):
                    AC.activation(hb[:, tt], x3[:, tt], ACT.Square, accum_out=ss[:, tt:tt + 1]).then_inc(SEM["norm_sq"], 1)
                square(0)
                for tt in range(TT):
                    if tt + 1 < TT:
                        square(tt + 1)
                    act.wait_ge(SEM["norm_ms"], up(c.of("norm_ms") + tt + 1))
                    apart(act, c.of("norm_ms") + tt + 1)
                    AC.activation(sd[:, tt:tt + 1], ss[:, tt:tt + 1], ACT.Sqrt).then_inc(SEM["norm_sd"], 1)
                for tt in range(TT):
                    for q in range(2):
                        tr_out(act, "act", c, 2 * tt + q, hT[:, 4 * q:4 * q + 4, tt * P:(tt + 1) * P], 4)

            def dve_(dve, c):
                def mean(tt):
                    dve.wait_ge(SEM["norm_sq"], up(c.of("norm_sq") + tt + 1))
                    apart(dve, c.of("norm_sq") + tt + 1)
                    m = ss[:, tt:tt + 1]
                    V.tensor_scalar(m, m, 1.0 / D, EPS, ALU.mult, ALU.add).then_inc(SEM["norm_ms"], 1)
                dve.wait_ge(SEM["grow_in"], 16 * c.of("grow") + 16)
                apart(dve, 16 * c.of("grow") + 16)
                mean(0)
                for tt in range(TT):
                    if tt + 1 < TT:
                        mean(tt + 1)
                    dve.wait_ge(SEM["norm_sd"], up(c.of("norm_sd") + tt + 1))
                    apart(dve, c.of("norm_sd") + tt + 1)
                    V.reciprocal(sd[:, tt:tt + 1], sd[:, tt:tt + 1])
                    V.drain()
                    V.scalar_tensor_tensor(hb[:, tt], x3[:, tt], sd[:, tt:tt + 1], v(GROW, D),
                                           ALU.mult, ALU.mult).then_inc(SEM["norm_h"], 1)

            def pe_(pe, c):
                for tt in range(TT):
                    pe.wait_ge(SEM["norm_h"], up(c.of("norm_h") + tt + 1))
                    apart(pe, c.of("norm_h") + tt + 1)
                    for q in range(2):
                        tr_pe(pe, c, 2 * tt + q, [hb[:, tt, (4 * q + a) * P:(4 * q + a + 1) * P] for a in range(4)])

            return Stage({"norm_sq": 4, "norm_ms": 4, "norm_sd": 4, "norm_h": 4, "grow": 1, "tr": 8},
                  sp=sp_, act=act_, dve=dve_, pe=pe_)

        ST = [v(SC + 512 * tt, 512) for tt in range(TT)]
        SQ = [v(PTS + 512 * (tt % 2), 512) for tt in range(TT)]

        def rotate(dst, src, tc, ts, nh, nb, half, paired=False):
            w = nb * 2 * half
            cu = v(QST, nh * w).rearrange("p (h b) -> p h b", h=nh)
            cv = v(QST + 512, nh * w).rearrange("p (h b j e) -> p h b j e", h=nh, b=nb, j=2)
            V.tensor_tensor(cu, src, tc.unsqueeze(1).to_broadcast([P, nh, w]), ALU.mult)
            s5 = src.rearrange("p h (b j e) -> p h b j e", b=nb, j=2)
            t4 = ts.rearrange("p (b j e) -> p b j e", b=nb, j=2)
            for b in range(nb):
                for j in range(2):
                    V.tensor_tensor(cv[:, :, b, j], s5[:, :, b, 1 - j],
                                    t4[:, b, j].unsqueeze(1).to_broadcast([P, nh, half]), ALU.mult)
            V.drain()
            cv3 = v(QST + 512, nh * w).rearrange("p (h b) -> p h b", h=nh)
            if paired:
                def by(a):
                    return a.rearrange("p (s a) e -> p s a e", s=2)
                to = dst.rearrange("p (a s) e -> p s a e", s=2)
                return V.tensor_tensor(to, by(cu), by(cv3), ALU.add)
            return V.tensor_tensor(dst, cu, cv3, ALU.add)

        def qk_tile(k, cfg, prev):
            nh = cfg["nh"]

            def pe_(pe, c):
                def before(tt):
                    if prev:
                        pe.wait_ge(SEM["qk_ready"], up(c.of("qk_ready") + 4 * (k - 1) + tt + 1))
                        apart(pe, c.of("qk_ready") + 4 * (k - 1) + tt + 1)
                        tr_pe(pe, c, 4 * (k - 1) + tt, prev["ins"](tt))
                dense_pe(pe, c, k, lambda kk, tt: hT[:, kk, tt * P:(tt + 1) * P], 8, cfg["ncols"], before)

            def act_(act, c):
                for tt in range(TT):
                    if prev:
                        tr_out(act, "act", c, 4 * (k - 1) + tt, prev["dst"](c, k - 1, tt), prev["cnt"])
                    act.wait_ge(SEM["mm"], up(unit(c, k, tt)))
                    apart(act, unit(c, k, tt))
                    AC.activation(ST[tt][:, 0:cfg["ncols"]], PS[:, tt, 0:cfg["ncols"]], ACT.Copy)
                    if cfg.get("v_out"):
                        AC.activation(cfg["v_out"](tt), PS[:, tt, nh * E:cfg["ncols"]], ACT.Copy)
                    act.wait_ge(SEM["qk_ms"], up(c.of("qk_ms") + 4 * k + tt - 1 if k + tt else c.of("qk_ms")))
                    apart(act, c.of("qk_ms") + 4 * k + tt - 1 if k + tt else c.of("qk_ms"))
                    AC.activation(SQ[tt][:, 0:nh * E], PS[:, tt, 0:nh * E], ACT.Square).then_inc(SEM["ev"], 1)
                    act.wait_ge(SEM["qk_ms"], up(c.of("qk_ms") + 4 * k + tt + 1))
                    apart(act, c.of("qk_ms") + 4 * k + tt + 1)
                    AC.activation(v(SM + 16 + 8 * tt, nh), v(SM + 16 + 8 * tt, nh), ACT.Sqrt).then_inc(SEM["qk_sd"], 1)

            def dve_(dve, c):
                for tt in range(TT):
                    ms = v(SM + 16 + 8 * tt, nh)
                    st = ST[tt][:, 0:nh * E].rearrange("p (h e) -> p h e", h=nh)
                    dve.wait_ge(SEM["ev"], up(unit(c, k, tt)))
                    apart(dve, unit(c, k, tt))
                    V.tensor_reduce(ms, SQ[tt][:, 0:nh * E].rearrange("p (h e) -> p h e", h=nh), AX.X, ALU.add)
                    V.drain()
                    V.tensor_scalar(ms, ms, 1.0 / E, EPS, ALU.mult, ALU.add).then_inc(SEM["qk_ms"], 1)
                    dve.wait_ge(SEM["qk_sd"], up(c.of("qk_sd") + 4 * k + tt + 1))
                    apart(dve, c.of("qk_sd") + 4 * k + tt + 1)
                    V.reciprocal(ms, ms)
                    V.drain()
                    V.tensor_tensor(st, st, ms.unsqueeze(2).to_broadcast([P, nh, E]), ALU.mult)
                    V.drain()
                    V.tensor_tensor(st, st, cfg["gain"](c, k).unsqueeze(1).to_broadcast([P, nh, E]), ALU.mult)
                    V.drain()
                    nb, half, tc, ts = cfg["rope"]
                    w = nb * 2 * half
                    rot = st[:, :, 0:w]
                    rotate(rot, rot, v(tc + w * tt, w), v(ts + w * tt, w), nh, nb, half,
                           cfg.get("paired")).then_inc(SEM["qk_ready"], 1)

            return {"pe": pe_, "act": act_, "dve": dve_}

        QKT, VA, QBT, KBT, VB, OA, OB = (BIG + o for o in (0, 12288, 18432, 20480, 20992, 21504, 23552))
        w_in = A["w_in"]
        RA = (1, 8, CO["ropeA_c"], CO["ropeA_s"])
        RB = (2, 16, CO["ropeB_c"], CO["ropeB_s"])

        def pair_ins(tt):
            return [ST[tt][:, a * P:(a + 1) * P] for a in range(4)]

        def dst_pairs(base):
            def dst(c, k, tt):
                o = (c.of("tile") + k) * 2048 + base
                return dyn(o, 2048).rearrange("p (a t) -> p a t", a=4)[:, :, tt * P:(tt + 1) * P]
            return dst

        cfgA = {"nh": 8, "ncols": 512, "rope": RA, "ins": pair_ins, "cnt": 4, "dst": dst_pairs(QKT),
                "gain": lambda c, k: dyn(GAINS + (c.of("tile") + k) * E, E)}
        cfgQB = {"nh": 8, "ncols": 512, "rope": RB, "cnt": 4, "ins": pair_ins, "paired": True,
                 "dst": lambda c, k, tt: v2(QBT, 4, S)[:, :, tt * P:(tt + 1) * P],
                 "gain": lambda c, k: v(GAINS + 6 * E, E)}
        cfgKB = {"nh": 2, "ncols": 256, "rope": RB, "cnt": 1,
                 "ins": lambda tt: [ST[tt][:, 0:P]],
                 "dst": lambda c, k, tt: v2(KBT, 1, S)[:, :, tt * P:(tt + 1) * P],
                 "v_out": lambda tt: v2(VB, TT, P)[:, tt],
                 "gain": lambda c, k: v(GAINS + 7 * E, E)}
        QKC = {"tr": 4, "T": 1, "qk_ms": 4, "qk_sd": 4, "qk_ready": 4, "tile": 1}

        def constants():
            def sp_(sp, c):
                sp.dma_start(x3, A["x"].rearrange("b (t p) d -> p (b t) d", p=P)).then_inc(SEM["const_in"], 16)
                sp.dma_start(v(CON, NCONST), A["consts"]).then_inc(SEM["const_in"], 16)
                sp.dma_start(v(GAINS, 512), A["qk_gains"].partition_broadcast(P)).then_inc(SEM["const_in"], 16)
                sp.dma_start(v(RVAL, 16).bitcast(I32), A["assignment"]).then_inc(SEM["mask_in"], 16)
                sp.dma_start(v(MASKA, MW // 2).bitcast(BF16), A["masks"]).then_inc(SEM["mask_in"], 16)

            def any_(eng, c):
                eng.wait_ge(SEM["const_in"], 48)

            return Stage({}, sp=sp_, pe=any_, act=any_, dve=any_, pool=any_)

        def project_first():
            first, inner = qk_tile(0, cfgA, None), qk_tile(0, cfgA, cfgA)
            qb, kb = qk_tile(6, cfgQB, cfgA), qk_tile(7, cfgKB, cfgQB)

            def qk_program(who):
                def run(eng, c):
                    first[who](eng, c)
                    with eng.Fori(1, 6) as i:
                        inner[who](eng, c.inside(i, QKC))
                    qb[who](eng, c)
                    kb[who](eng, c)
                    if who == "pe":
                        for tt in range(TT):
                            eng.wait_ge(SEM["qk_ready"], up(c.of("qk_ready") + 28 + tt + 1))
                            apart(eng, c.of("qk_ready") + 28 + tt + 1)
                            tr_pe(eng, c, 28 + tt, cfgKB["ins"](tt))
                    if who == "act":
                        for tt in range(TT):
                            tr_out(eng, "act", c, 28 + tt, cfgKB["dst"](c, 7, tt), 1)
                return run

            def sp_(sp, c):
                with sp.Fori(0, 6) as i:
                    dense_sp(sp, c.inside(i, QKC), 0, lambda h: rows(w_in, 8, h, i * 512, 512))
                dense_sp(sp, c, 6, lambda h: rows(w_in, 8, h, 4608, 512))
                dense_sp(sp, c, 7, lambda h: rows(w_in, 8, h, 5120, 256))
            heads = Stage({k: 8 * n for k, n in QKC.items()}, sp=sp_, pe=qk_program("pe"), act=qk_program("act"),
                  dve=qk_program("dve"))

            def v_sp(sp, c):
                with sp.Fori(0, 3) as i:
                    dense_sp(sp, c.inside(i, {"T": 1}), 0, lambda h: rows(w_in, 8, h, i * 512 + 3072, 512))

            def v_pe(pe, c):
                with pe.Fori(0, 3) as i:
                    dense_pe(pe, c.inside(i, {"T": 1}), 0, lambda kk, tt: hT[:, kk, tt * P:(tt + 1) * P], 8, 512)

            def v_act(act, c):
                with act.Fori(0, 3) as i:
                    ci = c.inside(i, {"T": 1})
                    for tt in range(TT):
                        act.wait_ge(SEM["mm"], up(unit(ci, 0, tt)))
                        apart(act, unit(ci, 0, tt))
                        AC.activation(dyn(VA + tt * 1536 + i * 512, 512), PS[:, tt], ACT.Copy).then_inc(SEM["ev"], 1)

            def v_dve(dve, c):
                dve.wait_ge(SEM["mask_in"], 32)
            return heads, Stage({"T": 3}, sp=v_sp, pe=v_pe, act=v_act, dve=v_dve)

        def attention(a):
            Gn, npairs, wide = a["groups"], a["pairs"], a.get("wide")
            KC = {"u": 8, "g": 8 * Gn, "staged": 2, "bias": 1 if a.get("sp") else 0}

            def prob(x):
                return (SC, SC + 1536, W, W + 2048)[x % 4] if wide else SC + 512 * (x % 4)

            ahead = 0 if wide else 1

            def bank(x):
                return ahead * (x % 2)

            banks = 3 if wide else 2

            def turned(x, gi):
                return (3, 4, 7)[gi] if wide else 3 + x % 2

            def turn_at(x):
                return PTS if wide else PTS + 512 * (x % 2)

            def negmax(x):
                return v(SM + 128 + x % 4, 1)

            def rowsum(x):
                return v(SM + 132 + x % 4, 1)

            def pairs(eng, c0, first, body):
                first(c0)
                with eng.Fori(0, npairs - 1) as p:
                    body(c0.inside(p, KC), p, False)
                c = At(c0)
                c.step(KC, npairs - 1)
                body(c, npairs - 1, True)

            def place(p, x):
                return p + x // 8, x % 8 // TT, x % TT

            def pe_(pe, c0):
                def QK(c, p, x):
                    pp, s, i = place(p, x)
                    if i == 0:
                        pe.wait_ge(SEM["staged"], up(c.of("staged") + x // 4 + 1))
                        apart(pe, c.of("staged"))
                    pe.wait_ge(SEM["sm"], up(c.of("u") + x - ahead))
                    apart(pe, c.of("u"))
                    for lhsT, rhs, o, n in a["scores"](pp, s, i):
                        last = PE.matmul(PS[:, bank(x) + o // 512, o % 512:o % 512 + n], lhsT, rhs, start=True, stop=True)
                    last.then_inc(SEM["qk"], 1)

                def T(c, x):
                    u, g = c.of("u"), c.of("g")
                    nt = a["W"](x % TT) // P
                    pe.wait_ge(SEM["normed"], up(u + x + 1))
                    apart(pe, u)
                    for gi in range(Gn):
                        pe.wait_ge(SEM["pt_free"], up(g + x * Gn + gi + 1 - banks))
                        apart(pe, g)
                        for q in range(gi * 4, min(nt, gi * 4 + 4)):
                            last = PE.transpose(PS[:, turned(x, gi), (q % 4) * P:(q % 4 + 1) * P],
                                                v(prob(x) + q * P, P), ident)
                        last.then_inc(SEM["pt_rdy"], 1)

                def body(c, p, final):
                    u, g = c.of("u"), c.of("g")
                    for x in range(8):
                        _, s, i = place(p, x)
                        nt = a["W"](i) // P
                        if x + 3 < 8 or not final:
                            QK(c, p, x + 3)
                        if x + 1 < 8 or not final:
                            T(c, x + 1)
                        if i == 0:
                            pe.wait_ge(SEM["o_done"], up(c.of("staged") + s - 1))
                            apart(pe, u)
                            pe.wait_ge(SEM["v_staged"], up(c.of("staged") + s + 1))
                            apart(pe, u)
                        tiles = a["tiles"](i)
                        for q in range(nt):
                            if q % 4 == 0:
                                pe.wait_ge(SEM["pt_free"], up(g + x * Gn + q // 4 + 1))
                                apart(pe, g)
                            last = PE.matmul(PS[E * s:E * (s + 1), 5 + s, i * P:(i + 1) * P],
                                             v((VST3 if wide else VST)[s] + tiles[q] * E, E), v(turn_at(x) + q * P, P),
                                             start=(q == 0), stop=(q == nt - 1))
                        last.then_inc(SEM["pv"], 1)

                def first(c):
                    for x in range(3):
                        QK(c, 0, x)
                    T(c, 0)
                pairs(pe, c0, first, body)

            def act_(act, c0):
                def exp(c, p, x):
                    w = a["W"](x % TT)
                    act.wait_ge(SEM["sm"], up(c.of("u") + x + 1))
                    apart(act, c.of("u"))
                    sc = v(prob(x), w)
                    AC.activation(sc, sc, ACT.Exp, bias=negmax(x), scale=a["scale"],
                                  accum_out=rowsum(x)).then_inc(SEM["p_rdy"], 1)

                def copy_T(c, x):
                    u, g = c.of("u"), c.of("g")
                    w = a["W"](x % TT)
                    for gi in range(Gn):
                        n = min(w - gi * 512, 512)
                        act.wait_ge(SEM["pt_rdy"], up(g + x * Gn + gi + 1))
                        apart(act, g)
                        if gi == 0:
                            act.wait_ge(SEM["pv"], up(u + x - ahead))
                            apart(act, u)
                        AC.activation(v(turn_at(x) + gi * 512, n), PS[:, turned(x, gi), 0:n], ACT.Copy).then_inc(
                            SEM["pt_free"], 1)

                def body(c, p, final):
                    for x in range(8):
                        if x + 2 < 8 or not final:
                            exp(c, p, x + 2)
                        if x + 1 < 8 or not final:
                            copy_T(c, x + 1)

                def first(c):
                    exp(c, 0, 0)
                    exp(c, 0, 1)
                    copy_T(c, 0)
                pairs(act, c0, first, body)

            def dve_(dve, c0):
                def top(c, p, x):
                    pp, s, i = place(p, x)
                    w = a["W"](i)
                    dve.wait_ge(SEM["qk"], up(c.of("u") + x + 1))
                    apart(dve, c.of("u"))
                    dve.wait_ge(SEM["pt_rdy"], up(c.of("g") + Gn * (x - 3)))
                    apart(dve, c.of("g"))
                    if i == 0 and a.get("sp"):
                        dve.wait_ge(SEM["staged"], up(c.of("staged") + x // 4 + 1))
                        apart(dve, c.of("staged"))
                    m = v(SM + 136 + x % 4, 1)
                    sc = PS[:, bank(x):bank(x) + 3].rearrange("p a b -> p (a b)")[:, 0:w]
                    V.tensor_tensor_reduce(out=v(prob(x), w), in0=sc, in1=a["mask"](s, i), scale=1.0,
                                           scalar=-3e38, op0=ALU.add, op1=ALU.max, accum_out=m)
                    V.drain()
                    V.tensor_scalar(negmax(x), m, -a["scale"], None, ALU.mult).then_inc(SEM["sm"], 1)

                def norm(c, p, x):
                    dve.wait_ge(SEM["p_rdy"], up(c.of("u") + x + 1))
                    apart(dve, c.of("u"))
                    r = v(SM + 140 + x % 4, 1)
                    V.reciprocal(r, rowsum(x))
                    V.drain()
                    pr = v(prob(x), a["W"](x % TT))
                    V.tensor_scalar(pr, pr, r, None, ALU.mult).then_inc(SEM["normed"], 1)

                def body(c, p, final):
                    for x in range(8):
                        if x + 3 < 8 or not final:
                            top(c, p, x + 3)
                        if x + 2 < 8 or not final:
                            norm(c, p, x + 2)
                        _, s, i = place(p, x)
                        if i == TT - 1:
                            dve.wait_ge(SEM["pv"], up(c.of("u") + x + 1))
                            apart(dve, c.of("u"))
                            a["finish"](p, s, PS[E * s:E * (s + 1), 5 + s]).then_inc(SEM["o_done"], 1)

                def first(c):
                    for x in range(3):
                        top(c, 0, x)
                    norm(c, 0, 0)
                    norm(c, 0, 1)
                pairs(dve, c0, first, body)

            def pool_(pool, c0):
                def bring(c, p, s):
                    G.drain()
                    a["stage"](pool, c, p, s).then_inc(SEM["staged"], 1)

                def bring_values(c, p, s):
                    G.drain()
                    a["values"](p, s).then_inc(SEM["v_staged"], 1)

                for s in range(2):
                    bring(c0, 0, s)
                    bring_values(c0, 0, s)
                with pool.Fori(0, npairs - 1) as p:
                    c = c0.inside(p, KC)
                    for s in range(2):
                        pool.wait_ge(SEM["sm"], up(c.of("u") + 4 * (s + 1)))
                        apart(pool, c.of("u"))
                        bring(c.inside(1, KC), p + 1, s)
                        pool.wait_ge(SEM["pv"], up(c.of("u") + 4 * (s + 1)))
                        apart(pool, c.of("u"))
                        bring_values(c, p + 1, s)

            def sp_(sp, c0):
                if a.get("sp"):
                    sp_after(sp, c0)
                    a["sp"](sp, c0, 0, 0)
                    a["sp"](sp, c0, 0, 1)
                    with sp.Fori(0, npairs - 1) as p:
                        c = c0.inside(p, KC)
                        for s in range(2):
                            sp.wait_ge(SEM["staged"], up(c.of("staged") + s + 1))
                            apart(sp, c.of("staged"))
                            a["sp"](sp, c, p + 1, s)

            return Stage({k: n * npairs for k, n in KC.items()}, pe=pe_, act=act_, dve=dve_, pool=pool_, sp=sp_)

        def bring_tiles(dst, at, stride):
            src = dyn(at, TT * stride).rearrange("p (k n) -> p k n", k=TT)[:, :, 0:E]
            return G.tensor_copy(v2(dst, TT, E), src)

        def qst(s, g, n, p=E):
            return v(QST + 512 * g, n, p, E * s)

        def kst(s, g, n):
            return v(KST + 512 * g, n, E, E * s)

        def attention_first():
            def stage_(pool, c, p, s):
                for g in range(3):
                    G.tensor_copy(qst(s, g, S), dyn(QKT + (4 * g) * 512 + p * 512, S, E, E * s))
                    last = G.tensor_copy(kst(s, g, S), dyn(QKT + (12 + 4 * g) * 512 + p * 512, S, E, E * s))
                return last

            def scores(p, s, i):
                lo, hi = near(i)
                r = []
                for g, o, c0, n in ((2, 0, 0, S), (1, S, 0, S), (0, 2 * S, lo * P, (hi - lo) * P)):
                    r.append((v(QST + 512 * g + i * P, P, E, E * s),
                              v(KST + 512 * g + c0, n, E, E * s), o, n))
                return r

            moff = [sum(width_a(j) for j in range(i)) for i in range(TT)]
            maskb = v(MASKA, MW // 2).bitcast(BF16)

            def tiles(i):
                lo, hi = near(i)
                return list(range(8)) + [8 + k for k in range(lo, hi)]

            def values(p, s):
                for n, g in enumerate((2, 1, 0)):
                    last = bring_tiles(VST3[s] + n * TT * E, VA + g * 512 + s * E + p * P, 1536)
                return last

            dilated = attention({"groups": 3, "wide": True, "pairs": 4, "scale": ATT_SCALE, "W": width_a,
                                 "stage": stage_, "scores": scores, "values": values, "tiles": tiles,
                                 "finish": lambda p, s, ps: V.tensor_copy(dyn(OA + p * 512, S, E, E * s), ps),
                                 "mask": lambda s, i: maskb[:, moff[i]:moff[i] + width_a(i)]})

            grouped = attention({"groups": 1, "pairs": 4, "scale": ATT_SCALE, "W": lambda i: S,
                                 "stage": lambda pool, c, p, s: G.tensor_copy(qst(s, 0, S), dyn(QBT + p * 512, S, E, E * s)),
                                 "scores": lambda p, s, i: [(v(QST + i * P, P, E, E * s), v(KBT, S, E, E * s), 0, S)],
                                 "values": lambda p, s: G.tensor_copy(v2(VST[s], TT, E), v2(VB, TT, P)[:, :, s * E:s * E + E]),
                                 "tiles": lambda i: list(range(TT)),
                                 "finish": lambda p, s, ps: V.tensor_copy(dyn(OB + p * 512, S, E, E * s), ps),
                                 "mask": lambda s, i: v(CO["zeros"], S)})
            return dilated, grouped

        def transpose_stage(items):
            def units():
                k = 0
                for src, dst, F in items:
                    for tt in range(TT):
                        for q in range(F // 4):
                            yield k, tt, q, src, dst
                            k += 1
            total = sum(F for _, _, F in items)

            def pe_(pe, c):
                for k, tt, q, src, dst in units():
                    tr_pe(pe, c, k, [src[:, tt, (4 * q + a) * P:(4 * q + a + 1) * P] for a in range(4)])

            def dve_(dve, c):
                for k, tt, q, src, dst in units():
                    if k % 2 == 1:
                        dve.wait_ge(SEM["tr_free"], up(c.of("tr") + k))
                        apart(dve, c.of("tr") + k)
                        tr_out(dve, "dve", c, k, dst[:, 4 * q:4 * q + 4, tt * P:(tt + 1) * P], 4)

            def act2(act, c):
                for k, tt, q, src, dst in units():
                    if k % 2 == 0:
                        act.wait_ge(SEM["tr_free"], up(c.of("tr") + k))
                        apart(act, c.of("tr") + k)
                        tr_out(act, "act", c, k, dst[:, 4 * q:4 * q + 4, tt * P:(tt + 1) * P], 4)
            return Stage({"tr": total}, pe=pe_, act=act2, dve=dve_)

        def merge_stage(B, nbr, yT, w_branch, w_gate, gate_bias, gb_at):
            merged = v2(B + 4096 + (2048 if nbr == 3 else 0), TT, D)
            base = B + 4096 + (2048 if nbr == 3 else 0)
            PJ = base + 8192
            GS = PJ + 2048
            KC = {"T": 2 * nbr, "sig": 4 * nbr}

            def sp_(sp, c0):
                sp_after(sp, c0)
                sp.dma_start(v(gb_at, nbr * D), gate_bias(c0).partition_broadcast(P)).then_inc(SEM["gb_in"], 16)
                with sp.Fori(0, 2) as n:
                    c = c0.inside(n, KC)
                    for b in range(nbr):
                        dense_sp(sp, c, 2 * b, lambda h: rows(w_branch(c0, b), 4, h, n * 512, 512))
                        dense_sp(sp, c, 2 * b + 1, lambda h: rows(w_gate[0](c0), 8, h, n * 512 + w_gate[1] + b * D, 512))

            def pe_(pe, c0):
                with pe.Fori(0, 2) as n:
                    c = c0.inside(n, KC)
                    for b in range(nbr):
                        dense_pe(pe, c, 2 * b, lambda kk, tt: yT[b][:, kk, tt * P:(tt + 1) * P], 4, 512)
                        dense_pe(pe, c, 2 * b + 1, lambda kk, tt: hT[:, kk, tt * P:(tt + 1) * P], 8, 512)

            def act_(act, c0):
                with act.Fori(0, 2) as n:
                    c = c0.inside(n, KC)
                    for b in range(nbr):
                        for tt in range(TT):
                            act.wait_ge(SEM["mm"], up(unit(c, 2 * b, tt)))
                            apart(act, unit(c, 2 * b, tt))
                            act.wait_ge(SEM["applied"], up(c.of("sig") + (4 * b + tt - 3 if b else 0)))
                            apart(act, c.of("sig") + (4 * b + tt - 3 if b else 0))
                            AC.activation(v(PJ + 512 * tt, 512), PS[:, tt], ACT.Copy).then_inc(SEM["ev"], 1)
                        for tt in range(TT):
                            act.wait_ge(SEM["sig_in"], up(c.of("sig") + 4 * b + tt + 1))
                            apart(act, c.of("sig") + 4 * b + tt + 1)
                            g = v(GS + 512 * tt, 512)
                            AC.activation(g, g, ACT.Sigmoid).then_inc(SEM["sig_out"], 1)

            def dve_(dve, c0):
                V.memset(v(base, 4096), 0.0)
                V.drain()
                dve.wait_ge(SEM["gb_in"], 16 * c0.of("gb") + 16)
                apart(dve, 16 * c0.of("gb") + 16)
                with dve.Fori(0, 2) as n:
                    c = c0.inside(n, KC)
                    for b in range(nbr):
                        def logits(tt):
                            dve.wait_ge(SEM["mm"], up(unit(c, 2 * b + 1, tt)))
                            apart(dve, unit(c, 2 * b + 1, tt))
                            V.tensor_tensor(v(GS + 512 * tt, 512), PS[:, tt], dyn(gb_at + b * D + n * 512, 512),
                                            ALU.add).then_inc(SEM["ev"], 1)
                            V.drain().then_inc(SEM["sig_in"], 1)

                        def apply(tt):
                            dve.wait_ge(SEM["sig_out"], up(c.of("sig") + 4 * b + tt + 1))
                            apart(dve, c.of("sig") + 4 * b + tt + 1)
                            dve.wait_ge(SEM["ev"], up(unit(c, 2 * b, tt)))
                            apart(dve, unit(c, 2 * b, tt))
                            g = v(GS + 512 * tt, 512)
                            V.tensor_tensor(g, g, v(PJ + 512 * tt, 512), ALU.mult)
                            V.drain()
                            m = dyn(base + tt * D + n * 512, 512)
                            V.tensor_tensor(m, m, g, ALU.add).then_inc(SEM["applied"], 1)
                        for tt in range(TT):
                            logits(tt)
                            if tt:
                                apply(tt - 1)
                        apply(TT - 1)
                        V.drain()
            merge = Stage({"T": 4 * nbr, "sig": 8 * nbr, "gb": 1}, sp=sp_, pe=pe_, act=act_, dve=dve_)
            turned = v2(base + 4096, 8, S)
            return merge, transpose_stage([(merged, turned, 8)]), turned

        def out_products(mT, w_out):
            def sp_(sp, c0):
                with sp.Fori(0, 2) as n:
                    dense_sp(sp, c0.inside(n, {"T": 1}), 0, lambda h: rows(w_out(c0), 8, h, n * 512, 512))

            def pe_(pe, c0):
                with pe.Fori(0, 2) as n:
                    dense_pe(pe, c0.inside(n, {"T": 1}), 0, lambda kk, tt: mT[:, kk, tt * P:(tt + 1) * P], 8, 512)
            return sp_, pe_

        def out_stage(mT, w_out):
            sp_, pe_ = out_products(mT, w_out)

            def dve_(dve, c0):
                with dve.Fori(0, 2) as n:
                    c = c0.inside(n, {"T": 1})
                    for tt in range(TT):
                        dve.wait_ge(SEM["mm"], up(unit(c, 0, tt)))
                        apart(dve, unit(c, 0, tt))
                        xs = dyn(X + tt * D + n * 512, 512)
                        V.tensor_tensor(xs, xs, PS[:, tt], ALU.add).then_inc(SEM["ev"], 1)
            return Stage({"T": 2}, sp=sp_, pe=pe_, dve=dve_)

        R = SC
        GATES, GT, BT = R + 2560, R + 2624, R + 3200
        WR = BIG + 8192
        TAB = QST
        BE, BOFF, NBLK, FEW = SM + 64, SM + 128, SM + 192, SM + 256

        def router_stage():
            lg, mx, ix, e4, idxf = (v2(R, TT, NE), v2(R + 128, TT, 8), v2(R + 160, TT, 8),
                                    v2(R + 192, TT, 4), v2(R + 208, TT, 4))
            oh = v2(R + 256, 16, NE)
            M = v2(R + 768, TT, NE)
            tmp = v2(R + 896, 16, NE)
            posd = v2(R + 1408, TT, NE)
            Gm = v2(R + 1536, TT, NE)
            addrf = v(R + 1664, 16)
            addr = v(R + 1696, 16).bitcast(I32)
            brow = v(R + 1728, NE)
            gates = v2(GATES, TT, 4)
            sent = v(BIG + 12288, (NE + 1) * NPOS // P).bitcast(I32)

            def sp_(sp, c):
                sp.dma_start(v2(WR, 8, NE), A["w_router"].rearrange("(k p) e -> p k e", p=P)).then_inc(SEM["slot_in"], 16)
                sp.dma_start(brow, A["b_router"].partition_broadcast(P)).then_inc(SEM["slot_in"], 16)
                sp.dma_start(sent, A["nobody"]).then_inc(SEM["slot_in"], 16)
                sp.dma_start(v(BT, 512), A["b_gate_up_T"]).then_inc(SEM["slot_in"], 16)
                sp.wait_ge(SEM["slot_in"], 64)
                sp.dma_start(LIST.rearrange("(p n) o -> p (n o)", p=P), sent).then_inc(SEM["list_in"], 16)

            def pe_(pe, c):
                pe.wait_ge(SEM["slot_in"], 64)
                for tt in range(TT):
                    for k in range(8):
                        last = PE.matmul(PS[:, 0, tt * NE:(tt + 1) * NE], hT[:, k, tt * P:(tt + 1) * P],
                                         v2(WR, 8, NE)[:, k], start=(k == 0), stop=(k == 7))
                last.then_inc(SEM["logit_mm"], 1)
                pe.wait_ge(SEM["sel_rdy"], up(1))
                for tt in range(TT):
                    for q in range(tt + 1):
                        PE.matmul(PS[:, 1, tt * NE:(tt + 1) * NE], v(CO["ones"] if q < tt else CO["before"], P),
                                  M[:, q], start=(q == 0), stop=(q == tt))
                for q in range(TT):
                    last = PE.matmul(PS[:, 2, 0:NE], v(CO["ones"], P), M[:, q], start=(q == 0), stop=(q == TT - 1))
                last.then_inc(SEM["pos_mm"], 1)
                pe.wait_ge(SEM["gmat_rdy"], up(1))
                for tt in range(TT):
                    last = PE.transpose(PS[0:NE, 3, tt * P:(tt + 1) * P], Gm[:, tt], ident)
                last.then_inc(SEM["logit_mm"], 1)

            def act_(act, c):
                act.wait_ge(SEM["top_rdy"], up(1))
                AC.activation(e4, e4, ACT.Exp).then_inc(SEM["top_exp"], 1)
                act.wait_ge(SEM["logit_mm"], up(2))
                AC.activation(v(GT, S, NE), PS[0:NE, 3], ACT.Copy)

            def dve_(dve, c):
                dve.wait_ge(SEM["slot_in"], 64)
                dve.wait_ge(SEM["logit_mm"], up(1))
                V.tensor_tensor(lg, PS[:, 0, 0:TT * NE].rearrange("p (t e) -> p t e", t=TT),
                                brow.unsqueeze(1).to_broadcast([P, TT, NE]), ALU.add)
                V.drain()
                for tt in range(TT):
                    V.max(mx[:, tt], lg[:, tt])
                V.drain()
                for tt in range(TT):
                    V.max_index(ix[:, tt].bitcast(U32), mx[:, tt], lg[:, tt])
                V.tensor_tensor(e4, mx[:, :, 0:4], mx[:, :, 0:1].to_broadcast([P, TT, 4]), ALU.subtract)
                V.drain().then_inc(SEM["top_rdy"], 1)
                V.tensor_copy(idxf, ix[:, :, 0:4].bitcast(U32))
                V.drain()
                V.tensor_tensor(oh, v(CO["iota_e"], NE).unsqueeze(1).to_broadcast([P, 16, NE]),
                                v(R + 208, 16).unsqueeze(2).to_broadcast([P, 16, NE]), ALU.is_equal)
                V.drain()
                oh4 = v3(R + 256, TT, 4, NE)
                V.tensor_reduce(M, oh4.rearrange("p t k e -> p t e k"), AX.X, ALU.add)
                V.drain().then_inc(SEM["sel_rdy"], 1)
                dve.wait_ge(SEM["top_exp"], up(1))
                V.tensor_reduce(v(R + 1792, 4), e4, AX.X, ALU.add)
                V.drain()
                V.reciprocal(v(R + 1792, 4), v(R + 1792, 4))
                V.drain()
                V.tensor_tensor(gates, e4, v(R + 1792, 4).unsqueeze(2).to_broadcast([P, TT, 4]), ALU.mult)
                V.drain()
                V.tensor_tensor(tmp, oh, v(GATES, 16).unsqueeze(2).to_broadcast([P, 16, NE]), ALU.mult)
                V.drain()
                V.tensor_reduce(Gm, v3(R + 896, TT, 4, NE).rearrange("p t k e -> p t e k"), AX.X, ALU.add)
                V.drain().then_inc(SEM["gmat_rdy"], 1)
                dve.wait_ge(SEM["pos_mm"], up(1))
                V.tensor_tensor(posd, PS[:, 1, 0:TT * NE].rearrange("p (t e) -> p t e", t=TT),
                                v(CO["iota_list"], NE).unsqueeze(1).to_broadcast([P, TT, NE]), ALU.add)
                V.drain()
                for tt in range(TT):
                    V.tensor_tensor(tmp[:, 4 * tt:4 * tt + 4], oh[:, 4 * tt:4 * tt + 4],
                                    posd[:, tt].unsqueeze(1).to_broadcast([P, 4, NE]), ALU.mult)
                V.drain()
                V.tensor_reduce(addrf, tmp, AX.X, ALU.add)
                V.drain()
                V.tensor_copy(addr, addrf)
                V.drain().then_inc(SEM["addr_rdy"], 1)
                J = MAXBLK + 1
                cnt, nb, cum = v(TAB, NE, 1), v(TAB + 32, NE, 1), v(TAB + 64, NE, 1)
                t1 = v(TAB + 96, 4 * NE, 1).rearrange("p (e b) -> p e b", e=NE)
                V.tensor_copy(cnt, PS[0:1, 2, 0:NE])
                V.drain()
                V.tensor_tensor(t1, cnt.unsqueeze(2).to_broadcast([1, NE, 4]),
                                v(CO["steps"], 4, 1).unsqueeze(1).to_broadcast([1, NE, 4]), ALU.is_gt)
                V.drain()
                V.tensor_reduce(nb, t1, AX.X, ALU.add)
                V.drain()
                V.tensor_tensor_scan(cum, v(CO["ones"], NE, 1), nb, 0.0, ALU.mult, ALU.add)
                V.drain()
                cmp_ = AR[0:1, HT:HT + J * NE].rearrange("p (j e) -> p j e", j=J)
                cm2 = AR[0:1, HT + 2048:HT + 2048 + J * NE].rearrange("p (j e) -> p j e", j=J)
                V.tensor_tensor(cmp_, cum.unsqueeze(1).to_broadcast([1, J, NE]),
                                v(CO["iota_j"], J, 1).unsqueeze(2).to_broadcast([1, J, NE]), ALU.is_le)
                V.drain()
                V.tensor_tensor(cm2, cmp_, nb.unsqueeze(1).to_broadcast([1, J, NE]), ALU.mult)
                bef, stf, of = v(TAB + 256, J, 1), v(TAB + 320, J, 1), v(TAB + 384, J, 1)
                V.tensor_reduce(bef, cmp_, AX.X, ALU.add)
                V.drain()
                V.tensor_reduce(stf, cm2, AX.X, ALU.add)
                V.drain()
                V.tensor_tensor(stf, v(CO["iota_j"], J, 1), stf, ALU.subtract)
                step, left = v(TAB + 448, NE, 1), v(TAB + 512, J, 1)
                V.memset(step[:, NE - 1:NE], 0.0)
                V.tensor_tensor(step[:, 0:NE - 1], cnt[:, 1:NE], cnt[:, 0:NE - 1], ALU.subtract)
                V.drain()
                V.tensor_tensor(cm2, cmp_, step.unsqueeze(1).to_broadcast([1, J, NE]), ALU.mult)
                V.drain()
                V.tensor_reduce(left, cm2, AX.X, ALU.add)
                V.drain()
                V.tensor_scalar(left, left, cnt[:, 0:1], None, ALU.add)
                V.drain()
                V.scalar_tensor_tensor(left, stf, -float(P), left, ALU.mult, ALU.add)
                V.drain()
                V.tensor_scalar(left, left, float(P // 2), None, ALU.is_le)
                V.drain()
                V.tensor_copy(v(FEW, J, 1).bitcast(I32), left)
                V.tensor_scalar(stf, stf, float(P), None, ALU.mult)
                V.drain()
                V.scalar_tensor_tensor(of, bef, float(NPOS), stf, ALU.mult, ALU.add)
                V.tensor_scalar(bef, bef, float(NE - 1), None, ALU.min)
                V.drain()
                V.tensor_copy(v(BE, J, 1).bitcast(I32), bef)
                V.tensor_copy(v(BOFF, J, 1).bitcast(I32), of)
                V.tensor_copy(v(NBLK, 1, 1).bitcast(I32), cum[:, NE - 1:NE])
                V.drain().then_inc(SEM["table_rdy"], 1)

            def pool_(pool, c):
                pool.wait_ge(SEM["addr_rdy"], up(1))
                pool.wait_ge(SEM["list_in"], 16)
                for a_ in range(16):
                    G.indirect_dma_start(out=LIST, out_offset=bass.IndirectOffsetOnAxis(ap=addr.bitcast(U32)[:, a_:a_ + 1], axis=0),
                                         in_=v(RVAL, 16).bitcast(I32)[:, a_:a_ + 1], in_offset=None).then_inc(SEM["listed"], 16)
                pool.wait_ge(SEM["listed"], 16 * 16)
            return Stage({}, sp=sp_, pe=pe_, act=act_, dve=dve_, pool=pool_)

        XG, XT, AT_, Y_, GS_, US_, SG_ = HT, HT + 1024, HT + 2048, W, W + 1024, W + 1536, W + 2048
        IDXL, RSC, TOK, BCUR = W + 2560, W + 2561, W + 2562, W + 2564
        ch = [v2(BIG + 4096 * q, 8, 512) for q in range(4)] + [v2(BIG + 4096 * q, 4, D) for q in (4, 5)]

        def expert_stage():
            xg, y = v(XG, D), v(Y_, D)
            xT = v2(XT, 8, P)
            aT = v2(AT_, 8, P)
            idxl, rsc, tok = (v(o, 1).bitcast(I32) for o in (IDXL, RSC, TOK))
            J = MAXBLK + 1
            HB = P // 2

            def nblocks(eng):
                return eng.value_load(v(NBLK, 1, 1).bitcast(I32), min_val=1, max_val=MAXBLK)

            def entry(eng, at, j, hi):
                return eng.value_load(AR[0:1, bass.ds(j + at, 1)].bitcast(I32), min_val=0, max_val=hi)

            def sp_(sp, c):
                sp.wait_ge(SEM["table_rdy"], up(1))
                sp.wait_ge(SEM["listed"], 16 * 16)
                sp_after(sp, c)
                nb = nblocks(sp)
                o0 = entry(sp, BOFF, 0, NE * NPOS)
                sp.dma_start(idxl, LIST[bass.ds(o0, P), :]).then_inc(SEM["rows_in"], 16)
                with sp.Fori(0, nb) as j:
                    e = entry(sp, BE, j, NE - 1)
                    gu = A["w_gate_up"][bass.ds(e, 1)].rearrange("o (k p) f -> p (o k) f", p=P)
                    dn = A["w_down"][bass.ds(e, 1)].rearrange("o (f p) d -> p (o f) d", p=P)
                    srcs = [gu[:, :, 0:512], gu[:, :, 1024:1536], gu[:, :, 512:1024], gu[:, :, 1536:2048],
                            dn[:, 0:4], dn[:, 4:8]]
                    for q in range(6):
                        sp.wait_ge(SEM["ch_free"], up(6 * j + q + 1))
                        apart(sp, 6 * j + q + 1)
                        sp.dma_start(ch[q], srcs[q]).then_inc(SEM[f"ch{q}"], 16)

            def pe_(pe, c):
                pe.wait_ge(SEM["table_rdy"], up(1))
                nb = nblocks(pe)
                for _ in range(6):
                    PE.nop().then_inc(SEM["ch_free"], 1)

                def gather_T(n):
                    pe.wait_ge(SEM["gathered"], 16 * n)
                    apart(pe, 16 * n)
                    for q in range(8):
                        last = PE.transpose(PS[:, 4 + q // 4, (q % 4) * P:(q % 4 + 1) * P], xg[:, q * P:(q + 1) * P], ident)
                    last.then_inc(SEM["xt"], 1)
                gather_T(1)
                with pe.Fori(0, nb) as j:
                    pe.wait_ge(SEM["xt_free"], up(j + 1))
                    apart(pe, j + 1)
                    for q in range(4):
                        pe.wait_ge(SEM[f"ch{q}"], 16 * j + 16)
                        apart(pe, 16 * j + 16)
                        for f in range(4):
                            for k in range(8):
                                last = PE.matmul(PS[:, q, f * P:(f + 1) * P], ch[q][:, k, f * P:(f + 1) * P],
                                                 xT[:, k], start=(k == 0), stop=(k == 7))
                        last.then_inc(SEM["ch_free"], 1)
                    gather_T(j + 2)
                    pe.wait_ge(SEM["y_rdy"], up(j))
                    apart(pe, j)
                    few = entry(pe, FEW, j, 1)

                    def down(place):
                        for f in range(8):
                            if f % 4 == 0:
                                pe.wait_ge(SEM[f"ch{4 + f // 4}"], 16 * j + 16)
                                apart(pe, 16 * j + 16)
                                pe.wait_ge(SEM["act_rdy"], up(2 * j + 1 + f // 4))
                                apart(pe, 2 * j + 1 + f // 4)
                            for n in range(2):
                                to, tokens = place(n)
                                last = PE.matmul(to, aT[:, f, 0:tokens], ch[4 + f // 4][:, f % 4, n * 512:(n + 1) * 512],
                                                 start=(f == 0), stop=(f == 7))
                            if f % 4 == 3:
                                last.then_inc(SEM["ch_free"], 1)
                    with pe.If(few > 0):
                        down(lambda n: (PS[HB * n:HB * (n + 1), 6 + n], HB))
                    with pe.Else():
                        down(lambda n: (PS[:, 6 + n], P))

            def act_(act, c):
                act.wait_ge(SEM["table_rdy"], up(1))
                nb = nblocks(act)

                def copy_T(n):
                    act.wait_ge(SEM["xt"], up(n))
                    apart(act, n)
                    AC.activation(v(XT, D), PS[:, 4:6].rearrange("p a b -> p (a b)"), ACT.Copy).then_inc(SEM["xt_free"], 1)
                copy_T(1)
                with act.Fori(0, nb) as j:
                    o1 = entry(act, BOFF, j + 1, NE * NPOS)
                    act.wait_ge(SEM["rsc_rdy"], up(j + 1))
                    apart(act, j + 1)
                    act.dma_start(idxl, LIST[bass.ds(o1, P), :]).then_inc(SEM["rows_in"], 16)
                    for h in range(2):
                        act.wait_ge(SEM["act_g"], up(2 * j + h + 1))
                        apart(act, 2 * j + h + 1)
                        AC.activation(v(SG_, 512), v(GS_, 512), ACT.Sigmoid, scale=ALPHA).then_inc(SEM["sig_g"], 1)
                    copy_T(j + 2)
                    act.wait_ge(SEM["ch_free"], up(6 * j + 12))
                    apart(act, 6 * j + 12)
                    act.wait_ge(SEM["rows_out"], up(j))
                    apart(act, j)
                    few = entry(act, FEW, j, 1)
                    with act.If(few > 0):
                        AC.activation(v(Y_, 512, HB), PS[0:HB, 6], ACT.Copy)
                        AC.activation(v(Y_ + 512, 512, HB), PS[HB:P, 7], ACT.Copy).then_inc(SEM["y_rdy"], 1)
                    with act.Else():
                        AC.activation(y, PS[:, 6:8].rearrange("p a b -> p (a b)"), ACT.Copy).then_inc(SEM["y_rdy"], 1)

            def dve_(dve, c):
                nb = nblocks(dve)
                dve.wait_ge(SEM["rows_in"], 16)
                V.tensor_scalar(tok, idxl, 2, None, ALU.logical_shift_right).then_inc(SEM["tok_rdy"], 1)
                with dve.Fori(0, nb) as j:
                    e = entry(dve, BE, j, NE - 1)
                    dve.wait_ge(SEM["rows_out"], up(j))
                    apart(dve, j)
                    V.tensor_copy(rsc, idxl)
                    V.tensor_copy(v(BCUR, 16), dyn(BT + e * 16, 16))
                    V.drain().then_inc(SEM["rsc_rdy"], 1)
                    dve.wait_ge(SEM["rows_in"], 16 * j + 32)
                    apart(dve, 16 * j + 32)
                    dve.wait_ge(SEM["gathered"], 16 * j + 16)
                    apart(dve, 16 * j + 16)
                    V.tensor_scalar(tok, idxl, 2, None, ALU.logical_shift_right).then_inc(SEM["tok_rdy"], 1)
                    for h in range(2):
                        g, u, s_ = v2(GS_, 4, P), v2(US_, 4, P), v2(SG_, 4, P)

                        def bias(o):
                            return v(BCUR + o + 4 * h, 4).unsqueeze(2).to_broadcast([P, 4, P])
                        dve.wait_ge(SEM["ch_free"], up(6 * j + 6 + 2 * h + 1))
                        apart(dve, 6 * j + 6 + 2 * h + 1)
                        V.tensor_tensor(g, PS[:, 2 * h].rearrange("p (f t) -> p f t", f=4), bias(0), ALU.add)
                        V.drain()
                        V.tensor_scalar(g, g, LIMIT, None, ALU.min).then_inc(SEM["act_g"], 1)
                        dve.wait_ge(SEM["ch_free"], up(6 * j + 6 + 2 * h + 2))
                        apart(dve, 6 * j + 6 + 2 * h + 2)
                        V.tensor_tensor(u, PS[:, 2 * h + 1].rearrange("p (f t) -> p f t", f=4), bias(8), ALU.add)
                        V.drain()
                        V.tensor_scalar(u, u, LIMIT, -LIMIT, ALU.min, ALU.max)
                        V.drain()
                        V.scalar_tensor_tensor(v(US_, 512), v(US_, 512), 1.0, v(GS_, 512), ALU.add, ALU.mult)
                        V.drain()
                        dve.wait_ge(SEM["sig_g"], up(2 * j + h + 1))
                        apart(dve, 2 * j + h + 1)
                        V.tensor_tensor(v(AT_ + 512 * h, 512), v(US_, 512), v(SG_, 512), ALU.mult)
                        V.drain().then_inc(SEM["act_rdy"], 1)

            def pool_(pool, c):
                G.memset(xg, 0.0)
                G.memset(y, 0.0)
                G.drain()
                pool.wait_ge(SEM["table_rdy"], up(1))
                pool.wait_ge(SEM["h2_out"], 16)
                nb = nblocks(pool)

                def gather(n):
                    pool.wait_ge(SEM["tok_rdy"], up(n))
                    apart(pool, n)
                    G.indirect_dma_start(out=xg, out_offset=None, in_=H2D,
                                         in_offset=bass.IndirectOffsetOnAxis(ap=tok.bitcast(U32), axis=0),
                                         bounds_check=S - 1, oob_is_err=False).then_inc(SEM["gathered"], 16)
                gather(1)
                with pool.Fori(0, nb) as j:
                    pool.wait_ge(SEM["xt"], up(j + 1))
                    apart(pool, j + 1)
                    gather(j + 2)
                    pool.wait_ge(SEM["y_rdy"], up(j + 1))
                    apart(pool, j + 1)
                    G.indirect_dma_start(out=YD, out_offset=bass.IndirectOffsetOnAxis(ap=rsc.bitcast(U32), axis=0),
                                         in_=y, in_offset=None,
                                         bounds_check=S * TOPK - 1, oob_is_err=False).then_inc(SEM["scattered"], 16)
                    pool.wait_ge(SEM["scattered"], 16 * j + 16)
                    apart(pool, 16 * j + 16)
                    pool.sem_inc(SEM["rows_out"])
                pool.wait_ge(SEM["gathered"], nb * 16 + 16)
                apart(pool, nb * 16 + 16)
            return Stage({}, sp=sp_, pe=pe_, act=act_, dve=dve_, pool=pool_)

        def combine_stage():
            BD = W

            def sp_(sp, c):
                sp_after(sp, c)
                sp.dma_start(v(BD, D, NE), A["b_down"]).then_inc(SEM["bdown_in"], 16)
                for tt in range(TT):
                    sp.dma_start(v(BIG + 4096 * tt, 4096),
                                 YD[tt * 512:(tt + 1) * 512, :].rearrange("(p k) d -> p (k d)", k=4)).then_inc(
                                     SEM[f"comb{tt}"], 16)

            def pe_(pe, c):
                pe.wait_ge(SEM["bdown_in"], 16)
                for tt in range(TT):
                    for n in range(2):
                        last = PE.matmul(PS[:, 2 * tt + n], v(GT + tt * P, P, NE), v(BD + n * 512, 512, NE),
                                         start=True, stop=True)
                last.then_inc(SEM["fin_mm"], 1)

            def dve_(dve, c):
                dve.wait_ge(SEM["fin_mm"], up(1))
                for tt in range(TT):
                    V.tensor_tensor(x3[:, tt], x3[:, tt], PS[:, 2 * tt:2 * tt + 2].rearrange("p a b -> p (a b)"), ALU.add)
                V.drain()
                for tt in range(TT):
                    dve.wait_ge(SEM[f"comb{tt}"], 16)
                    for k in range(4):
                        V.scalar_tensor_tensor(x3[:, tt], v(BIG + 4096 * tt + D * k, D), v(GATES + 4 * tt + k, 1),
                                               x3[:, tt], ALU.mult, ALU.add)
                        V.drain()
            return Stage({}, sp=sp_, pe=pe_, dve=dve_)

        def output_stage():
            def sp_(sp, c):
                sp_after(sp, c)
                sp.dma_start(out.rearrange("b (t p) d -> p (b t) d", p=P), x3).then_inc(SEM["x_out"], 16)
                sp.wait_ge(SEM["x_out"], 16)
            return Stage({}, sp=sp_)

        YA, YB, YC = BIG, BIG + 2048, BIG + 4096

        def wl(name):
            return lambda c: A[name][bass.ds(c.of("layer"), 1)].rearrange("o a b -> (o a) b")

        w2 = wl("w_in_2")

        def dense_hT(k0, cols, across=()):
            def sp_(sp, c):
                for k, (c0, n) in enumerate(cols):
                    dense_sp(sp, c, k0 + k, lambda h: rows(w2(c), 8, h, c0, n))

            def pe_(pe, c):
                for k, (c0, n) in enumerate(cols):
                    dense_pe(pe, c, k0 + k, lambda kk, tt: hT[:, kk, tt * P:(tt + 1) * P], 8, n,
                             moving=(lambda kk: hT[:, kk]) if k in across else None)
            return sp_, pe_

        def sgu_stage():
            U, Vv, Z, WS, SCR, ROW = (LB + o for o in (0, 2048, 4096, 6144, 7168, 9216))
            sp0, pe0 = dense_hT(0, [(0, 512), (512, 512), (1024, 512)])
            st = v(SM, 16)

            def sp_(sp, c):
                sp_after(sp, c)
                l = c.of("layer")
                sp.dma_start(v2(WS, 8, P), A["sgu_w_T"][bass.ds(l, 1)].rearrange("o s g t -> s (o g) t")).then_inc(SEM["ws_in"], 16)
                sp.dma_start(v(ROW, 1024), A["sgu_ln"][bass.ds(l, 1)].rearrange("o w -> (o w)").partition_broadcast(P)).then_inc(SEM["ws_in"], 16)
                sp.dma_start(v(SM + 32, 8), A["sgu_b_T"][bass.ds(l, 1)].rearrange("o t g -> t (o g)")).then_inc(SEM["ws_in"], 16)
                sp0(sp, c)

            def pe_(pe, c):
                pe0(pe, c)
                pe.wait_ge(SEM["ws_rdy"], up(2 * c.of("layer") + 2))
                apart(pe, 2 * c.of("layer") + 2)
                for g in range(8):
                    last = PE.matmul(PS[:, 4 + g // 2, (g % 2) * 256:(g % 2 + 1) * 256], v2(WS, 8, P)[:, g],
                                     v3(Vv, TT, 8, E)[:, :, g], start=True, stop=True)
                last.then_inc(SEM["sgu_mm"], 1)

            def act_(act, c):
                for tt in range(TT):
                    act.wait_ge(SEM["mm"], up(unit(c, 0, tt)))
                    apart(act, unit(c, 0, tt))
                    AC.activation(v(U + 512 * tt, 512), PS[:, tt], ACT.Copy).then_inc(SEM["ev"], 1)
                for tt in range(TT):
                    act.wait_ge(SEM["mm"], up(unit(c, 1, tt)))
                    apart(act, unit(c, 1, tt))
                    AC.activation(v(Vv + 512 * tt, 512), PS[:, tt], ACT.Copy, accum_out=st[:, tt:tt + 1]).then_inc(SEM["ev"], 1)
                act.wait_ge(SEM["sgu_in"], up(2 * c.of("layer") + 1))
                apart(act, 2 * c.of("layer") + 1)
                for tt in range(TT):
                    last = AC.activation(v(SCR + 512 * tt, 512), v(Vv + 512 * tt, 512), ACT.Square, accum_out=st[:, 4 + tt:5 + tt])
                last.then_inc(SEM["ln_sd"], 1)
                act.wait_ge(SEM["sgu_in"], up(2 * c.of("layer") + 2))
                apart(act, 2 * c.of("layer") + 2)
                AC.activation(st[:, 4:8], st[:, 4:8], ACT.Sqrt).then_inc(SEM["ln_sd"], 1)
                for tt in range(TT):
                    act.wait_ge(SEM["mm"], up(unit(c, 2, tt)))
                    apart(act, unit(c, 2, tt))
                    AC.activation(v(Z + 512 * tt, 512), PS[:, tt], ACT.Copy)
                    AC.activation(v(YA + 512 * tt, 512), PS[:, tt], ACT.Sigmoid).then_inc(SEM["ev"], 1)

            def dve_(dve, c):
                layer = c.of("layer")
                v3d = v2(Vv, TT, 512)
                dve.wait_ge(SEM["ws_in"], 48 * layer + 48)
                apart(dve, 48 * layer + 48)
                V.tensor_tensor(v2(WS, 8, P), v2(WS, 8, P), v(CO["tril_T"], P).unsqueeze(1).to_broadcast([P, 8, P]),
                                ALU.mult).then_inc(SEM["ws_rdy"], 1)
                dve.wait_ge(SEM["ev"], up(unit(c, 1, 3)))
                apart(dve, unit(c, 1, 3))
                V.tensor_scalar(st[:, 0:4], st[:, 0:4], -1.0 / 512, None, ALU.mult)
                V.drain()
                for tt in range(TT):
                    last = V.tensor_scalar(v3d[:, tt], v3d[:, tt], st[:, tt:tt + 1], None, ALU.add)
                last.then_inc(SEM["sgu_in"], 1)
                dve.wait_ge(SEM["ln_sd"], up(2 * layer + 1))
                apart(dve, 2 * layer + 1)
                V.tensor_scalar(st[:, 4:8], st[:, 4:8], 1.0 / 512, EPS, ALU.mult, ALU.add).then_inc(SEM["sgu_in"], 1)
                dve.wait_ge(SEM["ln_sd"], up(2 * layer + 2))
                apart(dve, 2 * layer + 2)
                V.reciprocal(st[:, 4:8], st[:, 4:8])
                V.drain()
                for tt in range(TT):
                    V.scalar_tensor_tensor(v3d[:, tt], v3d[:, tt], st[:, 4 + tt:5 + tt], v(ROW, 512), ALU.mult, ALU.mult)
                V.drain()
                V.tensor_tensor(v3d, v3d, v(ROW + 512, 512).unsqueeze(1).to_broadcast([P, TT, 512]), ALU.add)
                V.drain().then_inc(SEM["ws_rdy"], 1)
                dve.wait_ge(SEM["ev"], up(unit(c, 2, 3)))
                apart(dve, unit(c, 2, 3))
                V.tensor_tensor(v(YA, 2048), v(YA, 2048), v(Z, 2048), ALU.mult)
                V.drain()
                V.tensor_tensor(v(YA, 2048), v(YA, 2048), v(U, 2048), ALU.mult)
                dve.wait_ge(SEM["sgu_mm"], up(layer + 1))
                apart(dve, layer + 1)
                for q in range(4):
                    V.tensor_tensor(v(SCR + 512 * q, 512).rearrange("p (g x) -> p g x", g=2),
                                    PS[:, 4 + q].rearrange("p (g x) -> p g x", g=2),
                                    v(SM + 32 + 2 * q, 2).unsqueeze(2).to_broadcast([P, 2, 256]), ALU.add)
                V.drain()
                for tt in range(TT):
                    ya = v(YA + 512 * tt, 512).rearrange("p (g c) -> p g c", g=8)
                    V.tensor_tensor(ya, ya, v3(SCR, 8, TT, E)[:, :, tt], ALU.mult)
            return Stage({"T": 3}, sp=sp_, pe=pe_, act=act_, dve=dve_)

        QM, KV, DN, CQT, CKVT, LROW, MQT, MKT = (LB + o for o in (0, 3072, 8192, 9856, 10880, 11392, 11776, 15872))

        def latent_stages():
            sp0, pe0 = dense_hT(0, [(1536, 416), (1952, 512)], across=(1,))
            st = v(SM, 8)
            dn = v2(DN, TT, 416)

            def sp_(sp, c):
                sp_after(sp, c)
                sp.dma_start(v(LROW, 384), A["mla_norms"][bass.ds(c.of("layer"), 1)].rearrange("o w -> (o w)").partition_broadcast(P)).then_inc(
                    SEM["bdown_in"], 16)
                sp0(sp, c)

            def act_(act, c):
                layer = c.of("layer")
                for tt in range(TT):
                    act.wait_ge(SEM["mm"], up(unit(c, 0, tt)))
                    apart(act, unit(c, 0, tt))
                    AC.activation(v(PTS + 384 * tt, 256), PS[:, tt, 0:256], ACT.Square, accum_out=st[:, tt:tt + 1])
                    AC.activation(v(PTS + 384 * tt + 256, 128), PS[:, tt, 256:384], ACT.Square, accum_out=st[:, 4 + tt:5 + tt])
                    AC.activation(dn[:, tt], PS[:, tt, 0:416], ACT.Copy).then_inc(SEM["ev"], 1)
                act.wait_ge(SEM["lat_ms"], up(layer + 1))
                apart(act, layer + 1)
                AC.activation(st, st, ACT.Sqrt).then_inc(SEM["lat_sd"], 1)
                for tt in range(TT):
                    act.wait_ge(SEM["mm"], up(unit(c, 1, tt)))
                    apart(act, unit(c, 1, tt))
                    AC.activation(v(SC + 512 * tt, 512), PS[:, tt], ACT.Copy)
                    AC.activation(v(YB + 512 * tt, 512), PS[:, tt], ACT.Sigmoid).then_inc(SEM["ev"], 1)
                for tt in range(TT):
                    act.wait_ge(SEM["tr"], up(c.of("tr") + tt + 1))
                    apart(act, c.of("tr") + tt + 1)
                    AC.activation(v2(CQT, 2, S)[:, :, tt * P:(tt + 1) * P],
                                  PS[:, 4 + tt, 0:256].rearrange("p (a t) -> p a t", a=2), ACT.Copy)
                    AC.activation(v(CKVT + tt * P, P), PS[:, 4 + tt, 256:384], ACT.Copy).then_inc(SEM["tr_free"], 1)

            def dve_(dve, c):
                layer = c.of("layer")
                dve.wait_ge(SEM["ev"], up(unit(c, 0, 3)))
                apart(dve, unit(c, 0, 3))
                V.tensor_scalar(st[:, 0:4], st[:, 0:4], 1.0 / 256, EPS, ALU.mult, ALU.add)
                V.tensor_scalar(st[:, 4:8], st[:, 4:8], 1.0 / 128, EPS, ALU.mult, ALU.add)
                V.drain().then_inc(SEM["lat_ms"], 1)
                dve.wait_ge(SEM["lat_sd"], up(layer + 1))
                apart(dve, layer + 1)
                V.reciprocal(st, st)
                V.drain()
                dve.wait_ge(SEM["bdown_in"], 16 * layer + 32)
                apart(dve, 16 * layer + 32)
                for tt in range(TT):
                    V.scalar_tensor_tensor(dn[:, tt, 0:256], dn[:, tt, 0:256], st[:, tt:tt + 1], v(LROW, 256), ALU.mult, ALU.mult)
                    V.scalar_tensor_tensor(dn[:, tt, 256:384], dn[:, tt, 256:384], st[:, 4 + tt:5 + tt], v(LROW + 256, 128),
                                           ALU.mult, ALU.mult)
                    V.drain().then_inc(SEM["lat_rdy"], 1)
                for tt in range(TT):
                    src = dn[:, tt, 384:416].unsqueeze(1)
                    rotate(v(SM + 64 + 32 * tt, 32).unsqueeze(1), src, v(CO["ropeM_c"] + 32 * tt, 32),
                           v(CO["ropeM_s"] + 32 * tt, 32), 1, 1, 16)
                    V.drain()
                    V.tensor_copy(v3(KV, TT, 8, 160)[:, tt, :, 0:32],
                                  v(SM + 64 + 32 * tt, 32).unsqueeze(1).to_broadcast([P, 8, 32]))
                dve.wait_ge(SEM["ev"], up(unit(c, 1, 3)))
                apart(dve, unit(c, 1, 3))
                V.tensor_tensor(v(YB, 2048), v(YB, 2048), v(SC, 2048), ALU.mult)

            def pe_(pe, c):
                pe0(pe, c)
                for tt in range(TT):
                    pe.wait_ge(SEM["lat_rdy"], up(4 * c.of("layer") + tt + 1))
                    apart(pe, 4 * c.of("layer") + tt + 1)
                    tr_pe(pe, c, tt, [dn[:, tt, a * P:(a + 1) * P] for a in range(3)])
            latents = Stage({"T": 2, "tr": 4}, sp=sp_, act=act_, dve=dve_, pe=pe_)

            uq, ukv = wl("mla_w_uq_2"), wl("mla_w_ukv_2")

            def sp2(sp, c):
                for n in range(2):
                    dense_sp(sp, c, n, lambda h: rows(uq(c), 2, h, n * 384, 384))
                for n in range(2):
                    dense_sp(sp, c, 2 + n, lambda h: (Wh[h][:, 0, 0:256], ukv(c)[:, n * 512 + h * 256:n * 512 + h * 256 + 256]))

            def pe2(pe, c):
                for n in range(2):
                    dense_pe(pe, c, n, lambda kk, tt: v2(CQT, 2, S)[:, kk, tt * P:(tt + 1) * P], 2, 384)
                for n in range(2):
                    dense_pe(pe, c, 2 + n, lambda kk, tt: v(CKVT + tt * P, P), 1, 512)

            def act2(act, c):
                for n in range(2):
                    for tt in range(TT):
                        act.wait_ge(SEM["mm"], up(unit(c, n, tt)))
                        apart(act, unit(c, n, tt))
                        src = PS[:, tt, 0:384].rearrange("p (h e) -> p h e", h=4)
                        dst = v3(QM, TT, 8, 96)[:, tt, 4 * n:4 * n + 4]
                        AC.activation(dst[:, :, 0:32], src[:, :, 64:96], ACT.Copy)
                        AC.activation(dst[:, :, 32:96], src[:, :, 0:64], ACT.Copy).then_inc(SEM["ev"], 1)
                for n in range(2):
                    for tt in range(TT):
                        act.wait_ge(SEM["mm"], up(unit(c, 2 + n, tt)))
                        apart(act, unit(c, 2 + n, tt))
                        AC.activation(v3(KV, TT, 8, 160)[:, tt, 4 * n:4 * n + 4, 32:160],
                                      PS[:, tt].rearrange("p (h e) -> p h e", h=4), ACT.Copy).then_inc(SEM["ev"], 1)

            def dve2(dve, c):
                dve.wait_ge(SEM["ev"], up(unit(c, 1, 3)))
                apart(dve, unit(c, 1, 3))
                for tt in range(TT):
                    q = v3(QM, TT, 8, 96)[:, tt, :, 0:32]
                    rotate(q, q, v(CO["ropeM_c"] + 32 * tt, 32), v(CO["ropeM_s"] + 32 * tt, 32), 8, 1, 16)
                    V.drain()
            raised = Stage({"T": 4}, sp=sp2, pe=pe2, act=act2, dve=dve2)

            def heads():
                k = 0
                for src, dst in ((v3(QM, TT, 8, 96), MQT), (v3(KV, TT, 8, 160), MKT)):
                    for tt in range(TT):
                        for hq in range(2):
                            yield k, tt, hq, src, dst
                            k += 1

            def pe3(pe, c):
                for k, tt, hq, src, dst in heads():
                    tr_pe(pe, c, k, [src[:, tt, 4 * hq + a, 0:96] for a in range(4)])

            def copy3(who, par):
                def run(eng, c):
                    for k, tt, hq, src, dst in heads():
                        if k % 2 == par:
                            eng.wait_ge(SEM["tr_free"], up(c.of("tr") + k))
                            apart(eng, c.of("tr") + k)
                            tr_out(eng, who, c, k, v2(dst, 8, S, 96)[:, 4 * hq:4 * hq + 4, tt * P:(tt + 1) * P], 4, 96)
                return run
            turned = Stage({"tr": 16}, pe=pe3, act=copy3("act", 0), dve=copy3("dve", 1))

            def W_(i):
                return P * (i + 1)

            def finish(p, s, ps):
                o = dyn(YB + p * 512, S, E, E * s)
                return V.tensor_tensor(o, ps, o, ALU.mult)
            return latents, raised, turned, attention({"groups": 1, "pairs": 4, "scale": MLA_SCALE, "W": W_,
                       "stage": lambda pool, c, p, s: G.tensor_copy(v(QST + 512 * s, S, 96), dyn(MQT + s * 512 + p * 1024, S, 96)),
                       "scores": lambda p, s, i: [(v(QST + 512 * s + i * P, P, 96), dyn(MKT + s * 512 + p * 1024, W_(i), 96), 0, W_(i))],
                       "values": lambda p, s: bring_tiles(VST[s], KV + s * 160 + 96 + p * 320, 1280),
                       "tiles": lambda i: list(range(i + 1)),
                       "finish": finish,
                       "mask": lambda s, i: v(CO["chunk_mask"] + S - W_(i), W_(i))})

        CQK, CV = LB, LB + 4096

        def chunk_stages():
            c0s = 1952 + 512
            sp0, pe_ = dense_hT(0, [(c0s, 512), (c0s + 512, 512), (c0s + 1024, 512), (c0s + 1536, 512)],
                                across=(0, 1, 3))

            def sp_(sp, c):
                sp_after(sp, c)
                sp0(sp, c)

            def act_(act, c):
                for k in range(4):
                    for tt in range(TT):
                        act.wait_ge(SEM["mm"], up(unit(c, k, tt)))
                        apart(act, unit(c, k, tt))
                        if k < 3:
                            o = CQK + k * 2048 + tt * 512 if k < 2 else CV + tt * 512
                            AC.activation(v(o, 512), PS[:, tt], ACT.Copy).then_inc(SEM["ev"], 1)
                        else:
                            AC.activation(v(SC + 512 * tt, 512), PS[:, tt], ACT.Copy)
                            AC.activation(v(YC + 512 * tt, 512), PS[:, tt], ACT.Sigmoid).then_inc(SEM["ev"], 1)

            def dve_(dve, c):
                dve.wait_ge(SEM["ev"], up(unit(c, 3, 3)))
                apart(dve, unit(c, 3, 3))
                V.tensor_tensor(v(YC, 2048), v(YC, 2048), v(SC, 2048), ALU.mult)
            heads = Stage({"T": 4}, sp=sp_, pe=pe_, act=act_, dve=dve_)

            def W_(i):
                return P * (i + 1)

            BH = QST + 512

            def raw(s):
                return v(SC + 2048 + 256 * s, 256)

            def stage_(pool, c, p, s):
                pool.wait_ge(SEM[f"bias_rows{s}"], 16 * c.of("bias") + 16)
                apart(pool, 16 * c.of("bias") + 16)
                b = BH + 512 * s
                G.tensor_scalar(v(b + 256, 256), raw(s), 1.0 / ATT_SCALE, None, ALU.mult)
                G.tensor_scalar(v(b, 256), raw(s)[:, 0:1].to_broadcast([P, 256]), 1.0 / ATT_SCALE, None, ALU.mult)
                G.drain()
                G.memset(v(b + 448, 64, 64), NEG)
                G.drain()
                G.tensor_copy(kst(s, 0, S), dyn(CQK + 2048 + p * 512, S, E, E * s))
                return G.tensor_copy(qst(s, 0, S), dyn(CQK + p * 512, S, E, E * s))

            def spb(sp, c, p, s):
                src = A["rel_rows"][bass.ds(c.of("layer") * 8 + 2 * p + s, 1)].rearrange("o p w -> (o p) w")
                sp.dma_start(raw(s), src).then_inc(SEM[f"bias_rows{s}"], 16)

            def finish(p, s, ps):
                o = dyn(YC + p * 512, S, E, E * s)
                return V.tensor_tensor(o, ps, o, ALU.mult)
            return heads, attention({"groups": 1, "pairs": 4, "scale": ATT_SCALE, "W": W_, "stage": stage_, "sp": spb,
                       "scores": lambda p, s, i: [(v(QST + i * P, P, E, E * s), kst(s, 0, W_(i)), 0, W_(i))],
                       "values": lambda p, s: bring_tiles(VST[s], CV + s * E + p * P, 512),
                       "tiles": lambda i: list(range(i + 1)),
                       "finish": finish,
                       "mask": lambda s, i: v(BH + 512 * s + S - W_(i), W_(i))})

        def out_post_stage(mT, w_out, YO):
            products_sp, pe_ = out_products(mT, w_out)
            st = v(SM, 4)
            sq = v(SM + 8, 8)
            yo = v2(YO, TT, D)

            def sp_(sp, c):
                sp_after(sp, c)
                sp.dma_start(v(GROW, D), A["post_g_2"][bass.ds(c.of("layer"), 1)].rearrange("o w -> (o w)").partition_broadcast(P)).then_inc(
                    SEM["grow_in"], 16)
                products_sp(sp, c)

            def act_(act, c):
                for n in range(2):
                    for tt in range(TT):
                        act.wait_ge(SEM["mm"], up(unit(c, n, tt)))
                        apart(act, unit(c, n, tt))
                        AC.activation(yo[:, tt, n * 512:(n + 1) * 512], PS[:, tt], ACT.Copy)
                        AC.activation(v(YO + 4096 + 2048 * n + 512 * tt, 512), PS[:, tt], ACT.Square,
                                      accum_out=sq[:, 4 * n + tt:4 * n + tt + 1]).then_inc(SEM["ev"], 1)
                        if n == 1:
                            act.wait_ge(SEM["post_ms"], up(c.of("post_ms") + tt + 1))
                            apart(act, c.of("post_ms") + tt + 1)
                            AC.activation(st[:, tt:tt + 1], st[:, tt:tt + 1], ACT.Sqrt).then_inc(SEM["post_sd"], 1)

            def dve_(dve, c):
                dve.wait_ge(SEM["grow_in"], 16 * c.of("grow") + 16)
                apart(dve, 16 * c.of("grow") + 16)
                for tt in range(TT):
                    s_ = st[:, tt:tt + 1]
                    dve.wait_ge(SEM["ev"], up(unit(c, 1, tt)))
                    apart(dve, unit(c, 1, tt))
                    V.tensor_tensor(s_, sq[:, tt:tt + 1], sq[:, 4 + tt:5 + tt], ALU.add)
                    V.drain()
                    V.tensor_scalar(s_, s_, 1.0 / D, EPS, ALU.mult, ALU.add).then_inc(SEM["post_ms"], 1)
                    dve.wait_ge(SEM["post_sd"], up(c.of("post_sd") + tt + 1))
                    apart(dve, c.of("post_sd") + tt + 1)
                    V.reciprocal(s_, s_)
                    V.drain()
                    V.scalar_tensor_tensor(yo[:, tt], yo[:, tt], s_, v(GROW, D), ALU.mult, ALU.mult)
                    V.drain()
                    V.tensor_tensor(x3[:, tt], x3[:, tt], yo[:, tt], ALU.add)
            return Stage({"T": 2, "grow": 1, "post_ms": 4, "post_sd": 4}, sp=sp_, pe=pe_, act=act_, dve=dve_)

        load = constants()
        norm_mix = norm_stage(lambda c: A["norm_mix_g"], BIG)
        heads_1, values_1 = project_first()
        dilated, grouped = attention_first()
        merge_1, turn_merged_1, mT = merge_stage(
            BIG, 2, [v2(OA, 4, S), v2(OB, 4, S)], lambda c, b: A["w_proj_a"] if b == 0 else A["w_proj_b"],
            (lambda c: w_in, 5376), lambda c: A["b_gate"], BIG + 16384)
        out_1 = out_stage(mT, lambda c: A["w_out"])
        norm_ffn = norm_stage(lambda c: A["norm_ffn_g"], BIG, want_h2=True)
        route = router_stage()
        experts = expert_stage()
        combine = combine_stage()

        norm_pre = norm_stage(lambda c: A["pre_g_2"][bass.ds(c.of("layer"), 1)].rearrange("o w -> (o w)"), LB)
        gating = sgu_stage()
        latents, raised, turn_latent, latent_attention = latent_stages()
        heads_2, chunk_attention = chunk_stages()
        YT = [v2(LB, 4, S), v2(YB, 4, S), v2(YC, 4, S)]
        turn_2 = transpose_stage([(v2(YA, TT, 512), YT[0], 4)])
        merge_2, turn_merged_2, mT2 = merge_stage(
            LB, 3, YT, lambda c, b: A["w_branch_2"][bass.ds(c.of("layer"), 1)].rearrange("o n c d -> (o n) c d")[b],
            (w2, 4512), lambda c: A["gate_b_2"][bass.ds(c.of("layer"), 1)].rearrange("o w -> (o w)"), SC)
        out_2 = out_post_stage(mT2, wl("w_out_2"), LB)
        output = output_stage()

        per_layer = {"layer": 1}
        for st in (norm_pre, gating, latents, raised, turn_latent, latent_attention, heads_2,
                   chunk_attention, turn_2, merge_2, turn_merged_2, out_2):
            for k, n in st.counts.items():
                per_layer[k] = per_layer.get(k, 0) + n
            per_layer["fence"] = per_layer.get("fence", 0) + 1

        block = ctx.enter_context(nc.Block())

        @block.sync
        def _(sp):
            c = At()
            load.sp(sp, c)
            norm_mix.sp(sp, c)
            heads_1.sp(sp, c)
            values_1.sp(sp, c)
            dilated.sp(sp, c)
            grouped.sp(sp, c)
            merge_1.sp(sp, c)
            turn_merged_1.sp(sp, c)
            out_1.sp(sp, c)
            norm_ffn.sp(sp, c)
            route.sp(sp, c)
            experts.sp(sp, c)
            combine.sp(sp, c)
            with sp.Fori(0, 2) as layer:
                cl = c.inside(layer, per_layer)
                norm_pre.sp(sp, cl)
                gating.sp(sp, cl)
                latents.sp(sp, cl)
                raised.sp(sp, cl)
                turn_latent.sp(sp, cl)
                latent_attention.sp(sp, cl)
                heads_2.sp(sp, cl)
                chunk_attention.sp(sp, cl)
                turn_2.sp(sp, cl)
                merge_2.sp(sp, cl)
                turn_merged_2.sp(sp, cl)
                out_2.sp(sp, cl)
            c.step(per_layer, 2)
            output.sp(sp, c)

        @block.tensor
        def _(pe):
            c = At()
            load.pe(pe, c)
            norm_mix.pe(pe, c)
            heads_1.pe(pe, c)
            values_1.pe(pe, c)
            dilated.pe(pe, c)
            grouped.pe(pe, c)
            merge_1.pe(pe, c)
            turn_merged_1.pe(pe, c)
            out_1.pe(pe, c)
            norm_ffn.pe(pe, c)
            route.pe(pe, c)
            experts.pe(pe, c)
            combine.pe(pe, c)
            with pe.Fori(0, 2) as layer:
                cl = c.inside(layer, per_layer)
                norm_pre.pe(pe, cl)
                gating.pe(pe, cl)
                latents.pe(pe, cl)
                raised.pe(pe, cl)
                turn_latent.pe(pe, cl)
                latent_attention.pe(pe, cl)
                heads_2.pe(pe, cl)
                chunk_attention.pe(pe, cl)
                turn_2.pe(pe, cl)
                merge_2.pe(pe, cl)
                turn_merged_2.pe(pe, cl)
                out_2.pe(pe, cl)
            c.step(per_layer, 2)
            output.pe(pe, c)

        @block.scalar
        def _(act):
            c = At()
            load.act(act, c)
            norm_mix.act(act, c)
            heads_1.act(act, c)
            values_1.act(act, c)
            dilated.act(act, c)
            grouped.act(act, c)
            merge_1.act(act, c)
            turn_merged_1.act(act, c)
            out_1.act(act, c)
            norm_ffn.act(act, c)
            route.act(act, c)
            experts.act(act, c)
            combine.act(act, c)
            with act.Fori(0, 2) as layer:
                cl = c.inside(layer, per_layer)
                norm_pre.act(act, cl)
                gating.act(act, cl)
                latents.act(act, cl)
                raised.act(act, cl)
                turn_latent.act(act, cl)
                latent_attention.act(act, cl)
                heads_2.act(act, cl)
                chunk_attention.act(act, cl)
                turn_2.act(act, cl)
                merge_2.act(act, cl)
                turn_merged_2.act(act, cl)
                out_2.act(act, cl)
            c.step(per_layer, 2)
            output.act(act, c)

        @block.vector
        def _(dve):
            c = At()
            load.dve(dve, c)
            norm_mix.dve(dve, c)
            heads_1.dve(dve, c)
            values_1.dve(dve, c)
            dilated.dve(dve, c)
            grouped.dve(dve, c)
            merge_1.dve(dve, c)
            turn_merged_1.dve(dve, c)
            out_1.dve(dve, c)
            norm_ffn.dve(dve, c)
            route.dve(dve, c)
            experts.dve(dve, c)
            combine.dve(dve, c)
            with dve.Fori(0, 2) as layer:
                cl = c.inside(layer, per_layer)
                norm_pre.dve(dve, cl)
                gating.dve(dve, cl)
                latents.dve(dve, cl)
                raised.dve(dve, cl)
                turn_latent.dve(dve, cl)
                latent_attention.dve(dve, cl)
                heads_2.dve(dve, cl)
                chunk_attention.dve(dve, cl)
                turn_2.dve(dve, cl)
                merge_2.dve(dve, cl)
                turn_merged_2.dve(dve, cl)
                out_2.dve(dve, cl)
            c.step(per_layer, 2)
            output.dve(dve, c)

        @block.gpsimd
        def _(pool):
            c = At()
            for n in names:
                if n not in FROM_ZERO:
                    pool.sem_inc(SEM[n], BASE)
            load.pool(pool, c)
            norm_mix.pool(pool, c)
            heads_1.pool(pool, c)
            values_1.pool(pool, c)
            dilated.pool(pool, c)
            grouped.pool(pool, c)
            merge_1.pool(pool, c)
            turn_merged_1.pool(pool, c)
            out_1.pool(pool, c)
            norm_ffn.pool(pool, c)
            route.pool(pool, c)
            experts.pool(pool, c)
            combine.pool(pool, c)
            with pool.Fori(0, 2) as layer:
                cl = c.inside(layer, per_layer)
                norm_pre.pool(pool, cl)
                gating.pool(pool, cl)
                latents.pool(pool, cl)
                raised.pool(pool, cl)
                turn_latent.pool(pool, cl)
                latent_attention.pool(pool, cl)
                heads_2.pool(pool, cl)
                chunk_attention.pool(pool, cl)
                turn_2.pool(pool, cl)
                merge_2.pool(pool, cl)
                turn_merged_2.pool(pool, cl)
                out_2.pool(pool, cl)
            c.step(per_layer, 2)
            output.pool(pool, c)



def lay_out(inputs):
    f = {k: np.ascontiguousarray(a) for k, a in inputs.items()}
    cat = np.concatenate
    m = {k: f[k] for k in ("x", "norm_mix_g", "w_in", "w_proj_a", "w_proj_b", "w_out", "norm_ffn_g", "w_router",
                           "b_router", "w_gate_up", "w_down", "b_down", "w_in_2", "pre_g_2", "post_g_2",
                           "mla_w_uq_2", "mla_w_ukv_2", "w_branch_2", "w_out_2")}
    m["w_proj_b"] = f["w_proj_b"].reshape(2, 4, E, D).transpose(1, 0, 2, 3).reshape(S, D)
    m["b_gate"] = f["b_gate"].reshape(-1)
    m["gate_b_2"] = f["gate_b_2"].reshape(2, -1)
    m["qk_gains"] = cat([f["qn_a"].reshape(-1), f["kn_a"].reshape(-1), f["qn_b"], f["kn_b"]])
    m["b_gate_up_T"] = f["b_gate_up"].reshape(NE, 16, P).transpose(2, 0, 1).reshape(P, NE * 16)
    m["sgu_w_T"] = f["sgu_w_2"].transpose(0, 3, 1, 2)
    m["sgu_b_T"] = f["sgu_b_2"].transpose(0, 2, 1)
    m["sgu_ln"] = cat([f["sgu_ln_g_2"], f["sgu_ln_b_2"]], 1)
    m["mla_norms"] = cat([f["mla_q_norm_g_2"], f["mla_kv_norm_g_2"]], 1)
    r, cc = np.arange(P)[:, None], np.arange(256)[None, :]
    m["rel_rows"] = f["ca_rel_bias_2"][:, :, np.minimum(r + P - cc, 128) + 128].reshape(16, P, 256)
    m["consts"] = cat([a for _, a in constant_parts()], 1)
    m["masks"] = window_masks().astype(mybir.dt.np(BF16))
    t = np.arange(S).reshape(TT, P)
    m["assignment"] = (t.T[:, :, None] * TOPK + np.arange(TOPK)).reshape(P, 16).astype(np.int32)
    m["nobody"] = np.full((P, (NE + 1) * NPOS // P), 1 << 20, np.int32)
    return {k: np.ascontiguousarray(a) for k, a in m.items()}


def kernel(**inputs):
    import concourse.bacc as bacc
    from concourse.bass_utils import run_bass_kernel_spmd

    nc = bacc.Bacc("TRN2", target_bir_lowering=False, num_devices=1)
    m = lay_out(inputs)
    A = {k: nc.dram_tensor(f"in_{k}", a.shape, mybir.dt.from_np(a.dtype), kind="ExternalInput").ap() for k, a in m.items()}
    out = nc.dram_tensor("out_0", (1, S, D), F32, kind="ExternalOutput").ap()
    build(nc, A, out)
    r = run_bass_kernel_spmd(nc, [{f"in_{k}": a for k, a in m.items()}], core_ids=[0])
    return r.results[0]["out_0"]
```
